# Optimizing a Trainium2 kernel written in Bass

```python
import math
import jax, jax.numpy as jnp
from jax import lax
import numpy as np

D_MODEL = 1024
BATCH = 1
SEQ = 512
DEPTH = 2

N_EVEN = (DEPTH + 1) // 2
N_ODD = DEPTH // 2

POOL_WINDOWS = (2, 4, 8, 16)
POOL_GROUPS = 4
POOL_WIDTH = D_MODEL // 2
POOL_GDIM = POOL_WIDTH // POOL_GROUPS
SGU_GROUPS = 4
SGU_WIDTH = D_MODEL // 2
SGU_GDIM = SGU_WIDTH // SGU_GROUPS
SGU_CHUNK = 128
EVEN_IN = POOL_WIDTH + 2 * SGU_WIDTH
EVEN_MIX = POOL_WIDTH + SGU_WIDTH
NSA_HEADS = 8
NSA_KV_GROUPS = 2
NSA_HPG = NSA_HEADS // NSA_KV_GROUPS
NSA_HEAD_DIM = 64
NSA_WIDTH = NSA_HEADS * NSA_HEAD_DIM
NSA_KV_WIDTH = NSA_KV_GROUPS * NSA_HEAD_DIM
CMP_BLOCK = 32
CMP_STRIDE = 16
CMP_HIDDEN = 128
SEL_BLOCK = 64
SEL_TOPK = 16
WINDOW = 512
Q_BLOCK = 128
FORCE_SCORE = 1.0e4
ROPE_THETA = 500000.0
ROPE_DIM = NSA_HEAD_DIM // 4
RET_HEADS = 4
RET_HEAD_DIM = 128
RET_WIDTH = RET_HEADS * RET_HEAD_DIM
RET_CHUNK = 128
RET_THETA = 10000.0
ODD_IN = NSA_WIDTH + 6 * NSA_KV_WIDTH + 3 * NSA_HEADS + 4 * RET_WIDTH
ODD_MIX = NSA_WIDTH + RET_WIDTH
FFN_HIDDEN = -(-8 * D_MODEL // (3 * 256)) * 256
NEG_INF = -1.0e30


def rms_norm(x, g, eps=1e-6):
    xf = x.astype(jnp.float32)
    y = xf * lax.rsqrt(jnp.mean(xf * xf, axis=-1, keepdims=True) + eps)
    return (y * g.astype(jnp.float32)).astype(x.dtype)

def layer_norm(x, g, b, eps=1e-5):
    xf = x.astype(jnp.float32)
    mu = jnp.mean(xf, axis=-1, keepdims=True)
    var = jnp.mean(jnp.square(xf - mu), axis=-1, keepdims=True)
    return ((xf - mu) * lax.rsqrt(var + eps) * g.astype(jnp.float32) + b.astype(jnp.float32)).astype(x.dtype)

def masked_softmax(s, mask):
    return jax.nn.softmax(jnp.where(mask, s.astype(jnp.float32), NEG_INF), axis=-1)

def rope_tables(positions, rot_dim, theta):
    inv_freq = 1.0 / (theta ** (jnp.arange(0, rot_dim, 2, dtype=jnp.float32) / rot_dim))
    ang = positions.astype(jnp.float32)[..., None] * inv_freq
    return jnp.cos(ang)[:, None], jnp.sin(ang)[:, None]

def apply_rope(x, cos, sin):
    half = cos.shape[-1]
    x1, x2, rest = x[..., :half], x[..., half:2 * half], x[..., 2 * half:]
    c, s = cos.astype(x.dtype), sin.astype(x.dtype)
    return jnp.concatenate([x1 * c - x2 * s, x2 * c + x1 * s, rest], axis=-1)

def to_heads(x, n):
    b, t, _ = x.shape
    return x.reshape(b, t, n, -1).transpose(0, 2, 1, 3)

def swiglu(h, w_gate, w_up, w_down):
    return (jax.nn.silu(h @ w_gate) * (h @ w_up)) @ w_down

def pool_mixer(a, pool_w, pool_scale):
    b, t_len, _ = a.shape
    af = a.astype(jnp.float32).reshape(b, t_len, POOL_GROUPS, POOL_GDIM)
    cs = jnp.concatenate([jnp.zeros_like(af[:, :1]), jnp.cumsum(af, axis=1)], axis=1)
    t = jnp.arange(t_len)
    pooled = []
    for gi, w in enumerate(POOL_WINDOWS):
        lo = jnp.maximum(t + 1 - w, 0)
        win_sum = cs[:, 1:, gi] - cs[:, lo, gi]
        pooled.append(win_sum / (t + 1 - lo).astype(jnp.float32)[None, :, None])
    pooled = jnp.stack(pooled, axis=2)
    diff = (pooled - af).astype(a.dtype)
    y = jnp.einsum('btgc,gcd->btgd', diff, pool_w)
    return y.reshape(b, t_len, POOL_WIDTH) * pool_scale

def sgu_mixer(u, v, ln_g, ln_b, w_s, b_s):
    b, t_len, _ = u.shape
    u = jax.nn.gelu(u)
    v = layer_norm(jax.nn.gelu(v), ln_g, ln_b)
    n_chunk = t_len // SGU_CHUNK
    vc = v.reshape(b, n_chunk, SGU_CHUNK, SGU_GROUPS, SGU_GDIM)
    causal = jnp.tril(jnp.ones((SGU_CHUNK, SGU_CHUNK), dtype=bool))
    w_masked = jnp.where(causal[None], w_s, 0.0).astype(v.dtype)
    mixed = jnp.einsum('gts,bcsgd->bctgd', w_masked, vc) + b_s.T[None, None, :, :, None]
    return u * mixed.reshape(b, t_len, SGU_WIDTH)

def even_mixer(h, w_in, pool_w, pool_scale, sgu_ln_g, sgu_ln_b, sgu_w, sgu_b, w_out):
    z = h @ w_in
    a = z[..., :POOL_WIDTH]
    u = z[..., POOL_WIDTH:POOL_WIDTH + SGU_WIDTH]
    v = z[..., POOL_WIDTH + SGU_WIDTH:]
    y_a = pool_mixer(a, pool_w, pool_scale)
    y_b = sgu_mixer(u, v, sgu_ln_g, sgu_ln_b, sgu_w, sgu_b)
    return jnp.concatenate([y_a, y_b], axis=-1) @ w_out

def compress_blocks(k, pos_emb, w1, w2):
    t_len = k.shape[2]
    n_cmp = (t_len - CMP_BLOCK) // CMP_STRIDE + 1
    idx = np.arange(n_cmp)[:, None] * CMP_STRIDE + np.arange(CMP_BLOCK)[None, :]
    blocks = k[:, :, idx] + pos_emb
    flat = blocks.reshape(blocks.shape[:3] + (CMP_BLOCK * NSA_HEAD_DIM,))
    return jax.nn.gelu(flat @ w1) @ w2

def nsa_attention(q, k_cmp, v_cmp, k_sel, v_sel, k_win, v_win, gates, positions,
                  cmp_k_pos, cmp_k_w1, cmp_k_w2, cmp_v_pos, cmp_v_w1, cmp_v_w2):
    b, t_len, _ = q.shape
    G, M, d = NSA_KV_GROUPS, NSA_HPG, NSA_HEAD_DIM
    cos, sin = rope_tables(positions, ROPE_DIM, ROPE_THETA)
    q = apply_rope(to_heads(q, NSA_HEADS), cos, sin) * (d ** -0.5)
    k_cmp = apply_rope(to_heads(k_cmp, G), cos, sin)
    k_sel = apply_rope(to_heads(k_sel, G), cos, sin)
    k_win = apply_rope(to_heads(k_win, G), cos, sin)
    v_cmp, v_sel, v_win = to_heads(v_cmp, G), to_heads(v_sel, G), to_heads(v_win, G)

    kc = compress_blocks(k_cmp, cmp_k_pos, cmp_k_w1, cmp_k_w2)
    vc = compress_blocks(v_cmp, cmp_v_pos, cmp_v_w1, cmp_v_w2)
    n_cmp = kc.shape[2]
    cmp_end = jnp.arange(n_cmp) * CMP_STRIDE + CMP_BLOCK - 1

    n_sel = t_len // SEL_BLOCK
    top_k = min(SEL_TOPK, n_sel)
    c_start = np.arange(n_cmp) * CMP_STRIDE
    s_start = np.arange(n_sel) * SEL_BLOCK
    cmp_to_sel = ((c_start[:, None] < s_start[None, :] + SEL_BLOCK)
                  & (c_start[:, None] + CMP_BLOCK > s_start[None, :])).astype(np.float32)
    ks_blk = k_sel.reshape(b, G, n_sel, SEL_BLOCK, d)
    vs_blk = v_sel.reshape(b, G, n_sel, SEL_BLOCK, d)
    kw_pad = jnp.pad(k_win, ((0, 0), (0, 0), (WINDOW, 0), (0, 0)))
    vw_pad = jnp.pad(v_win, ((0, 0), (0, 0), (WINDOW, 0), (0, 0)))
    g = jax.nn.sigmoid(gates.astype(jnp.float32)).reshape(b, t_len, NSA_HEADS, 3)
    g = g.transpose(0, 2, 1, 3).astype(q.dtype)
    b_idx = jnp.arange(b)[:, None, None, None]
    g_idx = jnp.arange(G)[None, :, None, None]
    j_sel = jnp.arange(n_sel)

    def block(i):
        t0 = i * Q_BLOCK
        tq = t0 + jnp.arange(Q_BLOCK)
        qb = lax.dynamic_slice_in_dim(q, t0, Q_BLOCK, axis=2).reshape(b, G, M, Q_BLOCK, d)
        gb = lax.dynamic_slice_in_dim(g, t0, Q_BLOCK, axis=2)
        s = jnp.einsum('bgmqd,bgnd->bgmqn', qb, kc)
        p_cmp = masked_softmax(s, cmp_end[None, :] <= tq[:, None])
        p_cmp = p_cmp * (tq >= CMP_BLOCK - 1).astype(jnp.float32)[:, None]
        o_cmp = jnp.einsum('bgmqn,bgnd->bgmqd', p_cmp.astype(vc.dtype), vc)
        p_slc = jnp.einsum('bgmqn,nj->bgqj', p_cmp, cmp_to_sel)
        cur = tq // SEL_BLOCK
        sel_ok = j_sel[None, :] <= cur[:, None]
        forced = (j_sel[None, :] == 0) | (j_sel[None, :] == cur[:, None]) | (j_sel[None, :] == cur[:, None] - 1)
        score = jnp.where(sel_ok, jnp.where(forced, FORCE_SCORE, p_slc), -1.0)
        top_val, top_idx = lax.top_k(score, top_k)
        ks = ks_blk[b_idx, g_idx, top_idx]
        vs = vs_blk[b_idx, g_idx, top_idx]
        tok = top_idx[..., None] * SEL_BLOCK + jnp.arange(SEL_BLOCK)
        tok_ok = (top_val >= 0.0)[..., None] & (tok <= tq[:, None, None])
        s = jnp.einsum('bgmqd,bgqkld->bgmqkl', qb, ks).reshape(b, G, M, Q_BLOCK, top_k * SEL_BLOCK)
        p = masked_softmax(s, tok_ok.reshape(b, G, 1, Q_BLOCK, top_k * SEL_BLOCK))
        p = p.reshape(b, G, M, Q_BLOCK, top_k, SEL_BLOCK).astype(vs.dtype)
        o_sel = jnp.einsum('bgmqkl,bgqkld->bgmqd', p, vs)
        kwb = lax.dynamic_slice_in_dim(kw_pad, t0, WINDOW + Q_BLOCK, axis=2)
        vwb = lax.dynamic_slice_in_dim(vw_pad, t0, WINDOW + Q_BLOCK, axis=2)
        pos = t0 - WINDOW + jnp.arange(WINDOW + Q_BLOCK)
        win_ok = (pos[None, :] >= 0) & (pos[None, :] <= tq[:, None]) & (pos[None, :] > tq[:, None] - WINDOW)
        s = jnp.einsum('bgmqd,bgsd->bgmqs', qb, kwb)
        o_win = jnp.einsum('bgmqs,bgsd->bgmqd', masked_softmax(s, win_ok).astype(vwb.dtype), vwb)
        o = jnp.stack([o_cmp, o_sel, o_win], axis=-1).reshape(b, NSA_HEADS, Q_BLOCK, d, 3)
        return jnp.einsum('bhqdc,bhqc->bqhd', o, gb)

    out = lax.map(block, jnp.arange(t_len // Q_BLOCK))
    return out.transpose(1, 0, 2, 3, 4).reshape(b, t_len, NSA_WIDTH)

def retention(q, k, v, gate, positions, gn_g):
    b, t_len, _ = q.shape
    H, d, C = RET_HEADS, RET_HEAD_DIM, RET_CHUNK
    n_chunk = t_len // C
    cos, sin = rope_tables(positions, d, RET_THETA)
    q = apply_rope(to_heads(q, H), cos, sin)
    k = apply_rope(to_heads(k, H), cos, sin) * (d ** -0.5)
    v = to_heads(v, H)
    log_gamma = jnp.log1p(-jnp.exp2(-5.0 - jnp.arange(H, dtype=jnp.float32)))
    idx = jnp.arange(C, dtype=jnp.float32)
    rel = idx[:, None] - idx[None, :]
    decay = jnp.where(rel >= 0, jnp.exp(jnp.maximum(rel, 0.0)[None] * log_gamma[:, None, None]), 0.0)
    qc = q.reshape(b, H, n_chunk, C, d)
    kc = k.reshape(b, H, n_chunk, C, d)
    vc = v.reshape(b, H, n_chunk, C, d)
    s = jnp.einsum('bhcid,bhcjd->bhcij', qc, kc) * decay[None, :, None].astype(q.dtype)
    o_intra = jnp.einsum('bhcij,bhcje->bhcie', s, vc)
    zeta = jnp.exp((C - 1 - idx)[None, :] * log_gamma[:, None])
    chunk_kv = jnp.einsum('bhcjd,bhcje->bhcde', kc * zeta[None, :, None, :, None].astype(k.dtype), vc)
    g_chunk = jnp.exp(C * log_gamma)[None, :, None, None]

    def step(state, kv):
        return state * g_chunk + kv, state

    _, prev = lax.scan(step, jnp.zeros((b, H, d, d), jnp.float32),
                       jnp.moveaxis(chunk_kv, 2, 0).astype(jnp.float32))
    prev = jnp.moveaxis(prev, 0, 2)
    xi = jnp.exp((idx + 1.0)[None, :] * log_gamma[:, None])
    o_cross = jnp.einsum('bhcid,bhcde->bhcie', qc.astype(jnp.float32) * xi[None, :, None, :, None], prev)
    o = (o_intra.astype(jnp.float32) + o_cross).reshape(b, H, t_len, d).transpose(0, 2, 1, 3)
    mu = jnp.mean(o, axis=-1, keepdims=True)
    var = jnp.mean(jnp.square(o - mu), axis=-1, keepdims=True)
    o = ((o - mu) * lax.rsqrt(var + 1e-5)).reshape(b, t_len, RET_WIDTH) * gn_g.astype(jnp.float32)
    return (jax.nn.silu(gate.astype(jnp.float32)) * o).astype(gate.dtype)

def odd_mixer(h, positions, w_in, cmp_k_pos, cmp_k_w1, cmp_k_w2, cmp_v_pos, cmp_v_w1, cmp_v_w2,
              ret_gn_g, w_out):
    z = h @ w_in
    sizes = [NSA_WIDTH] + [NSA_KV_WIDTH] * 6 + [3 * NSA_HEADS] + [RET_WIDTH] * 4
    splits = np.cumsum(sizes)[:-1].tolist()
    q, kc, vc, ks, vs, kw, vw, gt, rq, rk, rv, rg = jnp.split(z, splits, axis=-1)
    y_c = nsa_attention(q, kc, vc, ks, vs, kw, vw, gt, positions,
                        cmp_k_pos, cmp_k_w1, cmp_k_w2, cmp_v_pos, cmp_v_w1, cmp_v_w2)
    y_d = retention(rq, rk, rv, rg, positions, ret_gn_g)
    return jnp.concatenate([y_c, y_d], axis=-1) @ w_out

def first_inputs(seed: int = 0) -> dict:
    key = jax.random.key(seed)
    ks = jax.random.split(key, 32)

    def nrm(k, shape, scale):
        return jax.random.normal(k, shape, jnp.float32) * scale

    def gain(k, shape):
        return 1.0 + 0.05 * jax.random.normal(k, shape, jnp.float32)

    NE, NO, D, F = N_EVEN, N_ODD, D_MODEL, FFN_HIDDEN
    x = nrm(ks[0], (BATCH, SEQ, D), 1.0)
    start = jax.random.randint(ks[1], (BATCH, 1), 0, 2048, dtype=jnp.int32)
    positions = start + jnp.arange(SEQ, dtype=jnp.int32)[None, :]
    cmp_in = CMP_BLOCK * NSA_HEAD_DIM
    return {
        "x": x,
        "positions": positions,
        "ln_mix_pre": gain(ks[2], (DEPTH, D)),
        "ln_mix_post": gain(ks[3], (DEPTH, D)),
        "ln_ffn_pre": gain(ks[4], (DEPTH, D)),
        "ln_ffn_post": gain(ks[5], (DEPTH, D)),
        "ffn_w_gate": nrm(ks[6], (DEPTH, D, F), D ** -0.5),
        "ffn_w_up": nrm(ks[7], (DEPTH, D, F), D ** -0.5),
        "ffn_w_down": nrm(ks[8], (DEPTH, F, D), F ** -0.5),
        "ev_w_in": nrm(ks[9], (NE, D, EVEN_IN), D ** -0.5),
        "ev_pool_w": nrm(ks[10], (NE, POOL_GROUPS, POOL_GDIM, POOL_GDIM), POOL_GDIM ** -0.5),
        "ev_pool_scale": 1.0 + 0.1 * jax.random.normal(ks[11], (NE, POOL_WIDTH), jnp.float32),
        "ev_sgu_ln_g": gain(ks[12], (NE, SGU_WIDTH)),
        "ev_sgu_ln_b": nrm(ks[13], (NE, SGU_WIDTH), 0.02),
        "ev_sgu_w": nrm(ks[14], (NE, SGU_GROUPS, SGU_CHUNK, SGU_CHUNK), SGU_CHUNK ** -0.5),
        "ev_sgu_b": 1.0 + 0.1 * jax.random.normal(ks[15], (NE, SGU_GROUPS, SGU_CHUNK), jnp.float32),
        "ev_w_out": nrm(ks[16], (NE, EVEN_MIX, D), EVEN_MIX ** -0.5),
        "od_w_in": nrm(ks[17], (NO, D, ODD_IN), D ** -0.5),
        "od_cmp_k_pos": nrm(ks[18], (NO, CMP_BLOCK, NSA_HEAD_DIM), 0.1),
        "od_cmp_k_w1": nrm(ks[19], (NO, cmp_in, CMP_HIDDEN), cmp_in ** -0.5),
        "od_cmp_k_w2": nrm(ks[20], (NO, CMP_HIDDEN, NSA_HEAD_DIM), CMP_HIDDEN ** -0.5),
        "od_cmp_v_pos": nrm(ks[21], (NO, CMP_BLOCK, NSA_HEAD_DIM), 0.1),
        "od_cmp_v_w1": nrm(ks[22], (NO, cmp_in, CMP_HIDDEN), cmp_in ** -0.5),
        "od_cmp_v_w2": nrm(ks[23], (NO, CMP_HIDDEN, NSA_HEAD_DIM), CMP_HIDDEN ** -0.5),
        "od_ret_gn_g": gain(ks[24], (NO, RET_WIDTH)),
        "od_w_out": nrm(ks[25], (NO, ODD_MIX, D), ODD_MIX ** -0.5),
    }

def first_block(x, positions, ln_mix_pre, ln_mix_post, ln_ffn_pre, ln_ffn_post,
              ffn_w_gate, ffn_w_up, ffn_w_down,
              ev_w_in, ev_pool_w, ev_pool_scale, ev_sgu_ln_g, ev_sgu_ln_b, ev_sgu_w, ev_sgu_b, ev_w_out,
              od_w_in, od_cmp_k_pos, od_cmp_k_w1, od_cmp_k_w2, od_cmp_v_pos, od_cmp_v_w1, od_cmp_v_w2,
              od_ret_gn_g, od_w_out):
    for layer in range(DEPTH):
        h = rms_norm(x, ln_mix_pre[layer])
        if layer % 2 == 0:
            e = layer // 2
            m = even_mixer(h, ev_w_in[e], ev_pool_w[e], ev_pool_scale[e], ev_sgu_ln_g[e],
                           ev_sgu_ln_b[e], ev_sgu_w[e], ev_sgu_b[e], ev_w_out[e])
        else:
            o = layer // 2
            m = odd_mixer(h, positions, od_w_in[o], od_cmp_k_pos[o], od_cmp_k_w1[o], od_cmp_k_w2[o],
                          od_cmp_v_pos[o], od_cmp_v_w1[o], od_cmp_v_w2[o], od_ret_gn_g[o], od_w_out[o])
        x = x + rms_norm(m, ln_mix_post[layer])
        h = rms_norm(x, ln_ffn_pre[layer])
        x = x + rms_norm(swiglu(h, ffn_w_gate[layer], ffn_w_up[layer], ffn_w_down[layer]), ln_ffn_post[layer])
    return x


DEPTH_2 = 1

HEAD_DIM = 64
N_HEADS_DIL = 8
N_HEADS_FOX = 8
D_DIL = N_HEADS_DIL * HEAD_DIM
D_FOX = N_HEADS_FOX * HEAD_DIM
D_MIX = D_DIL + D_FOX
D_IN = 3 * D_DIL + 3 * D_FOX + N_HEADS_FOX
DILATED_BRANCHES = ((128, 1), (512, 4), (2048, 16))
SEG = 128
BLOCK_Q = 128
N_BUCKETS = 32
MAX_DISTANCE = 2048
N_GROUPS = 4
EXPERTS_PER_GROUP = 8
N_EXPERTS = N_GROUPS * EXPERTS_PER_GROUP
TOP_K_IN_GROUP = 2
D_EXPERT = 256
EPS = 1e-6
SCALE = HEAD_DIM ** -0.5
NEG_INF_2 = -1e30


def _rmsnorm(x, g):
    x32 = x.astype(jnp.float32)
    y = x32 * lax.rsqrt(jnp.mean(x32 * x32, axis=-1, keepdims=True) + EPS)
    return (y * g.astype(jnp.float32)).astype(x.dtype)

def _t5_bucket(dist):
    max_exact = N_BUCKETS // 2
    d32 = jnp.maximum(dist, 1).astype(jnp.float32)
    large = max_exact + (jnp.log(d32 / max_exact) / math.log(MAX_DISTANCE / max_exact)
                         * (N_BUCKETS - max_exact)).astype(jnp.int32)
    large = jnp.minimum(large, N_BUCKETS - 1)
    return jnp.where(dist < max_exact, dist, large)

def _dilated_branch(q, k, v, rel_bias, dilation):
    B, T, H, Dh = q.shape
    L = T // dilation
    nb = -(-L // SEG)
    L_pad = nb * SEG

    def to_sub(a):
        a = a.reshape(B, L, dilation, H, Dh).transpose(0, 2, 1, 3, 4)
        a = jnp.pad(a, ((0, 0), (0, 0), (0, L_pad - L), (0, 0), (0, 0)))
        return a.reshape(B, dilation, nb, SEG, H, Dh)

    qs, ks, vs = to_sub(q), to_sub(k), to_sub(v)

    def with_prev(a):
        prev = jnp.pad(a, ((0, 0), (0, 0), (1, 0), (0, 0), (0, 0), (0, 0)))[:, :, :-1]
        return jnp.concatenate([prev, a], axis=3)

    kk, vv = with_prev(ks), with_prev(vs)

    i = jnp.arange(SEG)[:, None]
    j = jnp.arange(2 * SEG)[None, :]
    m = i - j + SEG
    band = (m >= 0) & (m <= SEG)
    bias = rel_bias[_t5_bucket(jnp.clip(m, 0, SEG) * dilation)]
    bias = bias.transpose(2, 0, 1).astype(jnp.float32)
    blk = jnp.arange(nb)[:, None, None]
    valid = band[None] & (blk * SEG - SEG + j[None] >= 0)

    s = jnp.einsum('brnqhd,brnkhd->brnhqk', qs, kk,
                   preferred_element_type=jnp.float32) * SCALE + bias
    s = jnp.where(valid[:, None], s, NEG_INF_2)
    mx = jnp.max(s, axis=-1, keepdims=True)
    p = jnp.exp(s - mx)
    den = jnp.sum(p, axis=-1, keepdims=True)
    o = jnp.einsum('brnhqk,brnkhd->brnqhd', (p / den).astype(v.dtype), vv)
    lse = (mx + jnp.log(den))[..., 0].transpose(0, 1, 2, 4, 3)

    def from_sub(a):
        a = a.reshape(B, dilation, L_pad, *a.shape[4:])[:, :, :L]
        a = jnp.moveaxis(a, 1, 2)
        return a.reshape(B, T, *a.shape[3:])

    return from_sub(o), from_sub(lse)

def _dilated_attention(q, k, v, rel_bias):
    outs, lses = [], []
    for _, dilation in DILATED_BRANCHES:
        o, l = _dilated_branch(q, k, v, rel_bias, dilation)
        outs.append(o)
        lses.append(l)
    w = jax.nn.softmax(jnp.stack(lses), axis=0)
    return jnp.einsum('gbth,gbthd->bthd', w.astype(q.dtype), jnp.stack(outs))

def _forgetting_attention(q, k, v, log_f):
    B, T, H, Dh = q.shape
    nq = T // BLOCK_Q
    c = jnp.cumsum(log_f, axis=1)
    c_k = c.transpose(0, 2, 1)
    k_pos = jnp.arange(T)
    qb = q.reshape(B, nq, BLOCK_Q, H, Dh).transpose(1, 0, 2, 3, 4)
    cb = c.reshape(B, nq, BLOCK_Q, H).transpose(1, 0, 3, 2)
    starts = jnp.arange(nq) * BLOCK_Q

    def block(args):
        qi, ci, t0 = args
        s = jnp.einsum('bqhd,bkhd->bhqk', qi, k, preferred_element_type=jnp.float32) * SCALE
        s = s + ci[..., None] - c_k[:, :, None, :]
        q_pos = t0 + jnp.arange(BLOCK_Q)
        s = jnp.where(k_pos[None, :] <= q_pos[:, None], s, NEG_INF_2)
        p = jax.nn.softmax(s, axis=-1)
        return jnp.einsum('bhqk,bkhd->bqhd', p.astype(v.dtype), v)

    o = lax.map(block, (qb, cb, starts))
    return o.transpose(1, 0, 2, 3, 4).reshape(B, T, H, Dh)

def _hierarchical_moe(xt, w_rg, b_rg, w_re, b_re, w_gate, w_up, w_down):
    N = xt.shape[0]
    group_logits = (xt @ w_rg + b_rg).astype(jnp.float32)
    group_probs = jax.nn.softmax(group_logits, axis=-1)
    g1, g_idx = lax.top_k(group_probs, 1)
    expert_logits = (xt @ w_re + b_re).astype(jnp.float32).reshape(N, N_GROUPS, EXPERTS_PER_GROUP)
    sel = jnp.take_along_axis(expert_logits, g_idx[:, :, None], axis=1)[:, 0]
    top_v, top_i = lax.top_k(sel, TOP_K_IN_GROUP)
    g2 = jax.nn.softmax(top_v, axis=-1)
    expert_id = g_idx * EXPERTS_PER_GROUP + top_i
    combine = jnp.sum(jax.nn.one_hot(expert_id, N_EXPERTS, dtype=jnp.float32)
                      * (g1 * g2)[..., None], axis=1).astype(xt.dtype)
    y = jnp.zeros_like(xt)
    for e in range(N_EXPERTS):
        he = jax.nn.silu(xt @ w_gate[e]) * (xt @ w_up[e])
        y = y + combine[:, e:e + 1] * (he @ w_down[e])
    return y

def second_inputs(seed: int = 0) -> dict:
    key = jax.random.key(seed)
    ks = jax.random.split(key, 20)
    f32 = jnp.float32
    nrm = lambda k, shape, s: jax.random.normal(k, shape, f32) * s
    return {
        "x": nrm(ks[0], (BATCH, SEQ, D_MODEL), 1.0),
        "w_in": nrm(ks[1], (DEPTH_2, D_MODEL, D_IN), D_MODEL ** -0.5),
        "b_forget": 2.0 + nrm(ks[2], (DEPTH_2, N_HEADS_FOX), 0.5),
        "attn_norm": 1.0 + nrm(ks[3], (DEPTH_2, D_MODEL), 0.02),
        "out_norm_dil": 1.0 + nrm(ks[4], (DEPTH_2, D_DIL), 0.02),
        "out_norm_fox": 1.0 + nrm(ks[5], (DEPTH_2, D_FOX), 0.02),
        "w_out": nrm(ks[6], (DEPTH_2, D_MIX, D_MODEL), D_MIX ** -0.5),
        "ffn_norm": 1.0 + nrm(ks[7], (DEPTH_2, D_MODEL), 0.02),
        "w_router_group": nrm(ks[8], (DEPTH_2, D_MODEL, N_GROUPS), D_MODEL ** -0.5),
        "b_router_group": nrm(ks[9], (DEPTH_2, N_GROUPS), 0.01),
        "w_router_expert": nrm(ks[10], (DEPTH_2, D_MODEL, N_EXPERTS), D_MODEL ** -0.5),
        "b_router_expert": nrm(ks[11], (DEPTH_2, N_EXPERTS), 0.01),
        "w_expert_gate": nrm(ks[12], (DEPTH_2, N_EXPERTS, D_MODEL, D_EXPERT), D_MODEL ** -0.5),
        "w_expert_up": nrm(ks[13], (DEPTH_2, N_EXPERTS, D_MODEL, D_EXPERT), D_MODEL ** -0.5),
        "w_expert_down": nrm(ks[14], (DEPTH_2, N_EXPERTS, D_EXPERT, D_MODEL), D_EXPERT ** -0.5),
        "rel_bias": nrm(ks[15], (N_BUCKETS, N_HEADS_DIL), 0.5),
        "final_norm": 1.0 + nrm(ks[16], (D_MODEL,), 0.02),
    }

def second_block(x, w_in, b_forget, attn_norm, out_norm_dil, out_norm_fox, w_out, ffn_norm,
              w_router_group, b_router_group, w_router_expert, b_router_expert,
              w_expert_gate, w_expert_up, w_expert_down, rel_bias, final_norm):
    B, T, D = x.shape
    splits = [D_DIL, 2 * D_DIL, 3 * D_DIL, 3 * D_DIL + D_FOX, 3 * D_DIL + 2 * D_FOX,
              3 * D_DIL + 3 * D_FOX]
    for layer in range(DEPTH_2):
        h = _rmsnorm(x, attn_norm[layer])
        proj = h @ w_in[layer]
        qa, ka, va, qf, kf, vf, f_pre = jnp.split(proj, splits, axis=-1)
        heads = lambda a, n: a.reshape(B, T, n, HEAD_DIM)
        o_dil = _dilated_attention(heads(qa, N_HEADS_DIL), heads(ka, N_HEADS_DIL),
                                   heads(va, N_HEADS_DIL), rel_bias)
        log_f = jax.nn.log_sigmoid((f_pre + b_forget[layer]).astype(jnp.float32))
        o_fox = _forgetting_attention(heads(qf, N_HEADS_FOX), heads(kf, N_HEADS_FOX),
                                      heads(vf, N_HEADS_FOX), log_f)
        o_dil = _rmsnorm(o_dil.reshape(B, T, D_DIL), out_norm_dil[layer])
        o_fox = _rmsnorm(o_fox.reshape(B, T, D_FOX), out_norm_fox[layer])
        x = x + jnp.concatenate([o_dil, o_fox], axis=-1) @ w_out[layer]
        h2 = _rmsnorm(x, ffn_norm[layer]).reshape(B * T, D)
        y = _hierarchical_moe(h2, w_router_group[layer], b_router_group[layer],
                              w_router_expert[layer], b_router_expert[layer],
                              w_expert_gate[layer], w_expert_up[layer], w_expert_down[layer])
        x = x + y.reshape(B, T, D)
    return _rmsnorm(x, final_norm)


def setup_inputs(seed=0):
    out = dict(first_inputs(seed))
    for name, value in second_inputs(seed + 1).items():
        if name != "x":
            out[name + "_2"] = value
    return out


def reference(
    x, positions, ln_mix_pre, ln_mix_post, ln_ffn_pre, ln_ffn_post, ffn_w_gate, ffn_w_up,
    ffn_w_down, ev_w_in, ev_pool_w, ev_pool_scale, ev_sgu_ln_g, ev_sgu_ln_b, ev_sgu_w, ev_sgu_b,
    ev_w_out, od_w_in, od_cmp_k_pos, od_cmp_k_w1, od_cmp_k_w2, od_cmp_v_pos, od_cmp_v_w1,
    od_cmp_v_w2, od_ret_gn_g, od_w_out, w_in_2, b_forget_2, attn_norm_2, out_norm_dil_2,
    out_norm_fox_2, w_out_2, ffn_norm_2, w_router_group_2, b_router_group_2, w_router_expert_2,
    b_router_expert_2, w_expert_gate_2, w_expert_up_2, w_expert_down_2, rel_bias_2,
    final_norm_2,
):
    x = first_block(
        x, positions, ln_mix_pre, ln_mix_post, ln_ffn_pre, ln_ffn_post, ffn_w_gate, ffn_w_up,
        ffn_w_down, ev_w_in, ev_pool_w, ev_pool_scale, ev_sgu_ln_g, ev_sgu_ln_b, ev_sgu_w,
        ev_sgu_b, ev_w_out, od_w_in, od_cmp_k_pos, od_cmp_k_w1, od_cmp_k_w2, od_cmp_v_pos,
        od_cmp_v_w1, od_cmp_v_w2, od_ret_gn_g, od_w_out,
    )
    return second_block(
        x, w_in_2, b_forget_2, attn_norm_2, out_norm_dil_2, out_norm_fox_2, w_out_2, ffn_norm_2,
        w_router_group_2, b_router_group_2, w_router_expert_2, b_router_expert_2,
        w_expert_gate_2, w_expert_up_2, w_expert_down_2, rel_bias_2, final_norm_2,
    )


_drawn_inputs = setup_inputs


def setup_inputs(seed=0):
    import zlib

    import numpy as np

    out = dict(_drawn_inputs(seed))
    spreads = {}
    factors = {'ev_sgu_ln_b': 4.5,
     'od_cmp_k_pos': 8.0,
     'attn_norm_2': 3.878,
     'out_norm_dil_2': 5.611,
     'out_norm_fox_2': 5.974,
     'ffn_norm_2': 7.216,
     'b_router_group_2': 8.0,
     'b_router_expert_2': 8.0,
     'final_norm_2': 2.728}
    for name, (base, spread) in spreads.items():
        noise = np.random.default_rng([zlib.crc32(name.encode()), seed]).standard_normal(out[name].shape)
        drawn = base * np.exp(spread * noise) if base else spread * noise
        out[name] = __import__('jax').numpy.asarray(drawn.astype(out[name].dtype))
    for name, factor in factors.items():
        out[name] = (out[name] * factor).astype(out[name].dtype)
    return out
```

```python
import numpy as np
from contextlib import ExitStack
import concourse.bass as bass
from concourse import mybir

fp32 = mybir.dt.float32
bf16 = mybir.dt.bfloat16
i32 = mybir.dt.int32
ALU = mybir.AluOpType
ACT = mybir.ActivationFunctionType
AX = mybir.AxisListType

P = 128
D = 1024
T = 512
MT = T // P
KT = D // P
F = 2816
FT = F // P
EV = 1536
OD = 3352
W2 = 3080
DH = 64
NH = 8
RH, RD = 4, 128
NC, CB, CS = 31, 32, 16
NE, DE = 32, 256
NG, EG = 4, 8
NO = 2 * T // P - 1
NB = NE + NO
assert NB % 3 == 0
WR = 4096
BIG = 1.0e30
QC, KC_, VC_, KS_, VS_, KW_, VW_, GT_ = 0, 512, 640, 768, 896, 1024, 1152, 1280
RQ_, RK_, RV_, RG_ = 1304, 1816, 2328, 2840
QA_, KA_, VA_, QF_, KF_, VF_, FP_ = 0, 512, 1024, 1536, 2048, 2560, 3072
TW = 640


class Chain:

    def __init__(self, eng, sem, base=0):
        self.eng, self.sem, self.n = eng, sem, base

    def add(self, ins):
        ins.then_inc(self.sem, 1)
        self.n = self.n + 1

    def wait(self):
        self.eng.wait_ge(self.sem, self.n)


def program(nc, a, out):
    h2_dram = nc.dram_tensor("h2_rows", [T, D], fp32).ap()
    slot_dram = nc.dram_tensor("expert_rows", [NB * P, D], fp32).ap()
    bias_dram = nc.dram_tensor("distance_bias", [NH, TW], fp32).ap()

    ctx = ExitStack()
    with ctx:
        def sb(name, shape, dt=fp32):
            return ctx.enter_context(nc.sbuf_tensor(name, shape, dt))

        def sem(name):
            return ctx.enter_context(nc.semaphore(name))

        X = sb("X", [P, MT, D])
        HT = sb("HT", [P, KT, T])
        Y = sb("Y", [P, MT, D])
        RING = sb("RING", [P, 3 * WR])
        Z = sb("Z", [P, MT * OD])
        BIAS = sb("BIAS", [P, NH, 512])
        ST = sb("ST", [P, 2112])
        WK = sb("WK", [P, 3072])
        PR = WK[:, 0:1024].rearrange("p (s n) -> p s n", s=2)
        SBI = WK[:, 1024:2048].rearrange("p (s n) -> p s n", s=2)
        PTS = WK[:, 2048:3072].rearrange("p (s k n) -> p s k n", s=2, k=4)
        SIL = WK[:, 0:1536].rearrange("p (s n) -> p s n", s=3)
        GP = sb("GP", [P, 2, D])
        ident = sb("ident", [P, P])
        ones = sb("ones", [P, P])
        ident_b = sb("ident_b", [P, P], bf16)
        upper = sb("upper", [P, P])
        causal_b = sb("causal_b", [P, P], bf16)
        cmask_b = sb("cmask_b", [P, MT, NC + 1], bf16)
        gains = sb("gains", [P, 7, KT])
        stat = sb("stat", [P, 64])
        PB = ctx.enter_context(nc.psum_tensor("PB", [P, 8, 512], fp32))

        s_const = sem("const_loaded")
        idle = sb("idle", [P, 2])
        s_gains = sem("gains_loaded")
        s_x = sem("x_loaded")
        ring_full = [sem(f"ring_full{i}") for i in range(3)]

        chunks = []

        def ring_slot(n):
            return RING[:, (n % 3) * WR:(n % 3 + 1) * WR]

        def arrived(eng, n):
            eng.wait_ge(ring_full[n % 3], chunks[n]["value"])

        def add_chunk(*loads):
            n = len(chunks)
            before = chunks[n - 3]["value"] if n >= 3 else 0
            chunks.append({"loads": loads, "value": before + 16 * len(loads), "done": None})
            return n

        def load_chunk(eng, n):
            if n >= 3:
                s, v = chunks[n - 3]["done"]
                eng.wait_ge(s, v)
            for dst, src in chunks[n]["loads"]:
                eng.dma_start(dst, src).then_inc(ring_full[n % 3], 16)

        shared = {}

        class Sig:

            def __init__(self, name, total):
                if name not in shared:
                    shared[name] = [sem(name), 0]
                self.sem, self.base = shared[name]
                shared[name][1] += total

            def at(self, v):
                return self.sem, v + self.base

        class Norm:
            def __init__(self, name, src, ready, parts, gain=None, rows=None, normed=True):
                self.name, self.src, self.ready, self.parts = name, src, ready, parts
                self.gain, self.rows, self.normed = gain, rows, normed
                n = MT * len(parts) if normed else 0
                self.stats = Sig("norm_stats", n)
                self.rec = Sig("norm_rstd", n)
                self.xn = Sig("norm_scaled", n)
                self.tr = Sig("norm_transposed", 2 * MT)
                self.ht = Sig("norm_ht", 2 * MT)
                self.sq = Sig("norm_square", n)

            def act(self, act):
                if not self.normed:
                    return
                n, c = 0, 0
                for m in range(MT):
                    act.wait_ge(self.ready[0], self.ready[1](m))
                    for i, (c0, c1) in enumerate(self.parts):
                        nc.scalar.activation(SIL[:, 0:2, :].rearrange("p a b -> p (a b)")[:, 0:c1 - c0],
                                             self.src[:, m, c0:c1], ACT.Square,
                                             accum_out=stat[:, 8 * i + m:8 * i + m + 1]).then_inc(self.sq.sem, 1)
                        n += 1
                        act.wait_ge(*self.sq.at(n))
                        nc.scalar.activation(stat[:, 16 + 8 * i + m:17 + 8 * i + m], stat[:, 8 * i + m:8 * i + m + 1],
                                             ACT.Sqrt, bias=stat[:, 60:61], scale=1.0 / (c1 - c0)).then_inc(self.stats.sem, 1)

            def dve(self, dve):
                np_ = len(self.parts)
                nx = 0
                for m in range(MT):
                    if self.normed:
                        for i, (c0, c1) in enumerate(self.parts):
                            dve.wait_ge(*self.stats.at(m * np_ + i + 1))
                            nc.vector.reciprocal(stat[:, 32 + 8 * i + m:33 + 8 * i + m],
                                                 stat[:, 16 + 8 * i + m:17 + 8 * i + m]).then_inc(self.rec.sem, 1)
                            dve.wait_ge(*self.rec.at(m * np_ + i + 1))
                            r = stat[:, 32 + 8 * i + m:33 + 8 * i + m]
                            if self.rows is None:
                                nc.vector.tensor_scalar(Y[:, m, c0:c1], self.src[:, m, c0:c1], r, None, ALU.mult
                                                        ).then_inc(self.xn.sem, 1)
                            else:
                                nc.vector.scalar_tensor_tensor(Y[:, m, c0:c1], self.src[:, m, c0:c1], r, self.rows,
                                                               ALU.mult, ALU.mult).then_inc(self.xn.sem, 1)
                    if m >= 1:
                        self.evac(dve, m - 1)
                self.evac(dve, MT - 1)

            def evac(self, dve, m):
                for hf in range(2):
                    u = 2 * m + hf
                    dve.wait_ge(*self.tr.at(u + 1))
                    dst = HT[:, 4 * hf:4 * hf + 4, m * P:(m + 1) * P]
                    src = PB[:, u % 4, :].rearrange("p (a b) -> p a b", a=4)
                    if self.gain is None:
                        nc.vector.tensor_copy(dst, src).then_inc(self.ht.sem, 1)
                    else:
                        g = gains[:, self.gain, 4 * hf:4 * hf + 4].unsqueeze(2).to_broadcast([P, 4, P])
                        nc.vector.tensor_tensor(dst, src, g, ALU.mult).then_inc(self.ht.sem, 1)

            def pe(self, pe):
                for m in range(MT):
                    if self.normed:
                        pe.wait_ge(*self.xn.at((m + 1) * len(self.parts)))
                    else:
                        pe.wait_ge(self.ready[0], self.ready[1](m))
                    for hf in range(2):
                        u = 2 * m + hf
                        if u >= 4:
                            pe.wait_ge(*self.ht.at(u - 3))
                        for k in range(4):
                            t = nc.tensor.transpose(PB[:, u % 4, k * P:(k + 1) * P],
                                                    Y[:, m, (4 * hf + k) * P:(4 * hf + k + 1) * P], ident[:])
                        t.then_inc(self.tr.sem, 1)

            def ready_tile(self, m):
                return self.ht.at(2 * (m + 1))

        class Proj:

            def __init__(self, name, norm, w, width, dst, fn):
                self.name, self.norm, self.dst, self.fn = name, norm, dst, fn
                self.cols = [(c, min(c + 512, width)) for c in range(0, width, 512)]
                self.mm = Sig("proj_mm", MT * len(self.cols))
                w_v = w.rearrange("(k p) n -> p k n", p=P)
                self.n0 = len(chunks)
                for j, (c0, c1) in enumerate(self.cols):
                    wd = c1 - c0
                    n = len(chunks)
                    dst_ = ring_slot(n)[:, 0:KT * wd].rearrange("p (k n) -> p k n", k=KT)
                    add_chunk((dst_, w_v[:, :, c0:c1]))
                    chunks[n]["done"] = self.mm.at(MT * (j + 1))
                self.who = []
                cnt = {"act": 0, "dve": 0}
                for u in range(MT * len(self.cols)):
                    e = fn(u)[0]
                    cnt[e] += 1
                    self.who.append((e, cnt[e]))
                self.total = cnt
                self.out = {e: Sig("proj_out_" + e, cnt[e]) for e in cnt}

            def pe(self, pe):
                for j, (c0, c1) in enumerate(self.cols):
                    wd = c1 - c0
                    w = ring_slot(self.n0 + j)[:, 0:KT * wd].rearrange("p (k n) -> p k n", k=KT)
                    arrived(pe, self.n0 + j)
                    for m in range(MT):
                        u = MT * j + m
                        if j == 0:
                            pe.wait_ge(*self.norm.ready_tile(m))
                        if u >= 8:
                            e, v = self.who[u - 8]
                            pe.wait_ge(*self.out[e].at(v))
                        for k in range(KT):
                            t = nc.tensor.matmul(PB[:, (4 + u) % 8, 0:wd], HT[:, k, m * P:(m + 1) * P], w[:, k, :],
                                                 start=(k == 0), stop=(k == KT - 1))
                        t.then_inc(self.mm.sem, 1)

            def take(self, eng, name):
                for j, (c0, c1) in enumerate(self.cols):
                    for m in range(MT):
                        u = MT * j + m
                        e, func = self.fn(u)
                        if e != name:
                            continue
                        eng.wait_ge(*self.mm.at(u + 1))
                        if name == "act":
                            nc.scalar.activation(self.dst[:, m, c0:c1], PB[:, (4 + u) % 8, 0:c1 - c0], func
                                                 ).then_inc(self.out["act"].sem, 1)
                        else:
                            nc.vector.tensor_copy(self.dst[:, m, c0:c1], PB[:, (4 + u) % 8, 0:c1 - c0]
                                                  ).then_inc(self.out["dve"].sem, 1)

            def wait_all(self, eng):
                for e in ("act", "dve"):
                    if self.total[e]:
                        eng.wait_ge(*self.out[e].at(self.total[e]))

        class Down:
            def __init__(self, name, nk, w, gain_row, src_ready):
                self.name, self.nk, self.gain_row, self.src_ready = name, nk, gain_row, src_ready
                n = 0 if gain_row is None else MT
                self.free = Sig("down_chunk", (nk + 3) // 4 - 1)
                self.mm = Sig("down_mm", 1)
                self.sq = Sig("down_square", n)
                self.st = Sig("down_stats", n)
                self.rec = Sig("down_rstd", n)
                self.dc = Sig("down_scaled", n)
                self.xr = Sig("down_x", MT)
                w_v = w.rearrange("(k p) n -> p k n", p=P)
                self.n0 = len(chunks)
                self.ks = [(k, min(k + 4, nk)) for k in range(0, nk, 4)]
                for j, (k0, k1) in enumerate(self.ks):
                    n = len(chunks)
                    dst_ = ring_slot(n)[:, 0:(k1 - k0) * D].rearrange("p (k n) -> p k n", n=D)
                    add_chunk((dst_, w_v[:, k0:k1, :]))
                    chunks[n]["done"] = self.free.at(j + 1) if j < len(self.ks) - 1 else self.mm.at(1)

            def pe(self, pe, src):
                self.src_ready(pe)
                for j, (k0, k1) in enumerate(self.ks):
                    w = ring_slot(self.n0 + j).rearrange("p (k n) -> p k n", n=D)
                    arrived(pe, self.n0 + j)
                    for k in range(k0, k1):
                        for m in range(MT):
                            for hf in range(2):
                                t = nc.tensor.matmul(PB[:, 2 * m + hf, :], src[:, k, m * P:(m + 1) * P],
                                                     w[:, k - k0, hf * 512:(hf + 1) * 512],
                                                     start=(k == 0), stop=(k == self.nk - 1))
                    t.then_inc((self.free if j < len(self.ks) - 1 else self.mm).sem, 1)

            def act(self, act):
                if self.gain_row is None:
                    return
                act.wait_ge(*self.mm.at(1))
                for m in range(MT):
                    nc.scalar.activation(SIL[:, 0:2, :], PB[:, 2 * m:2 * m + 2, :], ACT.Square,
                                         accum_out=stat[:, m:m + 1]).then_inc(self.sq.sem, 1)
                    act.wait_ge(*self.sq.at(m + 1))
                    nc.scalar.activation(stat[:, 16 + m:17 + m], stat[:, m:m + 1], ACT.Sqrt,
                                         bias=stat[:, 60:61], scale=1.0 / D).then_inc(self.st.sem, 1)

            def dve(self, dve):
                if self.gain_row is None:
                    dve.wait_ge(*self.mm.at(1))
                    for m in range(MT):
                        nc.vector.tensor_tensor(X[:, m, :], PB[:, 2 * m:2 * m + 2, :].rearrange("p a b -> p (a b)"),
                                                X[:, m, :], ALU.add).then_inc(self.xr.sem, 1)
                    return
                wait_gain(dve, self.gain_row)
                for m in range(MT):
                    dve.wait_ge(*self.st.at(m + 1))
                    nc.vector.reciprocal(stat[:, 32 + m:33 + m], stat[:, 16 + m:17 + m]).then_inc(self.rec.sem, 1)
                    dve.wait_ge(*self.rec.at(m + 1))
                    nc.vector.scalar_tensor_tensor(Y[:, m, :], PB[:, 2 * m:2 * m + 2, :].rearrange("p a b -> p (a b)"),
                                                   stat[:, 32 + m:33 + m], GP[:, self.gain_row % 2, :],
                                                   ALU.mult, ALU.mult).then_inc(self.dc.sem, 1)
                    dve.wait_ge(*self.dc.at(m + 1))
                    nc.vector.tensor_tensor(X[:, m, :], Y[:, m, :], X[:, m, :], ALU.add).then_inc(self.xr.sem, 1)

            def ready(self):
                return self.xr.sem, lambda m: self.xr.base + m + 1

        class GateUp:

            def __init__(self, name, norm, wg, wu):
                self.norm = norm
                self.gm = Sig("ffn_gate_mm", FT)
                self.um = Sig("ffn_up_mm", FT)
                self.sl = Sig("ffn_silu", FT)
                self.hid = Sig("ffn_hidden", FT + 3)
                self.n0 = len(chunks)
                g_v = wg.rearrange("(k p) n -> p k n", p=P)
                u_v = wu.rearrange("(k p) n -> p k n", p=P)
                for c in range(FT // 2):
                    n = len(chunks)
                    s = ring_slot(n).rearrange("p (t k n) -> p t k n", t=2, k=KT)
                    add_chunk((s[:, 0], g_v[:, :, c * 256:(c + 1) * 256]), (s[:, 1], u_v[:, :, c * 256:(c + 1) * 256]))
                    chunks[n]["done"] = self.um.at(2 * (c + 1))

            def pe(self, pe):
                pe.wait_ge(*self.norm.ready_tile(MT - 1))

                def tile(it, k):
                    n = self.n0 + k // 2
                    if k % 2 == 0:
                        base = chunks[n]["value"]
                        pe.wait_ge(ring_full[n % 3], it * 32 + base)
                    pe.wait_ge(*self.hid.at(it * 6 + (k + 1)))
                    s = ring_slot(n).rearrange("p (t k n) -> p t k n", t=2, k=KT)
                    for t in range(2):
                        for kk in range(KT):
                            x = nc.tensor.matmul(PB[:, 2 * (k % 3) + t, :], s[:, t, kk, (k % 2) * P:(k % 2 + 1) * P],
                                                 HT[:, kk, :], start=(kk == 0), stop=(kk == KT - 1))
                        x.then_inc((self.gm if t == 0 else self.um).sem, 1)

                with pe.Fori(0, FT // 6) as it:
                    for k in range(6):
                        tile(it, k)
                for k in range(FT - FT // 6 * 6):
                    tile(FT // 6, k)

            def act(self, act):
                def tile(it, k):
                    act.wait_ge(*self.gm.at(it * 6 + (k + 1)))
                    act.wait_ge(*self.hid.at(it * 6 + (k + 1)))
                    nc.scalar.activation(SIL[:, k % 3, :], PB[:, 2 * (k % 3), :], ACT.Silu).then_inc(self.sl.sem, 1)

                with act.Fori(0, FT // 6) as it:
                    for k in range(6):
                        tile(it, k)
                for k in range(FT - FT // 6 * 6):
                    tile(FT // 6, k)

            def dve(self, dve):
                dve.sem_inc(self.hid.sem, 3)
                Zt = Z[:, 0:FT * 512].rearrange("p (j t) -> p j t", t=512)

                def tile(it, k):
                    dve.wait_ge(*self.sl.at(it * 6 + (k + 1)))
                    dve.wait_ge(*self.um.at(it * 6 + (k + 1)))
                    dst = Zt[:, bass.ds(it * 6 + k, 1), :] if not isinstance(it, int) else Zt[:, 6 * it + k:6 * it + k + 1, :]
                    nc.vector.tensor_tensor(dst.rearrange("p a t -> p (a t)"), PB[:, 2 * (k % 3) + 1, :],
                                            SIL[:, k % 3, :], ALU.mult).then_inc(self.hid.sem, 1)

                with dve.Fori(0, FT // 6) as it:
                    for k in range(6):
                        tile(it, k)
                for k in range(FT - FT // 6 * 6):
                    tile(FT // 6, k)

            def done(self, eng):
                eng.wait_ge(*self.hid.at(3 + FT))

        gain_rows = [a["ln_mix_post"][0], a["ln_ffn_post"][0], a["ln_mix_post"][1], a["ln_ffn_post"][1],
                     a["ffn_norm_2"][0], a["final_norm_2"]]
        s_gain = [sem("gain_row0"), sem("gain_row1")]

        def wait_gain(eng, r):
            eng.wait_ge(s_gain[r % 2], 16 * (r // 2 + 1))

        def load_gain(eng, r):
            src = gain_rows[r].rearrange("(a n) -> a n", a=1).to_broadcast([P, D])
            eng.dma_start(GP[:, r % 2, :], src).then_inc(s_gain[r % 2], 16)

        ln = lambda e: (e, ACT.Copy)

        n1 = Norm("n1", X, (s_x, lambda m: 16), [(0, D)], gain=0)
        Ze = Z[:, 0:MT * EV].rearrange("p (m n) -> p m n", m=MT)
        ev_fn = lambda u: ("dve", None) if u < 4 else ("act", ACT.Gelu_apprx_tanh)
        p_ev = Proj("ev_in", n1, a["ev_w_in"][0], EV, Ze, ev_fn)
        zo = [MT * EV]

        def zpart(words, shape_str=None, **kw):
            v = Z[:, zo[0]:zo[0] + words]
            zo[0] += words
            return v.rearrange(shape_str, **kw) if shape_str else v

        poolA = zpart(4 * 2 * P, "p (g v t) -> p g v t", g=4, v=2)
        poolB = zpart(4 * P, "p (g t) -> p g t", g=4)
        poolW = zpart(4 * P, "p (g d) -> p g d", g=4)
        sguW = zpart(4 * P, "p (g d) -> p g d", g=4)
        sguWT = zpart(4 * P, "p (g d) -> p g d", g=4)
        lng = zpart(512)
        lnb = zpart(512)
        sgub = zpart(512)
        diffT = zpart(2 * 512, "p (s t) -> p s t", s=2)
        uT = zpart(2 * 512, "p (s t) -> p s t", s=2)
        pscale = zpart(4)
        bnst = zpart(4 * 6, "p (m s) -> p m s", m=4)
        bnag = zpart(4 * 2, "p (m s) -> p m s", m=4)
        s_ev = sem("even_consts")

        e_wt = sem("ev_sgu_wT_mm")
        e_wm = sem("ev_sgu_wT")
        e_bn = sem("ev_ln_stats")
        e_sd = sem("ev_ln_std")
        e_v = sem("ev_v")
        e_df = sem("ev_diff_mm")
        e_ds = sem("ev_diff")
        e_pm = sem("ev_pool_mm")
        e_um = sem("ev_uT_mm")
        e_us = sem("ev_uT")
        e_mx = sem("ev_mixed_mm")
        e_ya = sem("ev_pool_out")
        e_yb = sem("ev_sgu_out")

        def even_pe(pe):
            pe.wait_ge(s_ev, 16 * 9)
            p_ev.wait_all(pe)
            for g in range(4):
                t = nc.tensor.transpose(PB[:, 0, g * P:(g + 1) * P], sguW[:, g, :], ident[:])
            t.then_inc(e_wt, 1)
            for g in range(4):
                if g >= 2:
                    pe.wait_ge(e_ds, g - 1)
                b = PB[:, 1 + g % 2, :]
                for i in range(MT):
                    t = nc.tensor.matmul(b[:, i * P:(i + 1) * P], Ze[:, i, g * P:(g + 1) * P],
                                         poolA[:, g, 0 if i == 0 else 1, :], start=True, stop=(i == 0))
                    if i:
                        t = nc.tensor.matmul(b[:, i * P:(i + 1) * P], Ze[:, i - 1, g * P:(g + 1) * P],
                                             poolB[:, g, :], start=False, stop=True)
                t.then_inc(e_df, 1)
                if g >= 1:
                    pe.wait_ge(e_ds, g)
                    if g >= 3:
                        pe.wait_ge(e_ya, g - 2)
                    nc.tensor.matmul(PB[:, 3 + (g - 1) % 2, :], poolW[:, g - 1, :], diffT[:, (g - 1) % 2, :],
                                     start=True, stop=True).then_inc(e_pm, 1)
            pe.wait_ge(e_ds, 4)
            pe.wait_ge(e_ya, 2)
            nc.tensor.matmul(PB[:, 4, :], poolW[:, 3, :], diffT[:, 1, :], start=True, stop=True).then_inc(e_pm, 1)
            pe.wait_ge(e_wm, 1)
            pe.wait_ge(e_v, MT)
            for g in range(4):
                if g >= 1:
                    pe.wait_ge(e_us, g)
                for i in range(MT):
                    t = nc.tensor.transpose(PB[:, 5, i * P:(i + 1) * P], Ze[:, i, 512 + g * P:512 + (g + 1) * P], ident[:])
                t.then_inc(e_um, 1)
                if g >= 2:
                    pe.wait_ge(e_yb, g - 1)
                for i in range(MT):
                    b = PB[:, 6 + g % 2, i * P:(i + 1) * P]
                    nc.tensor.matmul(b, Ze[:, i, 1024 + g * P:1024 + (g + 1) * P], sguWT[:, g, :], start=True, stop=False)
                    t = nc.tensor.matmul(b, ones[0:1, :], sgub[0:1, g * P:(g + 1) * P], start=False, stop=True)
                t.then_inc(e_mx, 1)

        def even_act(act):
            act.wait_ge(e_bn, 2 * MT)
            nc.scalar.activation(stat[:, 40:44], bnag[:, :, 1], ACT.Sqrt, bias=stat[:, 61:62], scale=1.0).then_inc(e_sd, 1)
            for g in range(4):
                act.wait_ge(e_df, g + 1)
                if g >= 2:
                    act.wait_ge(e_pm, g - 1)
                nc.scalar.activation(diffT[:, g % 2, :], PB[:, 1 + g % 2, :], ACT.Copy).then_inc(e_ds, 1)
                if g >= 1:
                    act.wait_ge(e_pm, g)
                    nc.scalar.activation(HT[:, g - 1, :], PB[:, 3 + (g - 1) % 2, :], ACT.Copy,
                                         scale=pscale[:, g - 1:g]).then_inc(e_ya, 1)
            act.wait_ge(e_pm, 4)
            nc.scalar.activation(HT[:, 3, :], PB[:, 4, :], ACT.Copy, scale=pscale[:, 3:4]).then_inc(e_ya, 1)
            for g in range(4):
                act.wait_ge(e_um, g + 1)
                if g >= 2:
                    act.wait_ge(e_yb, g - 1)
                nc.scalar.activation(uT[:, g % 2, :], PB[:, 5, :], ACT.Copy).then_inc(e_us, 1)

        def even_dve(dve):
            dve.wait_ge(s_ev, 16 * 9)
            dve.wait_ge(*p_ev.out["act"].at(p_ev.total["act"]))
            for m in range(MT):
                nc.vector.bn_stats(bnst[:, m, :], Ze[:, m, 1024:1536]).then_inc(e_bn, 1)
            dve.wait_ge(e_bn, MT)
            for m in range(MT):
                nc.vector.bn_aggr(bnag[:, m, :], bnst[:, m, :]).then_inc(e_bn, 1)
            dve.wait_ge(e_sd, 1)
            nc.vector.reciprocal(stat[:, 44:48], stat[:, 40:44]).then_inc(e_bn, 1)
            dve.wait_ge(e_wt, 1)
            nc.vector.tensor_tensor(sguWT, PB[:, 0, :].rearrange("p (g t) -> p g t", g=4),
                                    upper[:].unsqueeze(1).to_broadcast([P, 4, P]), ALU.mult).then_inc(e_wm, 1)
            dve.wait_ge(e_bn, 2 * MT + 1)
            for m in range(MT):
                v = Ze[:, m, 1024:1536]
                nc.vector.tensor_scalar(v, v, bnag[:, m, 0:1], stat[:, 44 + m:45 + m], ALU.subtract, ALU.mult).then_inc(e_bn, 1)
            for m in range(MT):
                v = Ze[:, m, 1024:1536]
                dve.wait_ge(e_bn, 2 * MT + 2 + m)
                nc.vector.tensor_tensor(v, v, lng, ALU.mult).then_inc(e_bn, 1)
            for m in range(MT):
                v = Ze[:, m, 1024:1536]
                dve.wait_ge(e_bn, 3 * MT + 2 + m)
                nc.vector.tensor_tensor(v, v, lnb, ALU.add).then_inc(e_v, 1)
            for g in range(4):
                dve.wait_ge(e_us, g + 1)
                dve.wait_ge(e_mx, g + 1)
                nc.vector.tensor_tensor(HT[:, 4 + g, :], PB[:, 6 + g % 2, :], uT[:, g % 2, :], ALU.mult).then_inc(e_yb, 1)

        def even_done(eng):
            eng.wait_ge(e_ya, 4)
            eng.wait_ge(e_yb, 4)

        d_ev = Down("ev_out", KT, a["ev_w_out"][0], 0, even_done)
        n2 = Norm("n2", X, d_ev.ready(), [(0, D)], gain=2)
        f0 = GateUp("ffn0", n2, a["ffn_w_gate"][0], a["ffn_w_up"][0])
        d_f0 = Down("ffn0_down", FT, a["ffn_w_down"][0], 1, f0.done)
        n3 = Norm("n3", X, d_f0.ready(), [(0, D)], gain=1)
        Zo = Z[:, 0:MT * OD].rearrange("p (m n) -> p m n", m=MT)
        alt = lambda u: ("dve", None) if u % 2 == 0 else ("act", ACT.Copy)
        p_od = Proj("od_in", n3, a["od_w_in"][0], OD, Zo, alt)

        rope_tab = sb("rope_tab", [P, 2, MT, 72])
        posf = sb("posf", [P, MT])
        posi = sb("posi", [P, MT], i32)
        invf = sb("invf", [P, 72])
        gate_s = sb("gate_s", [P, MT, 3 * NH])
        cvalid = sb("cvalid", [P, MT])
        cmpw2 = sb("cmpw2", [P, 2, DH])
        cmpos = sb("cmpos", [DH, 2, CB])
        hidc = sb("hidc", [P, 2, 2 * NC])
        kcT = sb("kcT", [DH, 2, NC])
        vcc = sb("vcc", [NC, 2, DH])
        den = sb("den", [P, 8])
        nmx = sb("nmx", [P, 2])
        osc = sb("osc", [P, 8])

        cmp_n = []
        c_h = sem("cmp_hidden_mm")
        for i, w in enumerate(("od_cmp_k_w1", "od_cmp_v_w1")):
            n = len(chunks)
            dst_ = RING[0:DH, (n % 3) * WR:(n % 3 + 1) * WR].rearrange("p (l n) -> p l n", l=CB)
            cmp_n.append(add_chunk((dst_, a[w][0].rearrange("(l p) n -> p l n", p=DH))))
            chunks[n]["done"] = (c_h, i + 1)

        s_od = sem("odd_consts")
        r_ch = sem("rope_chain")
        r_sn = sem("rope_sines")
        r_pool = sem("ret_staged")
        o_gate = sem("nsa_gates")
        t_mm = sem("ret_T_mm")
        t_ev = sem("ret_T")
        t_s = sem("ret_scores_mm")
        t_d = sem("ret_decayed")
        t_o = sem("ret_out_mm")
        t_c = sem("ret_norm")
        t_sd = sem("ret_std")
        t_g = sem("ret_silu")
        t_y = sem("ret_y")

        decay = BIAS[:, 0:RH, :]
        gnr = BIAS[:, RH, :]
        R_q, R_k, R_v = [ST[:, i * 512:(i + 1) * 512].rearrange("p (m d) -> p m d", m=MT) for i in range(3)]
        RqT, RkT = HT[:, 0, :], HT[:, 1, :]
        Rs = [HT[:, 2 + j, 0:T - j * P] for j in range(MT)]
        Rc = PR[:, 0, :].rearrange("p (m d) -> p m d", m=MT)
        Rsq = PR[:, 1, :].rearrange("p (m d) -> p m d", m=MT)

        def angles_dve(dve):
            dve.wait_ge(s_od, 16 * 11)
            ch = Chain(dve, r_ch)
            ang, kk, t1 = [SIL[:, i, 0:MT * 72] for i in range(3)]
            v = lambda x: x.rearrange("p (m n) -> p m n", m=MT)
            ch.add(nc.vector.tensor_copy(posf[:], posi[:]))
            ch.wait()
            ch.add(nc.vector.tensor_tensor(v(ang), posf[:].unsqueeze(2).to_broadcast([P, MT, 72]),
                                           invf[:].unsqueeze(1).to_broadcast([P, MT, 72]), ALU.mult))
            ch.wait()
            magic = float(1.5 * 2 ** 23)
            ch.add(nc.vector.tensor_scalar(kk, ang, float(1 / (2 * np.pi)), magic, ALU.mult, ALU.add))
            ch.wait()
            ch.add(nc.vector.tensor_scalar(kk, kk, magic, None, ALU.subtract))
            c1 = 6.28125
            c2 = float(np.float32(np.round((2 * np.pi - c1) * 2 ** 20) / 2 ** 20))
            c3 = float(2 * np.pi - c1 - c2)
            for c in (c1, c2, c3):
                ch.wait()
                ch.add(nc.vector.scalar_tensor_tensor(ang, kk, -c, ang, ALU.mult, ALU.add))
            ch.wait()
            pi = float(np.float32(3.1415925))
            ch.add(nc.vector.tensor_scalar(rope_tab[:, 1].rearrange("p m n -> p (m n)"), ang, pi, -pi, ALU.min, ALU.max))
            ch.add(nc.vector.tensor_scalar(t1, ang, -1.0, None, ALU.mult))
            ch.wait()
            ch.add(nc.vector.tensor_tensor(t1, t1, ang, ALU.max))
            ch.wait()
            ch.add(nc.vector.tensor_scalar(rope_tab[:, 0].rearrange("p m n -> p (m n)"), t1, -1.0, float(np.pi / 2),
                                           ALU.mult, ALU.add))
            return ch

        ANGLE_STEPS = 11

        def rope_dve(dve, ch):
            dve.wait_ge(r_sn, 1)
            p_od.wait_all(dve)
            tmp = [HT[:, 2 * i:2 * i + 2, :].rearrange("p a b -> p (a b)") for i in range(4)]
            for base, heads, stride, n, f0_ in ((0, 10, 64, 8, 0), (KS_, 2, 64, 8, 0), (KW_, 2, 64, 8, 0),
                                                (RQ_, 4, 128, 64, 8), (RK_, 4, 128, 64, 8)):
                z = Zo[:, :, base:base + heads * stride].rearrange("p m (h d) -> p m h d", h=heads)
                x1, x2 = z[:, :, :, 0:n], z[:, :, :, n:2 * n]
                cs = rope_tab[:, 0, :, f0_:f0_ + n].unsqueeze(2).to_broadcast([P, MT, heads, n])
                sn = rope_tab[:, 1, :, f0_:f0_ + n].unsqueeze(2).to_broadcast([P, MT, heads, n])
                q = [x[:, 0:MT * heads * n].rearrange("p (m h d) -> p m h d", m=MT, h=heads) for x in tmp]
                ch.wait()
                ch.add(nc.vector.tensor_tensor(q[0], x1, cs, ALU.mult))
                ch.add(nc.vector.tensor_tensor(q[1], x2, sn, ALU.mult))
                ch.add(nc.vector.tensor_tensor(q[2], x2, cs, ALU.mult))
                ch.add(nc.vector.tensor_tensor(q[3], x1, sn, ALU.mult))
                ch.wait()
                ch.add(nc.vector.tensor_tensor(x1, q[0], q[1], ALU.subtract))
                ch.add(nc.vector.tensor_tensor(x2, q[2], q[3], ALU.add))

        ROPE_STEPS = ANGLE_STEPS + 30

        def odd_act_tables(act):
            act.wait_ge(r_ch, ANGLE_STEPS)
            nc.scalar.activation(rope_tab[:], rope_tab[:], ACT.Sin).then_inc(r_sn, 1)

        def ret_pool(pool):
            pool.wait_ge(r_ch, ROPE_STEPS)
            with pool.Fori(0, RH) as h:
                pool.wait_ge(t_o, h + 1)
                for src, dst in ((RQ_, R_q), (RK_, R_k), (RV_, R_v)):
                    nc.gpsimd.tensor_copy(dst, Zo[:, :, bass.ds(h * RD + src, RD)]).then_inc(r_pool, 1)

        def ret_pe(pe):
            pe.sem_inc(t_o, 1)
            with pe.Fori(0, RH) as h:
                pe.wait_ge(r_pool, h * 3 + 3)
                for i, s in enumerate((R_q, R_k)):
                    for m in range(MT):
                        t = nc.tensor.transpose(PB[:, i, m * P:(m + 1) * P], s[:, m, :], ident[:])
                    t.then_inc(t_mm, 1)
                pe.wait_ge(t_ev, h * 2 + 2)
                for j in range(MT):
                    nc.tensor.matmul(PB[:, 2 + j, 0:T - j * P], RkT[:, j * P:(j + 1) * P], RqT[:, j * P:T],
                                     start=True, stop=True).then_inc(t_s, 1)
                for i in range(MT):
                    pe.wait_ge(t_d, h * MT + i + 1)
                    if i == 0:
                        pe.wait_ge(t_c, h * 5 + 1)
                    for j in range(i + 1):
                        t = nc.tensor.matmul(PB[:, 6, i * P:(i + 1) * P], Rs[j][:, (i - j) * P:(i - j + 1) * P],
                                             R_v[:, j, :], start=(j == 0), stop=(j == i))
                t.then_inc(t_o, 1)

        def ret_act(act):
            p_od.wait_all(act)
            nc.scalar.activation(gate_s[:], Zo[:, :, GT_:GT_ + 24], ACT.Sigmoid).then_inc(o_gate, 1)
            act.wait_ge(r_ch, ROPE_STEPS)
            with act.Fori(0, RH) as h:
                for i, dst in enumerate((RqT, RkT)):
                    act.wait_ge(t_mm, h * 2 + i + 1)
                    nc.scalar.activation(dst, PB[:, i, :], ACT.Copy).then_inc(t_ev, 1)
                act.wait_ge(t_y, h + 1)
                nc.scalar.activation(SBI[:, 0, :].rearrange("p (m d) -> p m d", m=MT),
                                     Zo[:, :, bass.ds(h * RD + RG_, RD)], ACT.Silu).then_inc(t_g, 1)
                act.wait_ge(t_c, h * 5 + 5)
                nc.scalar.activation(stat[:, 48:52], stat[:, 44:48], ACT.Sqrt, bias=stat[:, 61:62], scale=1.0 / RD
                                     ).then_inc(t_sd, 1)

        def ret_dve(dve):
            dve.sem_inc(t_c, 1)
            dve.sem_inc(t_y, 1)
            with dve.Fori(0, RH) as h:
                for j in range(MT):
                    dve.wait_ge(t_s, h * MT + j + 1)
                    w = T - j * P
                    nc.vector.tensor_tensor(Rs[j], PB[:, 2 + j, 0:w],
                                            decay[:, bass.ds(h, 1), 0:w].rearrange("p a w -> p (a w)"), ALU.mult
                                            ).then_inc(t_d, 1)
                dve.wait_ge(t_o, h + 2)
                o = PB[:, 6, :].rearrange("p (m d) -> p m d", m=MT)
                ch = Chain(dve, t_c, h * 5 + 1)
                nc.vector.tensor_reduce(stat[:, 40:44], o, AX.X, ALU.add).then_inc(t_sd2, 1)
                dve.wait_ge(t_sd2, h * 3 + 1)
                nc.vector.tensor_scalar(stat[:, 40:44], stat[:, 40:44], 1.0 / RD, None, ALU.mult).then_inc(t_sd2, 1)
                dve.wait_ge(t_sd2, h * 3 + 2)
                nc.vector.tensor_tensor(Rc, o, stat[:, 40:44].unsqueeze(2).to_broadcast([P, MT, RD]), ALU.subtract
                                        ).then_inc(t_sd2, 1)
                dve.wait_ge(t_sd2, h * 3 + 3)
                ch.add(nc.vector.tensor_tensor(Rsq, Rc, Rc, ALU.mult))
                ch.wait()
                ch.add(nc.vector.tensor_reduce(stat[:, 44:48], Rsq, AX.X, ALU.add))
                ch.wait()
                g = gnr.rearrange("p (h d) -> p h d", h=RH)[:, bass.ds(h, 1), :].to_broadcast([P, MT, RD])
                ch.add(nc.vector.tensor_tensor(Rc, Rc, g, ALU.mult))
                ch.wait()
                dve.wait_ge(t_g, h + 1)
                ch.add(nc.vector.tensor_tensor(Rc, Rc, SBI[:, 0, :].rearrange("p (m d) -> p m d", m=MT), ALU.mult))
                dve.wait_ge(t_sd, h + 1)
                ch.wait()
                ch.add(nc.vector.reciprocal(stat[:, 52:56], stat[:, 48:52]))
                ch.wait()
                nc.vector.tensor_tensor(Y[:, :, bass.ds(h * RD + 512, RD)], Rc,
                                        stat[:, 52:56].unsqueeze(2).to_broadcast([P, MT, RD]), ALU.mult
                                        ).then_inc(t_y, 1)

        t_sd2 = sem("ret_center")

        c_t = sem("cmp_T_mm")
        c_b = sem("cmp_blocks")
        c_g = sem("cmp_gelu")
        c_m = sem("cmp_out_mm")
        c_o = sem("cmp_out")

        def cmp_blk(i):
            return HT[0:DH, 4 * i:4 * i + 4, :].rearrange("p a b -> p (a b)")[:, 0:CB * 2 * NC].rearrange(
                "p (l g n) -> p l g n", l=CB, g=2)

        def cmp_pe(pe):
            pe.wait_ge(t_d, RH * MT)
            for i, base in enumerate((KC_, VC_)):
                for g in range(2):
                    for m in range(MT):
                        t = nc.tensor.transpose(PB[0:DH, 2 * i + g, m * P:(m + 1) * P],
                                                Zo[:, m, base + g * DH:base + (g + 1) * DH], ident[:])
                    t.then_inc(c_t, 1)
            for i in range(2):
                arrived(pe, cmp_n[i])
                pe.wait_ge(c_b, 2 * i + 2)
                w = RING[0:DH, (cmp_n[i] % 3) * WR:(cmp_n[i] % 3 + 1) * WR].rearrange("p (l n) -> p l n", l=CB)
                blk = cmp_blk(i)
                for l in range(CB):
                    t = nc.tensor.matmul(PB[:, 4 + i, 0:2 * NC], w[:, l, :], blk[:, l, :, :], start=(l == 0), stop=(l == CB - 1))
                t.then_inc(c_h, 1)
            pe.wait_ge(c_g, 2)
            nc.tensor.matmul(PB[0:DH, 0, 0:2 * NC], cmpw2[:, 0, :], hidc[:, 0, :], start=True, stop=True).then_inc(c_m, 1)
            for g in range(2):
                nc.tensor.matmul(PB[0:NC, 1 + g, 0:DH], hidc[:, 1, g * NC:(g + 1) * NC], cmpw2[:, 1, :],
                                 start=True, stop=True).then_inc(c_m, 1)

        def cmp_dve(dve):
            dve.wait_ge(t_o, RH + 1)
            for i in range(2):
                for g in range(2):
                    dve.wait_ge(c_t, 2 * i + g + 1)
                    src = PB[0:DH, 2 * i + g, :]
                    win = bass.AP(src.tensor, src.offset, [list(src.ap[0]), [1, CB], [CS, NC]])
                    pos = cmpos[:, i, :].unsqueeze(2).to_broadcast([DH, CB, NC])
                    nc.vector.tensor_tensor(cmp_blk(i)[:, :, g, :], win, pos, ALU.add).then_inc(c_b, 1)
            dve.wait_ge(c_m, 1)
            nc.vector.tensor_copy(kcT[:].rearrange("p g n -> p (g n)"), PB[0:DH, 0, 0:2 * NC]).then_inc(c_o, 1)
            for g in range(2):
                dve.wait_ge(c_m, 2 + g)
                nc.vector.tensor_copy(vcc[:, g, :], PB[0:NC, 1 + g, 0:DH]).then_inc(c_o, 1)

        def cmp_act(act):
            for i in range(2):
                act.wait_ge(c_h, i + 1)
                nc.scalar.activation(hidc[:, i, :], PB[:, 4 + i, 0:2 * NC], ACT.Gelu_apprx_tanh).then_inc(c_g, 1)

        class Attention:

            def __init__(self, name, pairs, units, staged, kinds):
                self.name, self.pairs, self.units, self.staged = name, pairs, units, staged
                self.NU = len(units)
                self.stg = sem(name + "_staged")
                self.tm = sem(name + "_T_mm")
                self.te = sem(name + "_T")
                self.qk = sem(name + "_scores_mm")
                self.mx = sem(name + "_max")
                self.bi = sem(name + "_biased")
                self.ex = sem(name + "_exp")
                self.tr = sem(name + "_PT_mm")
                self.pa = sem(name + "_PT_even")
                self.pd = sem(name + "_PT_odd")
                self.pv = sem(name + "_out_mm")
                self.sc = sem(name + "_scale")
                self.oe = sem(name + "_out")
                self.nb = sum(u["bias"] is not None for u in units)

            def pe(self, pe):
                us, NU = self.units, self.NU

                def scores(it, u):
                    x = us[u]
                    w = x["w"]
                    s = PB[:, u % 2, 0:w]
                    m = x["i"]
                    nc_ = nc.tensor.matmul(s, x["qT"][:, m * P:(m + 1) * P], x["kT"][:, 0:w], start=True,
                                           stop=x["mask"] is None)
                    if x["mask"] is not None:
                        mask, c0 = x["mask"]
                        nc_ = nc.tensor.matmul(PB[:, u % 2, c0:w], ident_b[:], mask, start=False, stop=True)
                    nc_.then_inc(self.qk, 1)

                def turned(it, u):
                    x = us[u]
                    pe.wait_ge(self.ex, it * NU + u + 1)
                    w = x["w"]
                    for b in range((w + P - 1) // P):
                        bw = min(P, w - b * P)
                        t = nc.tensor.transpose(PB[0:bw, 2 + u % 2, b * P:(b + 1) * P],
                                                PR[:, u % 2, b * P:b * P + bw], ident[:])
                    t.then_inc(self.tr, 1)

                def values(it, u):
                    x = us[u]
                    if u % 2 == 0:
                        pe.wait_ge(self.pa, it * (NU // 2) + u // 2 + 1)
                    else:
                        pe.wait_ge(self.pd, it * (NU // 2) + u // 2 + 1)
                    pe.wait_ge(self.oe, it * NU + u + 1)
                    w = x["w"]
                    n = (w + P - 1) // P
                    for b in range(n):
                        bw = min(P, w - b * P)
                        t = nc.tensor.matmul(PB[:, 4 + u % 2, 0:DH], PTS[0:bw, u % 2, b, :], x["v"](b)[0:bw],
                                             start=(b == 0), stop=(b == n - 1))
                    t.then_inc(self.pv, 1)

                with pe.Fori(0, self.pairs) as it:
                    ns = len(self.staged)
                    pe.wait_ge(self.stg, it * self.n_pool + self.n_pool)
                    for k, (src, dst, scale) in enumerate(self.staged):
                        if k >= 2:
                            pe.wait_ge(self.te, it * ns + k - 1)
                        rows = src.shape[2]
                        nc.tensor.matmul(PB[0:DH, 6 + k % 2, 0:8], ident[:, 0:DH], ident[:, 0:8], start=True, stop=True)
                        for m in range(MT):
                            t = nc.tensor.transpose(PB[0:rows, 6 + k % 2, m * P:(m + 1) * P], src[:, m, :], ident[:])
                        t.then_inc(self.tm, 1)
                    pe.wait_ge(self.te, it * ns + ns)
                    scores(it, 0)
                    scores(it, 1)
                    for u in range(NU):
                        turned(it, u)
                        if u + 2 < NU:
                            scores(it, u + 2)
                        if u >= 1:
                            values(it, u - 1)
                    values(it, NU - 1)

            def act(self, act):
                us, NU = self.units, self.NU

                def exps(it, u):
                    x = us[u]
                    act.wait_ge(self.mx, it * NU + u + 1)
                    src = PB[:, u % 2, 0:x["w"]] if x["bias"] is None else SBI[:, u % 2, 0:x["w"]]
                    nc.scalar.activation(PR[:, u % 2, 0:x["w"]], src, ACT.Exp, bias=nmx[:, u % 2:u % 2 + 1],
                                         accum_out=den[:, u % 8:u % 8 + 1]).then_inc(self.ex, 1)

                with act.Fori(0, self.pairs) as it:
                    ns = len(self.staged)
                    for k, (src, dst, scale) in enumerate(self.staged):
                        act.wait_ge(self.tm, it * ns + k + 1)
                        nc.scalar.activation(dst, PB[0:src.shape[2], 6 + k % 2, :], ACT.Copy, scale=scale
                                             ).then_inc(self.te, 1)
                    exps(it, 0)
                    for u in range(NU):
                        if u + 1 < NU:
                            exps(it, u + 1)
                        if u % 2 == 0:
                            self.out_T(act, it, u)

            def out_T(self, eng, it, u):
                x = self.units[u]
                w = x["w"]
                eng.wait_ge(self.tr, it * self.NU + u + 1)
                rows = min(w, P)
                n = (w + P - 1) // P
                src = PB[0:rows, 2 + u % 2, 0:n * P]
                dst = PTS[0:rows, u % 2, 0:n, :].rearrange("p a b -> p (a b)")
                if u % 2 == 0:
                    nc.scalar.activation(dst, src, ACT.Copy).then_inc(self.pa, 1)
                else:
                    nc.vector.tensor_copy(dst, src).then_inc(self.pd, 1)

            def dve(self, dve):
                us, NU = self.units, self.NU
                ns_ = sum(1 if x["gate"] is None else (3 if x["valid"] else 2) for x in us)
                dve.sem_inc(self.oe, 2)

                def maxima(it, u):
                    x = us[u]
                    w = x["w"]
                    dve.wait_ge(self.qk, it * NU + u + 1)
                    src = PB[:, u % 2, 0:w]
                    if x["bias"] is not None:
                        nb_ = sum(y["bias"] is not None for y in us[:u + 1])
                        nc.vector.tensor_tensor(SBI[:, u % 2, 0:w], src, x["bias"](it), ALU.add).then_inc(self.bi, 1)
                        dve.wait_ge(self.bi, it * self.nb + nb_)
                        src = SBI[:, u % 2, 0:w]
                    nc.vector.tensor_reduce(nmx[:, u % 2:u % 2 + 1], src, AX.X, ALU.max, negate=True).then_inc(self.mx, 1)

                def add_out(it, u, cnt):
                    x = us[u]
                    dve.wait_ge(self.pv, it * NU + u + 1)
                    r = osc[:, u % 8:u % 8 + 1]

                    def step(ins):
                        cnt[0] += 1
                        ins.then_inc(self.sc, 1)
                        dve.wait_ge(self.sc, it * ns_ + cnt[0])
                    step(nc.vector.reciprocal(r, den[:, u % 8:u % 8 + 1]))
                    if x["gate"] is not None:
                        step(nc.vector.tensor_tensor(r, r, x["gate"](it), ALU.mult))
                        if x["valid"]:
                            step(nc.vector.tensor_tensor(r, r, cvalid[:, x["i"]:x["i"] + 1], ALU.mult))
                    y = x["y"](it)
                    if x["first"]:
                        nc.vector.tensor_scalar(y, PB[:, 4 + u % 2, 0:DH], r, None, ALU.mult).then_inc(self.oe, 1)
                    else:
                        dve.wait_ge(self.oe, it * NU + u + 2)
                        nc.vector.scalar_tensor_tensor(y, PB[:, 4 + u % 2, 0:DH], r, y, ALU.mult, ALU.add
                                                       ).then_inc(self.oe, 1)

                with dve.Fori(0, self.pairs) as it:
                    cnt = [0]
                    maxima(it, 0)
                    maxima(it, 1)
                    for u in range(NU):
                        if u % 2 == 1:
                            self.out_T(dve, it, u)
                        if u + 2 < NU:
                            maxima(it, u + 2)
                        if u >= 1:
                            add_out(it, u - 1, cnt)
                    add_out(it, NU - 1, cnt)

            def done(self, eng):
                eng.wait_ge(self.oe, 2 + self.pairs * self.NU)

        stv = lambda k, w: ST[:, k * 264:k * 264 + MT * w].rearrange("p (m d) -> p m d", m=MT)
        nsa_kT = sb("nsa_kT", [DH, 2, 2, T]) if False else None
        ksT = [HT[0:DH, 0 + g, :] for g in range(2)]
        kwT = [HT[0:DH, 2 + g, :] for g in range(2)]
        qTn = [HT[0:DH, 4 + g, :] for g in range(2)]
        k_mm = sem("nsa_kT_mm")
        k_ev = sem("nsa_kT")

        def unit(i, w, qT, kT, mask, v, y, gate=None, valid=False, bias=None, first=True):
            return dict(i=i, w=w, qT=qT, kT=kT, mask=mask, v=v, y=y, gate=gate, valid=valid, bias=bias, first=first)

        nsa_units = []
        for g in range(2):
            for i in range(MT):
                y = lambda it, g=g, i=i: Y[:, i, bass.ds(it * DH + g * 4 * DH, DH)]
                gate = lambda c, g=g, i=i: (lambda it: gate_s[:, i, bass.ds(it * 3 + (12 * g + c), 1)])
                w = (i + 1) * P
                nsa_units += [
                    unit(i, NC, qTn[g], kcT[:, g, :], (cmask_b[:, i, 0:NC], 0), lambda b, g=g: vcc[:, g, :], y, gate(0), True),
                    unit(i, w, qTn[g], ksT[g], (causal_b[:], i * P),
                         lambda b, g=g: Zo[:, b, VS_ + g * DH:VS_ + (g + 1) * DH], y, gate(1), first=False),
                    unit(i, w, qTn[g], kwT[g], (causal_b[:], i * P),
                         lambda b, g=g: Zo[:, b, VW_ + g * DH:VW_ + (g + 1) * DH], y, gate(2), first=False)]
        nsa = Attention("nsa", 4, nsa_units, [(stv(g, DH), qTn[g], 0.125) for g in range(2)], None)
        nsa.n_pool = 2

        def nsa_pool(pool):
            pool.wait_ge(t_o, RH + 1)
            pool.sem_inc(nsa_free, 2)
            with pool.Fori(0, 4) as it:
                pool.wait_ge(nsa.tm, it * 2)
                for g in range(2):
                    nc.gpsimd.tensor_copy(stv(g, DH), Zo[:, :, bass.ds(it * DH + g * 4 * DH, DH)]).then_inc(nsa.stg, 1)

        nsa_free = sem("nsa_free")

        def nsa_keys_pe(pe):
            pe.wait_ge(c_o, 3)
            for k, (base, g) in enumerate(((KS_, 0), (KS_, 1), (KW_, 0), (KW_, 1))):
                for m in range(MT):
                    t = nc.tensor.transpose(PB[0:DH, k, m * P:(m + 1) * P], Zo[:, m, base + g * DH:base + (g + 1) * DH],
                                            ident[:])
                t.then_inc(k_mm, 1)
            pe.wait_ge(k_ev, 4)

        def nsa_keys_act(act):
            for k, dst in enumerate(ksT + kwT):
                act.wait_ge(k_mm, k + 1)
                nc.scalar.activation(dst, PB[0:DH, k, :], ACT.Copy).then_inc(k_ev, 1)

        n_y1 = Norm("y1", Y, (nsa.oe, lambda m: 2 + nsa.pairs * nsa.NU), [(0, D)], normed=False)
        d_od = Down("od_out", KT, a["od_w_out"][0], 2, lambda eng: eng.wait_ge(*n_y1.ready_tile(MT - 1)))
        n4 = Norm("n4", X, d_od.ready(), [(0, D)], gain=3)
        f1 = GateUp("ffn1", n4, a["ffn_w_gate"][1], a["ffn_w_up"][1])
        d_f1 = Down("ffn1_down", FT, a["ffn_w_down"][1], 3, f1.done)
        n5 = Norm("n5", X, d_f1.ready(), [(0, D)], gain=4)
        Z2 = Z[:, 0:MT * W2].rearrange("p (m n) -> p m n", m=MT)
        p_2 = Proj("in2", n5, a["w_in_2"][0], W2, Z2, alt)

        lf = sb("lf", [P, MT, NH])
        lt = sb("lt", [P, 3, MT, NH])
        c8 = sb("c8", [P, 2, MT, NH])
        bfr = sb("bfr", [P, NH])
        rb = sb("rb", [NH * 4, NH])
        s_2 = sem("second_consts")
        g_ch = sem("forget_chain")
        g_ex = sem("forget_exp")
        g_mm = sem("forget_cumsum_mm")
        g_c = sem("forget_c8")
        b_mm = sem("bias_row_mm")
        b_sb = sem("bias_row")
        b_dr = sem("bias_row_dram")
        b_ld = sem("bias_table")
        onehot = GP_onehot = None
        bias_row = Z[0:NH, 13000:13000 + 0] if False else None

        def forget_dve(dve):
            dve.wait_ge(s_2, 16 * 2)
            p_2.wait_all(dve)
            ch = Chain(dve, g_ch)
            ch.add(nc.vector.tensor_tensor(lf[:], Z2[:, :, FP_:FP_ + NH], bfr[:].unsqueeze(1).to_broadcast([P, MT, NH]), ALU.add))
            ch.wait()
            ch.add(nc.vector.tensor_scalar(lt[:, 0], lf[:], -1.0, None, ALU.mult))
            ch.wait()
            ch.add(nc.vector.tensor_tensor(lt[:, 1], lt[:, 0], lf[:], ALU.min))
            ch.add(nc.vector.tensor_scalar(lf[:], lf[:], 0.0, None, ALU.min))
            dve.wait_ge(g_ex, 2)
            ch.wait()
            ch.add(nc.vector.tensor_tensor(lf[:], lf[:], lt[:, 2], ALU.subtract))
            dve.wait_ge(g_mm, 1)
            nc.vector.tensor_scalar(c8[:, 0], PB[:, 6, 0:MT * NH].rearrange("p (m h) -> p m h", m=MT), 8.0, None, ALU.mult
                                    ).then_inc(g_c, 1)
            nc.vector.tensor_scalar(c8[:, 1], PB[:, 6, 0:MT * NH].rearrange("p (m h) -> p m h", m=MT), -8.0, None, ALU.mult
                                    ).then_inc(g_c, 1)

        def forget_act(act):
            act.wait_ge(g_ch, 3)
            nc.scalar.activation(lt[:, 2], lt[:, 1], ACT.Exp).then_inc(g_ex, 1)
            act.wait_ge(g_ex, 1)
            nc.scalar.activation(lt[:, 2], lt[:, 2], ACT.Ln, bias=1.0).then_inc(g_ex, 1)

        def forget_pe(pe):
            pe.wait_ge(g_ch, 5)
            for m in range(MT):
                for j in range(m + 1):
                    t = nc.tensor.matmul(PB[:, 6, m * NH:(m + 1) * NH], upper[:] if j == m else ones[:], lf[:, j, :],
                                         start=(j == 0), stop=(j == m))
            t.then_inc(g_mm, 1)

        ohot = ST[0:NH * 4, 0:TW]
        brow = ST[0:NH, TW:2 * TW]
        badd = ST[0:NH, 2 * TW:3 * TW]

        def bias_pe(pe):
            pe.wait_ge(s_2, 16 * 2)
            pe.wait_ge(s_2b, 16 * 2)
            for k, (c0, c1) in enumerate(((0, 512), (512, TW))):
                t = nc.tensor.matmul(PB[0:NH, 6 + k, 0:c1 - c0], rb[:], ohot[:, c0:c1], start=True, stop=True)
            t.then_inc(b_mm, 1)

        s_2b = sem("bias_consts")

        def bias_dve(dve):
            dve.wait_ge(b_mm, 1)
            for k, (c0, c1) in enumerate(((0, 512), (512, TW))):
                nc.vector.tensor_tensor(brow[:, c0:c1], PB[0:NH, 6 + k, 0:c1 - c0], badd[:, c0:c1], ALU.add).then_inc(b_sb, 1)

        b_rev = sem("bias_turned")
        bias_raw = ST[:, 0:4 * T].rearrange("p (h t) -> p h t", h=4)

        def bias_turn_dve(dve, half):
            dve.wait_ge(b_ld, 16 * (half + 1))
            nc.vector.tensor_copy(BIAS[:, 4 * half:4 * half + 4, :], bias_raw[:, :, T - 1::-1]).then_inc(b_rev, 1)

        def st2(k, w):
            return STG[:, k * 264:k * 264 + MT * w].rearrange("p (m d) -> p m d", m=MT)

        STG = sb("STG", [P, 12 * 264 - 2112])
        def st2(k, w):
            buf, kk = (ST, k) if k < 8 else (STG, k - 8)
            return buf[:, kk * 264:kk * 264 + MT * w].rearrange("p (m d) -> p m d", m=MT)

        two_units = []
        staged = []
        for p in range(2):
            w66 = DH + 2
            qd, kd, qf, kf = [HT[0:(DH if t < 2 else w66), 4 * p + t, :] for t in range(4)]
            staged += [(st2(6 * p + 0, DH), qd, 0.125), (st2(6 * p + 1, DH), kd, 1.0),
                       (st2(6 * p + 2, w66), qf, 0.125), (st2(6 * p + 3, w66), kf, 1.0)]
            for i in range(MT):
                w = (i + 1) * P
                for k, (q_, k_, base) in enumerate(((qd, kd, 0), (qf, kf, 512))):
                    y = lambda it, p=p, i=i, base=base: Y[:, i, bass.ds(it * 2 * DH + (p * DH + base), DH)]
                    v = lambda b, p=p, k=k: st2(6 * p + 4 + k, DH)[:, b, :]
                    if k == 0:
                        bias = lambda it, p=p, i=i, w=w: BIAS[:, bass.ds(it * 2 + p, 1), T - w:T].rearrange("p a w -> p (a w)")
                        two_units.append(unit(i, w, q_, k_, None, v, y, bias=bias))
                    else:
                        two_units.append(unit(i, w, q_, k_, (causal_b[:], i * P), v, y))
        two = Attention("two", 4, two_units, staged, None)
        two.n_pool = 18
        s_one = sem("staged_ones")
        v_free = sem("two_v_free")

        def two_pool(pool):
            pool.wait_ge(nsa.tm, 8)
            for p in range(2):
                nc.gpsimd.memset(st2(6 * p + 2, DH + 2)[:, :, DH + 1:DH + 2], 1.0).then_inc(s_one, 1)
                nc.gpsimd.memset(st2(6 * p + 3, DH + 2)[:, :, DH:DH + 1], 1.0).then_inc(s_one, 1)
            pool.wait_ge(g_c, 2)
            pool.wait_ge(s_one, 4)
            p_2.wait_all(pool)
            with pool.Fori(0, 4) as it:
                pool.wait_ge(two.oe, it * two.NU + 2)
                for p in range(2):
                    def z(base):
                        return Z2[:, :, bass.ds(it * 2 * DH + (p * DH + base), DH)]
                    h = lambda k: c8[:, k, :, bass.ds(it * 2 + p, 1)]
                    for k, src in enumerate((QA_, KA_, QF_, KF_, VA_, VF_)):
                        dst = st2(6 * p + k, DH + 2 if k in (2, 3) else DH)
                        nc.gpsimd.tensor_copy(dst[:, :, 0:DH], z(src)).then_inc(two.stg, 1)
                    nc.gpsimd.tensor_copy(st2(6 * p + 2, DH + 2)[:, :, DH:DH + 1], h(0)).then_inc(two.stg, 1)
                    nc.gpsimd.tensor_copy(st2(6 * p + 3, DH + 2)[:, :, DH + 1:DH + 2], h(1)).then_inc(two.stg, 1)
        two.n_pool = 16

        n_y2 = Norm("y2", Y, (two.oe, lambda m: 2 + two.pairs * two.NU), [(0, 512), (512, D)], gain=5)
        d_2 = Down("out2", KT, a["w_out_2"][0], None, lambda eng: eng.wait_ge(*n_y2.ready_tile(MT - 1)))
        n6 = Norm("n6", X, d_2.ready(), [(0, D)], rows=GP[:, 0, :])

        o_ = [0]
        Zr = lambda words: (Z[:, o_[0]:o_[0] + words], o_.__setitem__(0, o_[0] + words))[0]
        wrt = Zr(KT * 36).rearrange("p (k n) -> p k n", k=KT)
        brt = Zr(36)
        strict = Zr(P)
        o_io = o_[0]
        io128, io40, tokid, pri = Zr(P), Zr(NB), Zr(MT), Zr(EG)
        lg = Zr(MT * 36).rearrange("p (m n) -> p m n", m=MT)
        L = lambda n: Zr(MT * n).rearrange("p (m n) -> p m n", m=MT)
        gm, g_oh, g_t, g1 = L(1), L(4), L(4), L(1)
        sel, se_t = L(EG), L(EG)
        oh1, oh2 = L(EG), L(EG)
        v1, v2, w1_, w2_, pm = L(1), L(1), L(1), L(1), L(1)
        a1, a2, aa = L(NE), L(NE), L(NE)
        rank, t32 = L(NE), L(NE)
        cnt_ = Zr(NE)
        nblk = Zr(NE)
        bend, bst, t32b = Zr(NE), Zr(NE), Zr(NE)
        slot1, slot2 = L(1), L(1)
        blk_ = L(1)
        si = sb("slot_i", [P, 2, MT], i32)
        idxf = Zr(NB)
        idxi = sb("idx_i", [P, NB + 2], i32)
        bex = Zr(NO * NE).rearrange("p (b e) -> p b e", e=NE)
        bexs = Zr(NO)
        bexi = sb("block_expert", [P, NB], i32)
        ohp = Zr(2 * P).rearrange("p (s n) -> p s n", s=2)
        ohb = Zr(2 * NB).rearrange("p (s n) -> p s n", s=2)
        moe0 = o_[0]
        s_rc = sem("router_consts")
        q_mm = sem("router_logits_mm")
        q_ch = sem("router_chain")
        q_ex = sem("router_exp")
        q_rk = sem("router_rank_mm")
        q_oh = sem("router_onehot")
        q_id = sem("router_index_mm")
        q_done = sem("router_done")
        s_h2 = sem("h2_rows_stored")

        def bc(x, n):
            return x.to_broadcast([P, MT, n])

        def router_pe(pe):
            pe.wait_ge(s_rc, 16 * 7)
            pe.wait_ge(*n6.ready_tile(MT - 1))
            for m in range(MT):
                for k in range(KT):
                    t = nc.tensor.matmul(PB[:, 4, m * 36:(m + 1) * 36], HT[:, k, m * P:(m + 1) * P], wrt[:, k, :],
                                         start=(k == 0), stop=(k == KT - 1))
            t.then_inc(q_mm, 1)
            pe.wait_ge(q_done, 1)
            for m in range(MT):
                for j in range(m + 1):
                    t = nc.tensor.matmul(PB[:, 5, m * NE:(m + 1) * NE], strict if j == m else ones[:], aa[:, j, :],
                                         start=(j == 0), stop=(j == m))
            t.then_inc(q_rk, 1)
            for j in range(MT):
                t = nc.tensor.matmul(PB[:, 6, 0:NE], ones[:], aa[:, j, :], start=(j == 0), stop=(j == MT - 1))
            t.then_inc(q_rk, 1)
            for n in range(2 * MT):
                pe.wait_ge(q_oh, 2 * (n + 1))
                nc.tensor.matmul(PB[:, 7, 0:NB], ohp[:, n % 2, :], ohb[:, n % 2, :], start=(n == 0), stop=(n == 2 * MT - 1)
                                 ).then_inc(q_id, 1)

        def router_act(act):
            act.wait_ge(q_ch, 3)
            nc.scalar.activation(g_t, g_t, ACT.Exp).then_inc(q_ex, 1)
            act.wait_ge(q_ch, ROUTER_V)
            nc.scalar.activation(w2_, w2_, ACT.Exp).then_inc(q_ex, 1)

        ROUTER_V = 31

        def router_dve(dve):
            dve.wait_ge(s_rc, 16 * 7)
            dve.wait_ge(q_mm, 1)
            ch = Chain(dve, q_ch)

            def tt(o, x, y, op):
                ch.wait() if ch.n else None
                ch.add(nc.vector.tensor_tensor(o, x, y, op))

            def ts(o, x, s1, s2, op0, op1=None):
                ch.wait()
                ch.add(nc.vector.tensor_scalar(o, x, s1, s2, op0, op1) if op1 is not None
                       else nc.vector.tensor_scalar(o, x, s1, None, op0))

            def red(o, x, op):
                ch.wait()
                ch.add(nc.vector.tensor_reduce(o, x, AX.X, op))

            def first_max(oh, x, mx_, n, tmp):
                tt(oh, x, bc(mx_, n), ALU.is_equal)
                tt(tmp, oh, pri[:, 0:n].unsqueeze(1).to_broadcast([P, MT, n]), ALU.mult)
                red(pm, tmp, ALU.max)
                tt(oh, tmp, bc(pm, n), ALU.is_equal)

            tt(lg, PB[:, 4, 0:MT * 36].rearrange("p (m n) -> p m n", m=MT), brt.unsqueeze(1).to_broadcast([P, MT, 36]), ALU.add)
            red(gm, lg[:, :, 0:4], ALU.max)
            tt(g_t, lg[:, :, 0:4], bc(gm, 4), ALU.subtract)
            dve.wait_ge(q_ex, 1)
            red(g1, g_t, ALU.add)
            ch.wait()
            ch.add(nc.vector.reciprocal(g1, g1))
            first_max(g_oh, lg[:, :, 0:4], gm, 4, g_t)
            le = lg[:, :, 4:36].rearrange("p m (g e) -> p m g e", g=NG)
            for g in range(NG):
                if g == 0:
                    tt(sel, le[:, :, 0, :], bc(g_oh[:, :, 0:1], EG), ALU.mult)
                else:
                    tt(se_t, le[:, :, g, :], bc(g_oh[:, :, g:g + 1], EG), ALU.mult)
                    tt(sel, sel, se_t, ALU.add)
            red(v1, sel, ALU.max)
            first_max(oh1, sel, v1, EG, se_t)
            ts(se_t, oh1, -3.0e38, None, ALU.mult)
            tt(sel, sel, se_t, ALU.add)
            red(v2, sel, ALU.max)
            first_max(oh2, sel, v2, EG, se_t)
            tt(w2_, v2, v1, ALU.subtract)
            for g in range(NG):
                o4 = lambda x: x.rearrange("p m (g e) -> p m g e", g=NG)[:, :, g, :]
                tt(o4(a1), oh1, bc(g_oh[:, :, g:g + 1], EG), ALU.mult)
                tt(o4(a2), oh2, bc(g_oh[:, :, g:g + 1], EG), ALU.mult)
            ch.wait()
            nc.vector.tensor_tensor(aa, a1, a2, ALU.add).then_inc(q_done, 1)
            dve.wait_ge(q_ex, 2)
            ts(w1_, w2_, 1.0, None, ALU.add)
            ch.wait()
            ch.add(nc.vector.reciprocal(w1_, w1_))
            tt(w2_, w2_, w1_, ALU.mult)
            tt(w1_, w1_, g1, ALU.mult)
            tt(w2_, w2_, g1, ALU.mult)
            dve.wait_ge(q_rk, 2)
            ch.wait()
            ch.add(nc.vector.tensor_copy(cnt_, PB[:, 6, 0:NE]))
            ch.wait()
            ch.add(nc.vector.tensor_copy(rank, PB[:, 5, 0:MT * NE].rearrange("p (m n) -> p m n", m=MT)))
            ts(nblk, cnt_, float(P), None, ALU.is_gt)
            for j in range(2, MT):
                ts(t32b, cnt_, float(j * P), None, ALU.is_gt)
                tt(nblk, nblk, t32b, ALU.add)
            ts(t32b, nblk, 0.0, None, ALU.mult)
            ch.wait()
            ch.add(nc.vector.tensor_tensor_scan(bend, nblk, t32b, 0.0, ALU.add, ALU.add))
            tt(bst, bend, nblk, ALU.subtract)
            tt(bex, bend.unsqueeze(1).to_broadcast([P, NO, NE]), io40[:, 0:NO].unsqueeze(2).to_broadcast([P, NO, NE]), ALU.is_le)
            red(bexs, bex, ALU.add)
            ts(bexs, bexs, float(NE - 1), None, ALU.min)
            ch.wait()
            ch.add(nc.vector.tensor_copy(bexi[:, NE:NB], bexs))
            ch.add(nc.vector.tensor_copy(bexi[:, 0:NE], io40[:, 0:NE]))
            ts(bst, bst, float(NE - 1), float(P), ALU.add, ALU.mult)
            tt(bst, bst, io40x[:, 0:NE], ALU.subtract)
            ts(t32, rank, float(P), None, ALU.is_ge)
            tt(t32, t32, bst.unsqueeze(1).to_broadcast([P, MT, NE]), ALU.mult)
            tt(rank, rank, t32, ALU.add)
            tt(rank, rank, io40x[:, 0:NE].unsqueeze(1).to_broadcast([P, MT, NE]), ALU.add)
            n = 0
            for k, (as_, sl) in enumerate(((a1, slot1), (a2, slot2))):
                tt(t32, rank, as_, ALU.mult)
                red(sl, t32, ALU.add)
                ch.wait()
                ch.add(nc.vector.tensor_copy(si[:, k, :], sl.rearrange("p m a -> p (m a)")))
                tt(bex2, bc(sl, NB), io40x.unsqueeze(1).to_broadcast([P, MT, NB]), ALU.is_ge)
                red(blk_, bex2, ALU.add)
                ts(blk_, blk_, 1.0, None, ALU.subtract)
                ts(pm, blk_, -float(P), None, ALU.mult)
                tt(pm, pm, sl, ALU.add)
                for m in range(MT):
                    if n >= 2:
                        dve.wait_ge(q_id, n - 1)
                    ch.wait()
                    nc.vector.tensor_scalar(ohp[:, n % 2, :], io128, pm[:, m, :], None, ALU.is_equal).then_inc(q_oh, 1)
                    nc.vector.tensor_scalar(ohb[:, n % 2, :], io40, blk_[:, m, :], tokid[:, m:m + 1], ALU.is_equal, ALU.mult
                                            ).then_inc(q_oh, 1)
                    n += 1
            dve.wait_ge(q_id, 2 * MT)
            ch.add(nc.vector.memset(idxi[:, NB:NB + 2], 0))
            nc.vector.tensor_copy(idxi[:, 0:NB], PB[:, 7, 0:NB]).then_inc(q_done, 1)
            ch.wait()
            dve.wait_ge(q_done, 2)

        bex2 = Zr(MT * NB).rearrange("p (m b) -> p m b", m=MT)
        io40x = Zr(NB)
        moe0 = o_[0]

        Xg = Z[:, moe0:moe0 + 3 * D].rearrange("p (s n) -> p s n", s=3)
        XgT = Y[:].rearrange("p m n -> p (m n)")[:, 0:3 * D].rearrange("p (s k n) -> p s k n", s=3, k=KT)
        Ob = [ST[:, 0:D], ST[:, D:2 * D], Z[:, moe0 + 3 * D:moe0 + 4 * D]]
        Hs, Hh, HhT = [WK[:, i * 768:(i + 1) * 768].rearrange("p (s n) -> p s n", s=3) for i in range(3)]
        assert moe0 + 4 * D <= MT * OD, moe0
        idc = sb("idx_col", [P, 3], i32)
        ht_flat = HT[:].rearrange("p k n -> p (k n)")
        bias_flat = BIAS[:].rearrange("p k n -> p (k n)")
        EGU = [RING[:, 0:4096], RING[:, 4096:8192], ht_flat]
        EDW = [RING[:, 8192:10240], RING[:, 10240:12288], bias_flat[:, 0:2048]]
        m_w = [sem(f"expert_gate_up_w{s}") for s in range(3)]
        m_wd = [sem(f"expert_down_w{s}") for s in range(3)]
        m_idle = sem("idle_steps")
        m_ix = sem("block_index")
        m_g = [sem(f"rows_gathered{s}") for s in range(3)]
        m_t = sem("rows_T_mm")
        m_te = sem("rows_T")
        m_gu = sem("gate_up_mm")
        m_si = sem("expert_silu")
        m_h = sem("expert_hidden")
        m_ht = sem("hidden_T_mm")
        m_he = sem("hidden_T")
        m_d = sem("expert_down_mm")
        m_od = sem("rows_out")
        m_st = [sem(f"rows_stored{s}") for s in range(3)]
        LOOPS = NB // 3 - 1

        def moe_sync(sp):
            def load_gu(s, e):
                gu = EGU[s].rearrange("p (k t n) -> p k t n", k=KT, t=2)
                for t, w in enumerate(("w_expert_gate_2", "w_expert_up_2")):
                    sp.dma_start(gu[:, :, t, :], a[w][0][e].rearrange("a (k p) n -> p (a k) n", p=P)).then_inc(m_w[s], 16)

            def load_d(s, e):
                sp.dma_start(EDW[s].rearrange("p (k n) -> p k n", k=2),
                             a["w_expert_down_2"][0][e].rearrange("a (k p) n -> p (a k) n", p=P)).then_inc(m_wd[s], 16)

            n = len(chunks)
            for c in range(n - 3, n):
                s, v = chunks[c]["done"]
                sp.wait_ge(s, v)
            for s in range(3):
                if s == 2:
                    sp.wait_ge(q_mm, 1)
                load_gu(s, slice(s, s + 1))
                load_d(s, slice(s, s + 1))
            sp.wait_ge(q_done, 2)
            with sp.Fori(0, LOOPS) as it:
                for s in range(3):
                    e = sp.value_load(bexi[0:1, bass.ds(it * 3 + (3 + s), 1)], min_val=0, max_val=NE - 1)
                    sp.wait_ge(m_gu, it * 3 + (s + 1))
                    load_gu(s, bass.ds(e, 1))
                    sp.wait_ge(m_d, it * 6 + (2 * s + 2))
                    load_d(s, bass.ds(e, 1))

        def moe_pool(pool):
            pool.wait_ge(s_h2, 16 * MT)
            pool.sem_inc(m_idle, 1)
            with pool.Fori(0, NB // 3) as it:
                for s in range(3):
                    pool.wait_ge(m_ix, it * 3 + (s + 1))
                    pool.wait_ge(m_idle, it * 3 + (s + 1))
                    nc.gpsimd.tensor_tensor(idle[:, 0:1], idle[:, 1:2], idle[:, 1:2], ALU.mult).then_inc(m_idle, 1)
                    nc.gpsimd.indirect_dma_start(
                        Xg[:, s, :], None, h2_dram[:, :],
                        bass.IndirectOffsetOnAxis(ap=idc[:, s:s + 1], axis=0)).then_inc(m_g[s], 16)

        def moe_pe(pe):
            def turn_rows(it, s):
                if not (isinstance(it, int) and 3 * it + s == 0):
                    pe.wait_ge(m_te, it * 6 + 2 * s)
                pe.wait_ge(m_g[s % 3], it * 16 + 16 * (s // 3 + 1))
                for hf in range(2):
                    for k in range(4):
                        t = nc.tensor.transpose(PB[:, hf, k * P:(k + 1) * P],
                                                Xg[:, s % 3, (4 * hf + k) * P:(4 * hf + k + 1) * P], ident[:])
                    t.then_inc(m_t, 1)

            def gate_up(it, s):
                pe.wait_ge(m_te, it * 6 + (2 * s + 2))
                pe.wait_ge(m_w[s % 3], it * 32 + 32 * (s // 3 + 1))
                gu = EGU[s % 3].rearrange("p (k n) -> p k n", k=KT)
                for k in range(KT):
                    t = nc.tensor.matmul(PB[:, 2 + s % 3, :], XgT[:, s % 3, k, :], gu[:, k, :], start=(k == 0), stop=(k == KT - 1))
                t.then_inc(m_gu, 1)

            def turn_hidden(it, s):
                pe.wait_ge(m_h, it * 3 + (s + 1))
                for j in range(2):
                    t = nc.tensor.transpose(PB[:, 5, j * P:(j + 1) * P], Hh[:, s, j * P:(j + 1) * P], ident[:])
                t.then_inc(m_ht, 1)

            def down(it, s):
                pe.wait_ge(m_he, it * 3 + (s + 1))
                pe.wait_ge(m_wd[s], it * 16 + 16)
                pe.wait_ge(m_od, it * 6 + (2 * s + 2))
                wd = EDW[s].rearrange("p (k n) -> p k n", k=2)
                for hf in range(2):
                    for j in range(2):
                        t = nc.tensor.matmul(PB[:, 6 + hf, :], HhT[:, s, j * P:(j + 1) * P], wd[:, j, hf * 512:(hf + 1) * 512],
                                             start=(j == 0), stop=(j == 1))
                    t.then_inc(m_d, 1)

            def step(it, s, turn=True, gu=True):
                if turn:
                    turn_rows(it, s + 2)
                turn_hidden(it, s)
                if gu:
                    gate_up(it, s + 1)
                down(it, s)

            turn_rows(0, 0)
            turn_rows(0, 1)
            gate_up(0, 0)
            with pe.Fori(0, LOOPS) as it:
                for s in range(3):
                    step(it, s)
            for s in range(3):
                step(LOOPS, s, turn=(s < 1), gu=(s < 2))

        def moe_act(act):
            def silu(it, s):
                act.wait_ge(m_gu, it * 3 + (s + 1))
                nc.scalar.activation(Hs[:, s % 3, :], PB[:, 2 + s % 3, 0:256], ACT.Silu).then_inc(m_si, 1)

            def store(it, s):
                act.wait_ge(m_od, it * 6 + (2 * s + 4))
                act.dma_start(slot_dram[bass.ds(it * (3 * P) + s * P, P), :], Ob[s]).then_inc(m_st[s], 16)

            silu(0, 0)
            with act.Fori(0, LOOPS) as it:
                for s in range(3):
                    silu(it, s + 1)
                    store(it, s)
            for s in range(3):
                if s < 2:
                    silu(LOOPS, s + 1)
                store(LOOPS, s)

        def moe_dve(dve):
            dve.sem_inc(m_od, 2)
            for s in range(3):
                dve.sem_inc(m_st[s], 16)
                nc.vector.tensor_copy(idc[:, s:s + 1], idxi[:, s:s + 1]).then_inc(m_ix, 1)

            def rows_T(it, s, index=True):
                for hf in range(2):
                    dve.wait_ge(m_t, it * 6 + (2 * s + hf + 1))
                    nc.vector.tensor_copy(XgT[:, s % 3, 4 * hf:4 * hf + 4, :].rearrange("p k n -> p (k n)"), PB[:, hf, :]
                                          ).then_inc(m_te, 1)
                if index:
                    nc.vector.tensor_copy(idc[:, s % 3:s % 3 + 1], idxi[:, bass.ds(it * 3 + (s + 3), 1)]).then_inc(m_ix, 1)

            def hidden_T(it, s):
                dve.wait_ge(m_ht, it * 3 + (s + 1))
                nc.vector.tensor_copy(HhT[:, s, :], PB[:, 5, 0:256]).then_inc(m_he, 1)

            def hidden(it, s):
                dve.wait_ge(m_si, it * 3 + (s + 1))
                nc.vector.tensor_tensor(Hh[:, s % 3, :], PB[:, 2 + s % 3, 256:512], Hs[:, s % 3, :], ALU.mult).then_inc(m_h, 1)

            def rows_out(it, s):
                dve.wait_ge(m_st[s], it * 16 + 16)
                for hf in range(2):
                    dve.wait_ge(m_d, it * 6 + (2 * s + hf + 1))
                    nc.vector.tensor_copy(Ob[s][:, hf * 512:(hf + 1) * 512], PB[:, 6 + hf, :]).then_inc(m_od, 1)

            def step(it, s, turn=True, gu=True, index=True):
                if turn:
                    rows_T(it, s + 2, index)
                hidden_T(it, s)
                if gu:
                    hidden(it, s + 1)
                rows_out(it, s)

            rows_T(0, 0)
            rows_T(0, 1)
            hidden(0, 0)
            with dve.Fori(0, LOOPS) as it:
                for s in range(3):
                    step(it, s)
            for s in range(3):
                step(LOOPS, s, turn=(s < 1), gu=(s < 2), index=False)

        l_g = [sem("token_rows0"), sem("token_rows1")]
        l_a = sem("last_add")
        l_sq = sem("last_square")
        l_st = sem("last_std")
        l_r = sem("last_rstd")
        l_y = sem("last_y")
        s_out = sem("out_stored")
        R1 = Z[:, moe0:moe0 + 2 * D].rearrange("p (s n) -> p s n", s=2)
        R2 = Z[:, moe0 + 2 * D:moe0 + 4 * D].rearrange("p (s n) -> p s n", s=2)

        def last_pool(pool):
            for s in range(3):
                pool.wait_ge(m_st[s], 16 + 16 * (NB // 3))
            pool.wait_ge(m_gu, NB)
            for m in range(MT):
                if m >= 2:
                    pool.wait_ge(l_a, 2 * (m - 1))
                for k, r in enumerate((R1, R2)):
                    nc.gpsimd.indirect_dma_start(
                        r[:, m % 2, :], None, slot_dram[:, :],
                        bass.IndirectOffsetOnAxis(ap=si[:, k, m:m + 1], axis=0)).then_inc(l_g[m % 2], 16)

        def last_dve(dve):
            wait_gain(dve, 5)
            for m in range(MT):
                dve.wait_ge(l_g[m % 2], 32 * (m // 2 + 1))
                nc.vector.scalar_tensor_tensor(X[:, m, :], R1[:, m % 2, :], w1_[:, m, :], X[:, m, :], ALU.mult, ALU.add
                                               ).then_inc(l_a, 1)
                dve.wait_ge(l_a, 2 * m + 1)
                nc.vector.scalar_tensor_tensor(X[:, m, :], R2[:, m % 2, :], w2_[:, m, :], X[:, m, :], ALU.mult, ALU.add
                                               ).then_inc(l_a, 1)
            for m in range(MT):
                dve.wait_ge(l_st, m + 1)
                nc.vector.reciprocal(stat[:, 32 + m:33 + m], stat[:, 16 + m:17 + m]).then_inc(l_r, 1)
                dve.wait_ge(l_r, m + 1)
                nc.vector.scalar_tensor_tensor(Y[:, m, :], X[:, m, :], stat[:, 32 + m:33 + m], GP[:, 1, :],
                                               ALU.mult, ALU.mult).then_inc(l_y, 1)

        def last_act(act):
            for m in range(MT):
                act.wait_ge(l_a, 2 * (m + 1))
                nc.scalar.activation(SIL[:, 0:2, :].rearrange("p a b -> p (a b)"), X[:, m, :], ACT.Square,
                                     accum_out=stat[:, m:m + 1]).then_inc(l_sq, 1)
                act.wait_ge(l_sq, m + 1)
                nc.scalar.activation(stat[:, 16 + m:17 + m], stat[:, m:m + 1], ACT.Sqrt, bias=stat[:, 60:61],
                                     scale=1.0 / D).then_inc(l_st, 1)

        out_v = out[0].rearrange("(m p) n -> p m n", p=P)
        s_init = sem("init")
        s_initd = sem("init_dve")

        block = ctx.enter_context(nc.Block())

        @block.sync
        def _(sp):
            sp.dma_start(ident[:], a["c_ident"]).then_inc(s_const, 16)
            sp.dma_start(X[:], a["x"][0].rearrange("(m p) n -> p m n", p=P)).then_inc(s_x, 16)
            for n in range(3):
                load_chunk(sp, n)
            for n in range(3, len(chunks)):
                load_chunk(sp, n)
            moe_sync(sp)
            for m in range(MT):
                sp.wait_ge(l_y, m + 1)
                sp.dma_start(out_v[:, m, :], Y[:, m, :]).then_inc(s_out, 16)
            sp.wait_ge(s_out, 16 * MT)

        @block.gpsimd
        def _(pool):
            nc.gpsimd.memset(ones[:], 1.0).then_inc(s_init, 1)
            nc.gpsimd.memset(idle[:], 0.0)
            nc.gpsimd.memset(stat[:, 60:61], 1e-6).then_inc(s_init, 1)
            nc.gpsimd.memset(stat[:, 61:62], 1e-5).then_inc(s_init, 1)
            for i, v in enumerate((a["ln_mix_pre"][0], a["ln_mix_pre"][1], a["ln_ffn_pre"][0], a["ln_ffn_pre"][1],
                                   a["attn_norm_2"][0])):
                pool.dma_start(gains[:, i, :], v.rearrange("(k p) -> p k", p=P), allow_slow_non_contiguous=True).then_inc(s_gains, 16)
            pool.dma_start(gains[:, 5, 0:4], a["out_norm_dil_2"][0].rearrange("(k p) -> p k", p=P),
                           allow_slow_non_contiguous=True).then_inc(s_gains, 16)
            pool.dma_start(gains[:, 5, 4:8], a["out_norm_fox_2"][0].rearrange("(k p) -> p k", p=P),
                           allow_slow_non_contiguous=True).then_inc(s_gains, 16)
            pool.dma_start(upper[:], a["c_upper"]).then_inc(s_gains, 16)
            for dst, src in ((poolA, a["c_poolA"]), (poolB, a["c_poolB"]),
                             (poolW, a["ev_pool_w"][0].rearrange("g c d -> c g d")),
                             (sguW, a["ev_sgu_w"][0].rearrange("g t s -> t g s")),
                             (lng, a["ev_sgu_ln_g"].to_broadcast([P, 512])),
                             (lnb, a["ev_sgu_ln_b"].to_broadcast([P, 512])),
                             (sgub[0:1, :], a["ev_sgu_b"].rearrange("a g t -> a (g t)")),
                             (pscale, a["ev_pool_scale"][0].rearrange("(k p) -> p k", p=P)),
                             (decay, a["c_decay"])):
                pool.dma_start(dst, src, allow_slow_non_contiguous=True).then_inc(s_ev, 16)
            load_gain(pool, 0)
            load_gain(pool, 1)
            for dst, src in ((posi[:], a["positions"][0].rearrange("(m p) -> p m", p=P)),
                             (invf[:], a["c_invf"].to_broadcast([P, 72])), (cvalid[:], a["c_cvalid"]),
                             (gnr, a["od_ret_gn_g"].to_broadcast([P, 512])),
                             (cmpw2[:, 0, :], a["od_cmp_k_w2"][0]), (cmpw2[:, 1, :], a["od_cmp_v_w2"][0]),
                             (cmpos[:, 0, :], a["od_cmp_k_pos"][0].rearrange("l d -> d l")),
                             (cmpos[:, 1, :], a["od_cmp_v_pos"][0].rearrange("l d -> d l")),
                             (causal_b[:], a["c_causal"]), (cmask_b[:], a["c_cmask"]), (ident_b[:], a["c_ident"])):
                pool.dma_start(dst, src, allow_slow_non_contiguous=True).then_inc(s_od, 16)
            for dst, src in ((bfr[:], a["b_forget_2"].to_broadcast([P, NH])), (rb[:], a["rel_bias_2"])):
                pool.dma_start(dst, src, allow_slow_non_contiguous=True).then_inc(s_2, 16)
            pool.wait_ge(*d_ev.xr.at(MT))
            load_gain(pool, 2)
            ret_pool(pool)
            nsa_pool(pool)
            pool.wait_ge(*d_f0.xr.at(MT))
            load_gain(pool, 3)
            nsa.done(pool)
            for dst, src in ((ohot, a["c_onehot"]), (badd, a["c_badd"].to_broadcast([NH, TW]))):
                pool.dma_start(dst, src, allow_slow_non_contiguous=True).then_inc(s_2b, 16)
            pool.wait_ge(b_sb, 2)
            pool.dma_start(bias_dram[:, :], brow).then_inc(b_dr, 16)
            pool.wait_ge(b_dr, 16)
            for half in range(2):
                src = bass.AP(bias_dram.tensor, half * 4 * TW, [[1, P], [TW, 4], [1, T]])
                pool.dma_start(bias_raw, src).then_inc(b_ld, 16)
                pool.wait_ge(b_rev, half + 1)
            pool.wait_ge(*d_od.xr.at(MT))
            load_gain(pool, 4)
            pool.wait_ge(*d_f1.xr.at(MT))
            load_gain(pool, 5)
            two_pool(pool)
            two.done(pool)
            for dst, src in ((wrt[:, :, 0:4], a["w_router_group_2"][0].rearrange("(k p) n -> p k n", p=P)),
                             (wrt[:, :, 4:36], a["w_router_expert_2"][0].rearrange("(k p) n -> p k n", p=P)),
                             (brt[:, 0:4], a["b_router_group_2"].to_broadcast([P, 4])),
                             (brt[:, 4:36], a["b_router_expert_2"].to_broadcast([P, NE])),
                             (strict, a["c_strict"]),
                             (Z[:, o_io:o_io + P + NB + MT + EG], a["c_iotas"]),
                             (io40x, a["c_io40x"].to_broadcast([P, NB]))):
                pool.dma_start(dst, src, allow_slow_non_contiguous=True).then_inc(s_rc, 16)
            for m in range(MT):
                pool.wait_ge(*n6.xn.at(m + 1))
                pool.dma_start(h2_dram[m * P:(m + 1) * P, :], Y[:, m, :]).then_inc(s_h2, 16)
            moe_pool(pool)
            last_pool(pool)

        @block.scalar
        def _(act):
            act.wait_ge(s_init, 3)
            n1.act(act)
            p_ev.take(act, "act")
            even_act(act)
            d_ev.act(act)
            n2.act(act)
            f0.act(act)
            d_f0.act(act)
            n3.act(act)
            odd_act_tables(act)
            p_od.take(act, "act")
            ret_act(act)
            cmp_act(act)
            nsa_keys_act(act)
            nsa.act(act)
            d_od.act(act)
            n4.act(act)
            f1.act(act)
            d_f1.act(act)
            n5.act(act)
            p_2.take(act, "act")
            forget_act(act)
            two.act(act)
            n_y2.act(act)
            n6.act(act)
            router_act(act)
            moe_act(act)
            last_act(act)

        @block.vector
        def _(dve):
            dve.wait_ge(s_const, 16)
            dve.wait_ge(s_gains, 16 * 8)
            dve.wait_ge(s_x, 16)
            n1.dve(dve)
            p_ev.take(dve, "dve")
            even_dve(dve)
            d_ev.dve(dve)
            n2.dve(dve)
            f0.dve(dve)
            d_f0.dve(dve)
            n3.dve(dve)
            ch = angles_dve(dve)
            p_od.take(dve, "dve")
            rope_dve(dve, ch)
            ret_dve(dve)
            cmp_dve(dve)
            nsa.dve(dve)
            bias_dve(dve)
            n_y1.dve(dve)
            d_od.dve(dve)
            bias_turn_dve(dve, 0)
            n4.dve(dve)
            bias_turn_dve(dve, 1)
            f1.dve(dve)
            d_f1.dve(dve)
            n5.dve(dve)
            p_2.take(dve, "dve")
            forget_dve(dve)
            dve.wait_ge(b_rev, 2)
            two.dve(dve)
            n_y2.dve(dve)
            d_2.dve(dve)
            wait_gain(dve, 4)
            n6.dve(dve)
            router_dve(dve)
            moe_dve(dve)
            last_dve(dve)

        @block.tensor
        def _(pe):
            pe.wait_ge(s_init, 3)
            pe.wait_ge(s_const, 16)
            pe.wait_ge(s_gains, 16 * 8)
            n1.pe(pe)
            p_ev.pe(pe)
            even_pe(pe)
            d_ev.pe(pe, HT)
            n2.pe(pe)
            f0.pe(pe)
            Zt = Z[:, 0:FT * 512].rearrange("p (j t) -> p j t", t=512)
            d_f0.pe(pe, Zt)
            n3.pe(pe)
            p_od.pe(pe)
            ret_pe(pe)
            cmp_pe(pe)
            nsa_keys_pe(pe)
            nsa.pe(pe)
            bias_pe(pe)
            n_y1.pe(pe)
            d_od.pe(pe, HT)
            n4.pe(pe)
            f1.pe(pe)
            d_f1.pe(pe, Zt)
            n5.pe(pe)
            p_2.pe(pe)
            forget_pe(pe)
            two.pe(pe)
            n_y2.pe(pe)
            d_2.pe(pe, HT)
            n6.pe(pe)
            router_pe(pe)
            moe_pe(pe)


def shape_constants():
    f = np.float32
    p, c = np.arange(P)[:, None], np.arange(P)[None, :]
    k = {"c_ident": (p == c).astype(f), "c_upper": (p <= c).astype(f), "c_strict": (p < c).astype(f)}
    poolA, poolB = np.zeros((P, 4, 2, P), f), np.zeros((P, 4, P), f)
    for g, w in enumerate((2, 4, 8, 16)):
        for v in range(2):
            count = np.minimum(c + 1, w) if v == 0 else w
            poolA[:, g, v] = ((p <= c) & (p > c - w)) / count - (p == c)
        poolB[:, g] = ((p > c + P - w)) / f(w)
    k["c_poolA"], k["c_poolB"] = poolA, poolB
    decay = np.zeros((P, RH, T), f)
    rel = np.arange(T)[None, :] - p
    for h in range(RH):
        decay[:, h] = np.where(rel >= 0, np.exp(np.maximum(rel, 0) * np.log1p(-2.0 ** (-5.0 - h))), 0) * RD ** -0.5
    k["c_decay"] = decay
    i8, i64 = np.arange(0, 16, 2, dtype=f), np.arange(0, 128, 2, dtype=f)
    inv = np.concatenate([f(1) / (f(500000.0) ** (i8 / f(16))), f(1) / (f(10000.0) ** (i64 / f(128)))])
    k["c_invf"] = inv.astype(f)[None]
    tq = np.arange(MT)[None, :] * P + p
    k["c_cvalid"] = (tq >= CB - 1).astype(f)
    k["c_causal"] = np.where(c <= p, 0, -BIG).astype(f)
    cm = np.zeros((P, MT, NC + 1), f)
    cm[:, :, :NC] = np.where(np.arange(NC) * CS + CB - 1 <= tq[:, :, None], 0, -BIG)
    k["c_cmask"] = cm
    dist = np.arange(TW) - (P - 1)
    d = np.maximum(dist, 1).astype(f)
    large = 16 + (np.log(d / f(16)) / f(np.log(2048 / 16)) * f(16)).astype(np.int32)
    bucket = np.where(dist < 16, np.maximum(dist, 0), np.minimum(large, 31))
    ok = dist >= 0
    count = (dist <= 128) * 1 + (dist % 4 == 0) + (dist % 16 == 0)
    k["c_onehot"] = ((np.arange(32)[:, None] == bucket[None]) & ok & (count > 0)).astype(f)
    k["c_badd"] = np.where(ok & (count > 0), np.log(np.maximum(count, 1)), -BIG).astype(f)[None]
    io = np.zeros((P, P + NB + MT + EG), f)
    io[:, :P] = np.arange(P)
    io[:, P:P + NB] = np.arange(NB)
    io[:, P + NB:P + NB + MT] = tq
    io[:, P + NB + MT:] = EG - np.arange(EG)
    k["c_iotas"] = io
    k["c_io40x"] = (np.arange(NB) * P).astype(f)[None]
    return k


def kernel(**inputs):
    import concourse.bacc as bacc
    from concourse.bass_utils import run_bass_kernel_spmd

    nc = bacc.Bacc("TRN2", target_bir_lowering=False, num_devices=1)
    arrays = {n: np.ascontiguousarray(v) for n, v in inputs.items()}
    arrays.update(shape_constants())
    aps = {n: nc.dram_tensor("in_" + n, v.shape, mybir.dt.from_np(v.dtype), kind="ExternalInput").ap()
           for n, v in arrays.items()}
    out = nc.dram_tensor("out_x", (1, T, D), fp32, kind="ExternalOutput").ap()
    program(nc, aps, out)
    r = run_bass_kernel_spmd(nc, [{"in_" + n: v for n, v in arrays.items()}], core_ids=[0])
    return r.results[0]["out_x"]
```

```python
import numpy as np
from contextlib import ExitStack
import concourse.bass as bass
from concourse import mybir

fp32 = mybir.dt.float32
fp32r = mybir.dt.float32r
bf16 = mybir.dt.bfloat16
i32 = mybir.dt.int32
ALU = mybir.AluOpType
ACT = mybir.ActivationFunctionType
AX = mybir.AxisListType

P = 128
D = 1024
T = 512
MT = T // P
KT = D // P
F = 2816
FT = F // P
EV = 1536
OD = 3352
W2 = 3080
DH = 64
NH = 8
RH, RD = 4, 128
NC, CB, CS = 31, 32, 16
NE, DE = 32, 256
NG, EG = 4, 8
NO = 2 * T // P - 1
NB = NE + NO
assert NB % 3 == 0
WR = 4096
BIG = 1.0e30
QC, KC_, VC_, KS_, VS_, KW_, VW_, GT_ = 0, 512, 640, 768, 896, 1024, 1152, 1280
RQ_, RK_, RV_, RG_ = 1304, 1816, 2328, 2840
QA_, KA_, VA_, QF_, KF_, VF_, FP_ = 0, 512, 1024, 1536, 2048, 2560, 3072
TW = 640


class Chain:

    def __init__(self, eng, sem, base=0):
        self.eng, self.sem, self.n = eng, sem, base

    def add(self, ins):
        ins.then_inc(self.sem, 1)
        self.n = self.n + 1

    def wait(self):
        self.eng.wait_ge(self.sem, self.n)


def program(nc, a, out):
    h2_dram = nc.dram_tensor("h2_rows", [T, D], fp32).ap()
    slot_dram = nc.dram_tensor("expert_rows", [NB * P, D], fp32).ap()
    bias_dram = nc.dram_tensor("distance_bias", [NH, TW], fp32).ap()

    ctx = ExitStack()
    with ctx:
        def sb(name, shape, dt=fp32):
            return ctx.enter_context(nc.sbuf_tensor(name, shape, dt))

        def sem(name):
            return ctx.enter_context(nc.semaphore(name))

        OPS_AT = -(-nc.sbuf_base // 32) * 32
        RING_AT = OPS_AT + 4 * 2 * KT * T
        sb("arena", [P, 2 * KT * T + 3 * WR])
        OPS = nc.alloc_sbuf_tensor_at("OPS", [P, 2 * KT, T], fp32, offset=OPS_AT)
        OPS_R = nc.alloc_sbuf_tensor_at("OPS_R", [P, 2 * KT, T], fp32r, offset=OPS_AT)
        RING = nc.alloc_sbuf_tensor_at("RING", [P, 3 * WR], fp32, offset=RING_AT)
        RING_R = nc.alloc_sbuf_tensor_at("RING_R", [P, 3 * WR], fp32r, offset=RING_AT)
        HT = OPS[:, 0:KT]
        HTH, HTL = OPS_R[:, 0:KT], OPS_R[:, KT:2 * KT]
        BIAS = OPS[:, KT:KT + NH]

        X = sb("X", [P, MT, D])
        Y = sb("Y", [P, MT, D])
        Z = sb("Z", [P, MT * OD])
        ST = sb("ST", [P, 2112])
        WK = sb("WK", [P, 3072])
        PR = WK[:, 0:1024].rearrange("p (s n) -> p s n", s=2)
        SBI = WK[:, 1024:2048].rearrange("p (s n) -> p s n", s=2)
        PTS = WK[:, 2048:3072].rearrange("p (s k n) -> p s k n", s=2, k=4)
        SIL = WK[:, 0:1536].rearrange("p (s n) -> p s n", s=3)
        RAW = WK[:, 2048:3072].rearrange("p (s n) -> p s n", s=2)
        GP = sb("GP", [P, 2, D])
        ident = sb("ident", [P, P])
        ones = sb("ones", [P, P])
        ident_b = sb("ident_b", [P, P], bf16)
        upper = sb("upper", [P, P])
        causal_b = sb("causal_b", [P, P], bf16)
        cmask_b = sb("cmask_b", [P, MT, NC + 1], bf16)
        gains = sb("gains", [P, 7, KT])
        stat = sb("stat", [P, 64])
        PB = ctx.enter_context(nc.psum_tensor("PB", [P, 8, 512], fp32))

        s_const = sem("const_loaded")
        idle = sb("idle", [P, 2])
        s_gain_n1 = sem("first_gain_loaded")
        s_gains = sem("gains_loaded")
        s_x = sem("x_loaded")
        ring_full = [sem(f"ring_full{i}") for i in range(3)]

        s_whi = sem("weights_high")
        s_wlo = sem("weights_low")
        chunks = []
        HW = WR // 2
        split_done = {"act": 0, "dve": 0}

        def ring_slot(n):
            return RING[:, (n % 3) * WR:(n % 3 + 1) * WR]

        def arrived(eng, n):
            eng.wait_ge(ring_full[n % 3], chunks[n]["value"])

        def add_chunk(*loads, words=0):
            n = len(chunks)
            assert len(loads) == 2
            splits = (chunks[-1]["splits"] if n else 0) + (1 if words else 0)
            chunks.append({"loads": loads, "value": 32 * (n // 3 + 1), "done": None, "words": words, "splits": splits})
            return n

        def split_chunk(eng, name, n, it=0):
            c, o = chunks[n], (n % 3) * WR
            raw, high = slice(o, o + c["words"]), slice(o + HW, o + HW + c["words"])
            if name == "act":
                eng.wait_ge(ring_full[n % 3], it * 32 + c["value"])
                nc.scalar.activation(RING_R[:, high], RING[:, raw], ACT.Copy).then_inc(s_whi, 1)
            else:
                eng.wait_ge(s_whi, it * 3 + c["splits"])
                nc.vector.tensor_tensor(RING_R[:, raw], RING[:, raw], RING_R[:, high].bitcast(fp32), ALU.subtract).then_inc(s_wlo, 1)

        def split_to(eng, name, n):
            for c in range(split_done[name], min(n, len(chunks))):
                if chunks[c]["words"]:
                    split_chunk(eng, name, c)
            split_done[name] = max(n, split_done[name])

        def wait_split(eng, n, it=0):
            eng.wait_ge(s_wlo, it * 3 + chunks[n]["splits"])

        def parts(n):
            o, w = (n % 3) * WR, chunks[n]["words"]
            return RING_R[:, o + HW:o + HW + w], RING_R[:, o:o + w]

        def product(o, x, w, start, stop):
            nc.tensor.matmul(o, x[0], w[0], start=start, stop=False)
            nc.tensor.matmul(o, x[0], w[1], start=False, stop=False)
            return nc.tensor.matmul(o, x[1], w[0], start=False, stop=stop)

        def load_chunk(eng, n):
            if n >= 3:
                s, v = chunks[n - 3]["done"]
                eng.wait_ge(s, v)
            for dst, src in chunks[n]["loads"]:
                eng.dma_start(dst, src).then_inc(ring_full[n % 3], 16)

        shared = {}

        class Sig:

            def __init__(self, name, total):
                if name not in shared:
                    shared[name] = [sem(name), 0]
                self.sem, self.base = shared[name]
                shared[name][1] += total

            def at(self, v):
                return self.sem, v + self.base

        class Norm:
            def __init__(self, name, src, ready, parts, gain=None, rows=None, normed=True, split=True):
                self.name, self.src, self.ready, self.parts = name, src, ready, parts
                self.gain, self.rows, self.normed, self.split = gain, rows, normed, split
                self.inverted = set()
                self.raw = Sig("norm_raw", 2 * MT if split else 0)
                self.hi = Sig("norm_high", 2 * MT if split else 0)
                n = MT * len(parts) if normed else 0
                self.stats = Sig("norm_stats", n)
                self.rec = Sig("norm_rstd", n)
                self.xn = Sig("norm_scaled", n)
                self.tr = Sig("norm_transposed", 2 * MT)
                self.ht = Sig("norm_ht", 2 * MT)
                self.sq = Sig("norm_square", n)

            def act(self, act):
                np_ = len(self.parts)

                def stats(m):
                    act.wait_ge(self.ready[0], self.ready[1](m))
                    for i, (c0, c1) in enumerate(self.parts):
                        nc.scalar.activation(SIL[:, 0:2, :].rearrange("p a b -> p (a b)")[:, 0:c1 - c0],
                                             self.src[:, m, c0:c1], ACT.Square,
                                             accum_out=stat[:, 8 * i + m:8 * i + m + 1]).then_inc(self.sq.sem, 1)
                        act.wait_ge(*self.sq.at(m * np_ + i + 1))
                        nc.scalar.activation(stat[:, 16 + 8 * i + m:17 + 8 * i + m], stat[:, 8 * i + m:8 * i + m + 1],
                                             ACT.Sqrt, bias=stat[:, 60:61], scale=1.0 / (c1 - c0)).then_inc(self.stats.sem, 1)

                def scale(m):
                    for i, (c0, c1) in enumerate(self.parts):
                        act.wait_ge(*self.rec.at(m * np_ + i + 1))
                        nc.scalar.activation(Y[:, m, c0:c1], self.src[:, m, c0:c1], ACT.Copy,
                                             scale=stat[:, 32 + 8 * i + m:33 + 8 * i + m]).then_inc(self.xn.sem, 1)

                def high(m):
                    for u in (2 * m, 2 * m + 1):
                        act.wait_ge(*self.raw.at(u + 1))
                        nc.scalar.activation(self.place(HTH, u), RAW[:, u % 2, :].rearrange("p (a b) -> p a b", a=4),
                                             ACT.Copy).then_inc(self.hi.sem, 1)

                for m in range(MT + 2):
                    if self.normed and m < MT:
                        stats(m)
                    if self.normed and self.rows is None and 1 <= m <= MT:
                        scale(m - 1)
                    if self.split and m >= 2:
                        high(m - 2)

            def place(self, t, u):
                m, hf = u // 2, u % 2
                return t[:, 4 * hf:4 * hf + 4, m * P:(m + 1) * P]

            def dve(self, dve):
                np_ = len(self.parts)
                for m in range(MT):
                    if self.normed:
                        self.reciprocals(dve, m)
                        for i, (c0, c1) in enumerate(self.parts):
                            if self.rows is not None:
                                dve.wait_ge(*self.rec.at(m * np_ + i + 1))
                                r = stat[:, 32 + 8 * i + m:33 + 8 * i + m]
                                nc.vector.scalar_tensor_tensor(Y[:, m, c0:c1], self.src[:, m, c0:c1], r, self.rows,
                                                               ALU.mult, ALU.mult).then_inc(self.xn.sem, 1)
                    if m >= 1:
                        self.evac(dve, m - 1)
                self.evac(dve, MT - 1)

            def reciprocals(self, dve, m):
                if m in self.inverted:
                    return
                self.inverted.add(m)
                np_ = len(self.parts)
                for i in range(np_):
                    dve.wait_ge(*self.stats.at(m * np_ + i + 1))
                    nc.vector.reciprocal(stat[:, 32 + 8 * i + m:33 + 8 * i + m],
                                         stat[:, 16 + 8 * i + m:17 + 8 * i + m]).then_inc(self.rec.sem, 1)

            def evac(self, dve, m):
                for hf in range(2):
                    u = 2 * m + hf
                    dve.wait_ge(*self.tr.at(u + 1))
                    dst = RAW[:, hf, :].rearrange("p (a b) -> p a b", a=4) if self.split else self.place(HT, u)
                    done = (self.raw if self.split else self.ht).sem
                    if self.split and m:
                        dve.wait_ge(*self.ht.at(u - 1))
                    src = PB[:, u % 4, :].rearrange("p (a b) -> p a b", a=4)
                    if self.gain is None:
                        nc.vector.tensor_copy(dst, src).then_inc(done, 1)
                    else:
                        g = gains[:, self.gain, 4 * hf:4 * hf + 4].unsqueeze(2).to_broadcast([P, 4, P])
                        nc.vector.tensor_tensor(dst, src, g, ALU.mult).then_inc(done, 1)
                for u in range(2 * m, 2 * m + 2 if self.split else 0):
                    dve.wait_ge(*self.hi.at(u + 1))
                    nc.vector.tensor_tensor(self.place(HTL, u), RAW[:, u % 2, :].rearrange("p (a b) -> p a b", a=4),
                                            self.place(HTH, u).bitcast(fp32), ALU.subtract).then_inc(self.ht.sem, 1)

            def pe(self, pe):
                for m in range(MT):
                    if self.normed:
                        pe.wait_ge(*self.xn.at((m + 1) * len(self.parts)))
                    else:
                        pe.wait_ge(self.ready[0], self.ready[1](m))
                    for hf in range(2):
                        u = 2 * m + hf
                        if u >= 4:
                            pe.wait_ge(*(self.raw if self.split else self.ht).at(u - 3))
                        for k in range(4):
                            t = nc.tensor.transpose(PB[:, u % 4, k * P:(k + 1) * P],
                                                    Y[:, m, (4 * hf + k) * P:(4 * hf + k + 1) * P], ident[:])
                        t.then_inc(self.tr.sem, 1)

            def ready_tile(self, m):
                return self.ht.at(2 * (m + 1))

        class Proj:

            def __init__(self, name, norm, w, width, dst, fn):
                self.name, self.norm, self.dst, self.fn = name, norm, dst, fn
                self.cols = [(c, min(c + 512, width)) for c in range(0, width, 512)]
                self.mm = Sig("proj_mm", (MT + 1) * len(self.cols))
                w_v = w.rearrange("(k p) n -> p k n", p=P)
                self.n0 = len(chunks)
                for j, (c0, c1) in enumerate(self.cols):
                    wd = c1 - c0
                    for hf in range(2):
                        n = len(chunks)
                        dst_ = ring_slot(n)[:, 0:4 * wd].rearrange("p (k n) -> p k n", k=4)
                        add_chunk((dst_[:, 0:2], w_v[:, 4 * hf:4 * hf + 2, c0:c1]),
                                  (dst_[:, 2:4], w_v[:, 4 * hf + 2:4 * hf + 4, c0:c1]), words=4 * wd)
                        chunks[n]["done"] = self.mm.at((MT + 1) * j + (1 if hf == 0 else MT + 1))
                self.who = []
                cnt = {"act": 0, "dve": 0}
                for u in range(MT * len(self.cols)):
                    e = fn(u)[0]
                    cnt[e] += 1
                    self.who.append((e, cnt[e]))
                self.total = cnt
                self.out = {e: Sig("proj_out_" + e, cnt[e]) for e in cnt}

            def pe(self, pe):
                for j, (c0, c1) in enumerate(self.cols):
                    wd = c1 - c0
                    for hf in range(2):
                        n = self.n0 + 2 * j + hf
                        wait_split(pe, n)
                        wh, wl = [x.rearrange("p (k n) -> p k n", k=4) for x in parts(n)]
                        for m in range(MT):
                            u = MT * j + m
                            if j == 0:
                                pe.wait_ge(*self.norm.ready_tile(m))
                            if u >= 8 and hf == 0:
                                e, v = self.who[u - 8]
                                pe.wait_ge(*self.out[e].at(v))
                            for k in range(4):
                                c = slice(m * P, (m + 1) * P)
                                t = product(PB[:, (4 + u) % 8, 0:wd], (HTH[:, 4 * hf + k, c], HTL[:, 4 * hf + k, c]),
                                            (wh[:, k], wl[:, k]), start=(hf + k == 0), stop=(hf == 1 and k == 3))
                            if hf == 1 or m == MT - 1:
                                t.then_inc(self.mm.sem, 1)

            def wait_cols(self, eng, n):
                for e in ("act", "dve"):
                    eng.wait_ge(*self.out[e].at(sum(w[0] == e for w in self.who[:MT * n])))

            def take(self, eng, name, after=None):
                for j, (c0, c1) in enumerate(self.cols):
                    split_to(eng, name, self.n0 + 2 * j + 4)
                    for m in range(MT):
                        u = MT * j + m
                        e, func = self.fn(u)
                        if e != name:
                            continue
                        eng.wait_ge(*self.mm.at((MT + 1) * j + m + 2))
                        if name == "act":
                            nc.scalar.activation(self.dst[:, m, c0:c1], PB[:, (4 + u) % 8, 0:c1 - c0], func
                                                 ).then_inc(self.out["act"].sem, 1)
                        else:
                            nc.vector.tensor_copy(self.dst[:, m, c0:c1], PB[:, (4 + u) % 8, 0:c1 - c0]
                                                  ).then_inc(self.out["dve"].sem, 1)
                    if after and j in after:
                        after[j]()

            def wait_all(self, eng):
                for e in ("act", "dve"):
                    if self.total[e]:
                        eng.wait_ge(*self.out[e].at(self.total[e]))

        class Down:

            def __init__(self, name, nk, w, gain_row, ready_k=None, ffn=None):
                self.name, self.nk, self.gain_row, self.ready_k, self.ffn = name, nk, gain_row, ready_k, ffn
                self.NJ = nk // 2
                self.xhi = Sig("hidden_high", self.NJ if ffn else 0)
                self.xlo = Sig("hidden_low", self.NJ if ffn else 0)
                n = 0 if gain_row is None else MT
                self.free = Sig("down_chunk", self.NJ - 1)
                self.mm = Sig("down_mm", MT)
                self.sq = Sig("down_square", n)
                self.st = Sig("down_stats", n)
                self.rec = Sig("down_rstd", n)
                self.dc = Sig("down_scaled", n)
                self.xr = Sig("down_x", MT)
                w_v = w.rearrange("(k p) n -> p k n", p=P)
                self.n0 = len(chunks)
                for j in range(self.NJ):
                    n = len(chunks)
                    dst_ = ring_slot(n)[:, 0:2 * D].rearrange("p (k n) -> p k n", n=D)
                    add_chunk(*((dst_[:, k], w_v[:, 2 * j + k, :]) for k in range(2)), words=2 * D)
                    chunks[n]["done"] = self.free.at(j + 1) if j < self.NJ - 1 else self.mm.at(MT)

            def pe(self, pe):
                for j in range(self.NJ):
                    wait_split(pe, self.n0 + j)
                    wh, wl = [x.rearrange("p (k n) -> p k n", n=D) for x in parts(self.n0 + j)]
                    if self.ffn:
                        pe.wait_ge(*self.xlo.at(j + 1))
                    if not self.ffn:
                        for k in (2 * j, 2 * j + 1):
                            self.ready_k(pe, k)
                    last = j == self.NJ - 1
                    for kk, m in ([(kk, m) for m in range(MT) for kk in range(2)] if last else
                                  [(kk, m) for kk in range(2) for m in range(MT)]):
                        k = 2 * j + kk
                        for hf in range(2):
                            c, w = slice(m * P, (m + 1) * P), slice(hf * 512, (hf + 1) * 512)
                            t = product(PB[:, 2 * m + hf, :], (HTH[:, k % KT, c], HTL[:, k % KT, c]),
                                        (wh[:, kk, w], wl[:, kk, w]), start=(k == 0), stop=(k == self.nk - 1))
                        if last and kk == 1:
                            t.then_inc(self.mm.sem, 1)
                    if not last:
                        t.then_inc(self.free.sem, 1)

            def split_hidden(self, eng, name, j):
                f, o = self.ffn, 2 * (j % 4)
                z = Z[:, 2 * j * 512:(2 * j + 2) * 512].rearrange("p (a t) -> p a t", a=2)
                if name == "act":
                    eng.wait_ge(*f.hid.at(3 + 2 * j + 2))
                    eng.wait_ge(*(f.um.at(FT) if j < 4 else self.free.at(j - 3)))
                    nc.scalar.activation(HTH[:, o:o + 2, :], z, ACT.Copy).then_inc(self.xhi.sem, 1)
                else:
                    eng.wait_ge(*self.xhi.at(j + 1))
                    nc.vector.tensor_tensor(HTL[:, o:o + 2, :], z, HTH[:, o:o + 2, :].bitcast(fp32), ALU.subtract).then_inc(self.xlo.sem, 1)

            def splits(self, eng, name):
                if self.ffn:
                    self.split_hidden(eng, name, 0)
                for j in range(self.NJ):
                    if self.ffn and j + 1 < self.NJ:
                        self.split_hidden(eng, name, j + 1)
                    split_to(eng, name, self.n0 + j + 3)

            def act(self, act):
                self.splits(act, "act")
                if self.gain_row is None:
                    return
                for m in range(MT):
                    act.wait_ge(*self.mm.at(m + 1))
                    nc.scalar.activation(SIL[:, 0:2, :], PB[:, 2 * m:2 * m + 2, :], ACT.Square,
                                         accum_out=stat[:, m:m + 1]).then_inc(self.sq.sem, 1)
                    act.wait_ge(*self.sq.at(m + 1))
                    nc.scalar.activation(stat[:, 16 + m:17 + m], stat[:, m:m + 1], ACT.Sqrt,
                                         bias=stat[:, 60:61], scale=1.0 / D).then_inc(self.st.sem, 1)

            def dve(self, dve, norm):
                self.splits(dve, "dve")
                if self.gain_row is None:
                    for m in range(MT):
                        dve.wait_ge(*self.mm.at(m + 1))
                        nc.vector.tensor_tensor(X[:, m, :], PB[:, 2 * m:2 * m + 2, :].rearrange("p a b -> p (a b)"),
                                                X[:, m, :], ALU.add).then_inc(self.xr.sem, 1)
                    return
                wait_gain(dve, self.gain_row)
                for m in range(MT):
                    dve.wait_ge(*self.st.at(m + 1))
                    nc.vector.reciprocal(stat[:, 52 + m:53 + m], stat[:, 16 + m:17 + m]).then_inc(self.rec.sem, 1)
                    dve.wait_ge(*self.rec.at(m + 1))
                    nc.vector.scalar_tensor_tensor(Y[:, m, :], PB[:, 2 * m:2 * m + 2, :].rearrange("p a b -> p (a b)"),
                                                   stat[:, 52 + m:53 + m], GP[:, self.gain_row % 2, :],
                                                   ALU.mult, ALU.mult).then_inc(self.dc.sem, 1)
                    dve.wait_ge(*self.dc.at(m + 1))
                    nc.vector.tensor_tensor(X[:, m, :], Y[:, m, :], X[:, m, :], ALU.add).then_inc(self.xr.sem, 1)
                    if m >= 1:
                        norm.reciprocals(dve, m - 1)

            def ready(self):
                return self.xr.sem, lambda m: self.xr.base + m + 1

        class GateUp:

            def __init__(self, name, norm, wg, wu):
                self.norm = norm
                self.gm = Sig("ffn_gate_mm", FT)
                self.um = Sig("ffn_up_mm", FT)
                self.sl = Sig("ffn_silu", FT)
                self.hid = Sig("ffn_hidden", FT + 3)
                self.n0 = len(chunks)
                g_v = wg.rearrange("(k p) n -> p k n", p=P)
                u_v = wu.rearrange("(k p) n -> p k n", p=P)
                for c in range(FT):
                    n = len(chunks)
                    s = ring_slot(n)[:, 0:HW].rearrange("p (t k n) -> p t k n", t=2, k=KT)
                    add_chunk((s[:, 0], g_v[:, :, c * P:(c + 1) * P]), (s[:, 1], u_v[:, :, c * P:(c + 1) * P]), words=HW)
                    chunks[n]["done"] = self.um.at(c + 1)

            def all_tiles(self, eng, tile):
                with eng.Fori(0, FT // 3) as it:
                    for k in range(3):
                        tile(it, k)
                for k in range(FT - FT // 3 * 3):
                    tile(FT // 3, k)

            def pe(self, pe):
                pe.wait_ge(*self.norm.ready_tile(MT - 1))

                def tile(it, k):
                    n = self.n0 + k
                    wait_split(pe, n, it)
                    pe.wait_ge(*self.hid.at(it * 3 + (k + 1)))
                    wh, wl = [x.rearrange("p (t k n) -> p t k n", t=2, k=KT) for x in parts(n)]
                    for t in range(2):
                        for kk in range(KT):
                            x = product(PB[:, 2 * k + t, :], (wh[:, t, kk], wl[:, t, kk]), (HTH[:, kk, :], HTL[:, kk, :]),
                                        start=(kk == 0), stop=(kk == KT - 1))
                        x.then_inc((self.gm if t == 0 else self.um).sem, 1)

                self.all_tiles(pe, tile)

            def act(self, act):
                split_to(act, "act", self.n0 + 2)

                def tile(it, k):
                    act.wait_ge(*self.gm.at(it * 3 + (k + 1)))
                    act.wait_ge(*self.hid.at(it * 3 + (k + 1)))
                    nc.scalar.activation(SIL[:, k, :], PB[:, 2 * k, :], ACT.Silu).then_inc(self.sl.sem, 1)
                    split_chunk(act, "act", self.n0 + k + 2, it)

                self.all_tiles(act, tile)
                split_done["act"] = self.n0 + FT + 2

            def dve(self, dve):
                split_to(dve, "dve", self.n0 + 2)
                dve.sem_inc(self.hid.sem, 3)
                Zt = Z[:, 0:FT * 512].rearrange("p (j t) -> p j t", t=512)

                def tile(it, k):
                    split_chunk(dve, "dve", self.n0 + k + 2, it)
                    dve.wait_ge(*self.sl.at(it * 3 + (k + 1)))
                    dve.wait_ge(*self.um.at(it * 3 + (k + 1)))
                    nc.vector.tensor_tensor(Zt[:, bass.ds(it * 3 + k, 1), :].rearrange("p a t -> p (a t)"),
                                            PB[:, 2 * k + 1, :], SIL[:, k, :], ALU.mult).then_inc(self.hid.sem, 1)

                self.all_tiles(dve, tile)
                split_done["dve"] = self.n0 + FT + 2

        gain_rows = [a["ln_mix_post"][0], a["ln_ffn_post"][0], a["ln_mix_post"][1], a["ln_ffn_post"][1],
                     a["ffn_norm_2"][0], a["final_norm_2"]]
        s_gain = [sem("gain_row0"), sem("gain_row1")]

        def wait_gain(eng, r):
            eng.wait_ge(s_gain[r % 2], 16 * (r // 2 + 1))

        def load_gain(eng, r):
            src = gain_rows[r].rearrange("(a n) -> a n", a=1).to_broadcast([P, D])
            eng.dma_start(GP[:, r % 2, :], src).then_inc(s_gain[r % 2], 16)

        n1 = Norm("n1", X, (s_x, lambda m: 16), [(0, D)], gain=0)
        Ze = Z[:, 0:MT * EV].rearrange("p (m n) -> p m n", m=MT)
        ev_fn = lambda u: ("dve", None) if u < 4 else ("act", ACT.Gelu_apprx_tanh)
        p_ev = Proj("ev_in", n1, a["ev_w_in"][0], EV, Ze, ev_fn)
        zo = [MT * EV]

        def zpart(words, shape_str=None, **kw):
            v = Z[:, zo[0]:zo[0] + words]
            zo[0] += words
            return v.rearrange(shape_str, **kw) if shape_str else v

        poolA = zpart(4 * 2 * P, "p (g v t) -> p g v t", g=4, v=2)
        poolB = zpart(4 * P, "p (g t) -> p g t", g=4)
        poolW = zpart(4 * P, "p (g d) -> p g d", g=4)
        sguW = zpart(4 * P, "p (g d) -> p g d", g=4)
        sguWT = zpart(4 * P, "p (g d) -> p g d", g=4)
        lng = zpart(512)
        lnb = zpart(512)
        sgub = zpart(512)
        diffT = zpart(2 * 512, "p (s t) -> p s t", s=2)
        uT = zpart(2 * 512, "p (s t) -> p s t", s=2)
        pscale = zpart(4)
        bnst = zpart(4 * 6, "p (m s) -> p m s", m=4)
        bnag = zpart(4 * 2, "p (m s) -> p m s", m=4)
        s_ev = sem("even_consts")

        e_wt = sem("ev_sgu_wT_mm")
        e_wm = sem("ev_sgu_wT")
        e_bn = sem("ev_ln_stats")
        e_sd = sem("ev_ln_std")
        e_v = sem("ev_v")
        e_df = sem("ev_diff_mm")
        e_ds = sem("ev_diff")
        e_pm = sem("ev_pool_mm")
        e_um = sem("ev_uT_mm")
        e_us = sem("ev_uT")
        e_mx = sem("ev_mixed_mm")
        e_ya = sem("ev_pool_out")
        e_yb = sem("ev_sgu_out")
        e_hi = sem("ev_high")
        e_lo = sem("ev_low")
        mixed = Y[:].rearrange("p m n -> p (m n)").rearrange("p (k t) -> p k t", k=KT)

        def even_pe(pe):
            pe.wait_ge(s_ev, 16 * 8)
            p_ev.wait_all(pe)
            for g in range(4):
                t = nc.tensor.transpose(PB[:, 0, g * P:(g + 1) * P], sguW[:, g, :], ident[:])
            t.then_inc(e_wt, 1)
            for g in range(4):
                if g >= 2:
                    pe.wait_ge(e_ds, g - 1)
                b = PB[:, 1 + g % 2, :]
                for i in range(MT):
                    t = nc.tensor.matmul(b[:, i * P:(i + 1) * P], Ze[:, i, g * P:(g + 1) * P],
                                         poolA[:, g, 0 if i == 0 else 1, :], start=True, stop=(i == 0))
                    if i:
                        t = nc.tensor.matmul(b[:, i * P:(i + 1) * P], Ze[:, i - 1, g * P:(g + 1) * P],
                                             poolB[:, g, :], start=False, stop=True)
                t.then_inc(e_df, 1)
                if g >= 1:
                    pe.wait_ge(e_ds, g)
                    if g >= 3:
                        pe.wait_ge(e_ya, g - 2)
                    nc.tensor.matmul(PB[:, 3 + (g - 1) % 2, :], poolW[:, g - 1, :], diffT[:, (g - 1) % 2, :],
                                     start=True, stop=True).then_inc(e_pm, 1)
            pe.wait_ge(e_ds, 4)
            pe.wait_ge(e_ya, 2)
            nc.tensor.matmul(PB[:, 4, :], poolW[:, 3, :], diffT[:, 1, :], start=True, stop=True).then_inc(e_pm, 1)
            pe.wait_ge(e_wm, 1)
            pe.wait_ge(e_v, MT)
            for g in range(4):
                if g >= 1:
                    pe.wait_ge(e_us, g)
                for i in range(MT):
                    t = nc.tensor.transpose(PB[:, 5, i * P:(i + 1) * P], Ze[:, i, 512 + g * P:512 + (g + 1) * P], ident[:])
                t.then_inc(e_um, 1)
                if g >= 2:
                    pe.wait_ge(e_yb, g - 1)
                for i in range(MT):
                    b = PB[:, 6 + g % 2, i * P:(i + 1) * P]
                    nc.tensor.matmul(b, Ze[:, i, 1024 + g * P:1024 + (g + 1) * P], sguWT[:, g, :], start=True, stop=False)
                    t = nc.tensor.matmul(b, ones[0:1, :], sgub[0:1, g * P:(g + 1) * P], start=False, stop=True)
                t.then_inc(e_mx, 1)

        def even_act(act):
            act.wait_ge(e_bn, 2 * MT)
            nc.scalar.activation(stat[:, 40:44], bnag[:, :, 1], ACT.Sqrt, bias=stat[:, 61:62], scale=1.0).then_inc(e_sd, 1)
            for g in range(4):
                act.wait_ge(e_df, g + 1)
                if g >= 2:
                    act.wait_ge(e_pm, g - 1)
                nc.scalar.activation(diffT[:, g % 2, :], PB[:, 1 + g % 2, :], ACT.Copy).then_inc(e_ds, 1)
                if g >= 1:
                    act.wait_ge(e_pm, g)
                    nc.scalar.activation(mixed[:, g - 1, :], PB[:, 3 + (g - 1) % 2, :], ACT.Copy,
                                         scale=pscale[:, g - 1:g]).then_inc(e_ya, 1)
            act.wait_ge(e_pm, 4)
            nc.scalar.activation(mixed[:, 3, :], PB[:, 4, :], ACT.Copy, scale=pscale[:, 3:4]).then_inc(e_ya, 1)
            for g in range(4):
                act.wait_ge(e_ya, g + 1)
                nc.scalar.activation(HTH[:, g, :], mixed[:, g, :], ACT.Copy).then_inc(e_hi, 1)
            for g in range(4):
                act.wait_ge(e_um, g + 1)
                if g >= 2:
                    act.wait_ge(e_yb, g - 1)
                nc.scalar.activation(uT[:, g % 2, :], PB[:, 5, :], ACT.Copy).then_inc(e_us, 1)
                if g >= 1:
                    even_high(act, g + 3)
            even_high(act, 7)

        def even_high(act, k):
            act.wait_ge(e_yb, k - 3)
            nc.scalar.activation(HTH[:, k, :], mixed[:, k, :], ACT.Copy).then_inc(e_hi, 1)

        def even_low(dve, k):
            dve.wait_ge(e_hi, k + 1)
            nc.vector.tensor_tensor(HTL[:, k, :], mixed[:, k, :], HTH[:, k, :].bitcast(fp32), ALU.subtract).then_inc(e_lo, 1)

        def even_dve(dve):
            dve.wait_ge(s_ev, 16 * 8)
            dve.wait_ge(*p_ev.out["act"].at(p_ev.total["act"]))
            for m in range(MT):
                nc.vector.bn_stats(bnst[:, m, :], Ze[:, m, 1024:1536]).then_inc(e_bn, 1)
            dve.wait_ge(e_bn, MT)
            for m in range(MT):
                nc.vector.bn_aggr(bnag[:, m, :], bnst[:, m, :]).then_inc(e_bn, 1)
            dve.wait_ge(e_sd, 1)
            nc.vector.reciprocal(stat[:, 44:48], stat[:, 40:44]).then_inc(e_bn, 1)
            dve.wait_ge(e_wt, 1)
            nc.vector.tensor_tensor(sguWT, PB[:, 0, :].rearrange("p (g t) -> p g t", g=4),
                                    upper[:].unsqueeze(1).to_broadcast([P, 4, P]), ALU.mult).then_inc(e_wm, 1)
            dve.wait_ge(e_bn, 2 * MT + 1)
            for m in range(MT):
                v = Ze[:, m, 1024:1536]
                nc.vector.tensor_scalar(v, v, bnag[:, m, 0:1], stat[:, 44 + m:45 + m], ALU.subtract, ALU.mult).then_inc(e_bn, 1)
            for m in range(MT):
                v = Ze[:, m, 1024:1536]
                dve.wait_ge(e_bn, 2 * MT + 2 + m)
                nc.vector.tensor_tensor(v, v, lng, ALU.mult).then_inc(e_bn, 1)
            for m in range(MT):
                v = Ze[:, m, 1024:1536]
                dve.wait_ge(e_bn, 3 * MT + 2 + m)
                nc.vector.tensor_tensor(v, v, lnb, ALU.add).then_inc(e_v, 1)
            for g in range(4):
                dve.wait_ge(e_us, g + 1)
                dve.wait_ge(e_mx, g + 1)
                nc.vector.tensor_tensor(mixed[:, 4 + g, :], PB[:, 6 + g % 2, :], uT[:, g % 2, :], ALU.mult).then_inc(e_yb, 1)
                even_low(dve, g)
            for k in range(4, KT):
                even_low(dve, k)

        def even_ready(eng, k):
            eng.wait_ge(e_lo, k + 1)
            if k == 0:
                eng.wait_ge(e_yb, 4)

        d_ev = Down("ev_out", KT, a["ev_w_out"][0], 0, even_ready)
        n2 = Norm("n2", X, d_ev.ready(), [(0, D)], gain=2)
        f0 = GateUp("ffn0", n2, a["ffn_w_gate"][0], a["ffn_w_up"][0])
        d_f0 = Down("ffn0_down", FT, a["ffn_w_down"][0], 1, ffn=f0)
        n3 = Norm("n3", X, d_f0.ready(), [(0, D)], gain=1)
        Zo = Z[:, 0:MT * OD].rearrange("p (m n) -> p m n", m=MT)
        alt = lambda u: ("dve", None) if u % 2 == 0 else ("act", ACT.Copy)
        p_od = Proj("od_in", n3, a["od_w_in"][0], OD, Zo, alt)

        rope_tab = sb("rope_tab", [P, 2, MT, 72])
        posf = sb("posf", [P, MT])
        posi = sb("posi", [P, MT], i32)
        invf = sb("invf", [P, 72])
        gate_s = sb("gate_s", [P, MT, 3 * NH])
        cvalid = sb("cvalid", [P, MT])
        cmpw2 = sb("cmpw2", [P, 2, DH])
        cmpos = sb("cmpos", [DH, 2, CB])
        hidc = sb("hidc", [P, 2, 2 * NC])
        kcT = sb("kcT", [DH, 2, NC])
        vcc = sb("vcc", [NC, 2, DH])
        den = sb("den", [P, 8])
        nmx = sb("nmx", [P, 2])
        osc = sb("osc", [P, 8])

        cmp_n = []
        c_h = sem("cmp_hidden_mm")
        for i, w in enumerate(("od_cmp_k_w1", "od_cmp_v_w1")):
            n = len(chunks)
            dst_ = RING[0:DH, (n % 3) * WR:(n % 3 + 1) * WR].rearrange("p (l n) -> p l n", l=CB)
            w_v = a[w][0].rearrange("(l p) n -> p l n", p=DH)
            cmp_n.append(add_chunk(*((dst_[:, l:l + CB // 2], w_v[:, l:l + CB // 2]) for l in (0, CB // 2))))
            chunks[n]["done"] = (c_h, i + 1)

        s_od = sem("odd_consts")
        r_ch = sem("rope_chain")
        r_sn = sem("rope_sines")
        r_pool = sem("ret_staged")
        o_gate = sem("nsa_gates")
        t_mm = sem("ret_T_mm")
        t_ev = sem("ret_T")
        t_s = sem("ret_scores_mm")
        t_d = sem("ret_decayed")
        t_o = sem("ret_out_mm")
        t_c = sem("ret_norm")
        t_sd = sem("ret_std")
        t_g = sem("ret_silu")
        t_y = sem("ret_y")

        decay = BIAS[:, 0:RH, :]
        gnr = BIAS[:, RH, :]
        R_q, R_k, R_v = [ST[:, i * 512:(i + 1) * 512].rearrange("p (m d) -> p m d", m=MT) for i in range(3)]
        RqT, RkT = HT[:, 0, :], HT[:, 1, :]
        Rs = [HT[:, 2 + j, 0:T - j * P] for j in range(MT)]
        Rc = PR[:, 0, :].rearrange("p (m d) -> p m d", m=MT)
        Rsq = PR[:, 1, :].rearrange("p (m d) -> p m d", m=MT)

        def angles_dve(dve):
            dve.wait_ge(s_od, 16 * 10)
            ch = Chain(dve, r_ch)
            ang, kk, t1 = [SIL[:, i, 0:MT * 72] for i in range(3)]
            v = lambda x: x.rearrange("p (m n) -> p m n", m=MT)
            ch.add(nc.vector.tensor_copy(posf[:], posi[:]))
            ch.wait()
            ch.add(nc.vector.tensor_tensor(v(ang), posf[:].unsqueeze(2).to_broadcast([P, MT, 72]),
                                           invf[:].unsqueeze(1).to_broadcast([P, MT, 72]), ALU.mult))
            ch.wait()
            magic = float(1.5 * 2 ** 23)
            ch.add(nc.vector.tensor_scalar(kk, ang, float(1 / (2 * np.pi)), magic, ALU.mult, ALU.add))
            ch.wait()
            ch.add(nc.vector.tensor_scalar(kk, kk, magic, None, ALU.subtract))
            c1 = 6.28125
            c2 = float(np.float32(np.round((2 * np.pi - c1) * 2 ** 20) / 2 ** 20))
            c3 = float(2 * np.pi - c1 - c2)
            for c in (c1, c2, c3):
                ch.wait()
                ch.add(nc.vector.scalar_tensor_tensor(ang, kk, -c, ang, ALU.mult, ALU.add))
            ch.wait()
            pi = float(np.float32(3.1415925))
            ch.add(nc.vector.tensor_scalar(rope_tab[:, 1].rearrange("p m n -> p (m n)"), ang, pi, -pi, ALU.min, ALU.max))
            ch.add(nc.vector.tensor_scalar(t1, ang, -1.0, None, ALU.mult))
            ch.wait()
            ch.add(nc.vector.tensor_tensor(t1, t1, ang, ALU.max))
            ch.wait()
            ch.add(nc.vector.tensor_scalar(rope_tab[:, 0].rearrange("p m n -> p (m n)"), t1, -1.0, float(np.pi / 2),
                                           ALU.mult, ALU.add))
            return ch

        ANGLE_STEPS = 11

        Q_ROPES = ((0, 10, 64, 8, 0), (KS_, 2, 64, 8, 0), (KW_, 2, 64, 8, 0))
        RET_Q, RET_K = (RQ_, 4, 128, 64, 8), (RK_, 4, 128, 64, 8)

        def rope_dve(dve, ch, ropes):
            dve.wait_ge(r_sn, 1)
            p_od.wait_cols(dve, -(-max(b + h * w for b, h, w, _, _ in ropes) // 512))
            yf = Y[:].rearrange("p m n -> p (m n)")
            tmp = [yf[:, i * D:(i + 1) * D] for i in range(4)]
            for base, heads, stride, n, f0_ in ropes:
                z = Zo[:, :, base:base + heads * stride].rearrange("p m (h d) -> p m h d", h=heads)
                x1, x2 = z[:, :, :, 0:n], z[:, :, :, n:2 * n]
                cs = rope_tab[:, 0, :, f0_:f0_ + n].unsqueeze(2).to_broadcast([P, MT, heads, n])
                sn = rope_tab[:, 1, :, f0_:f0_ + n].unsqueeze(2).to_broadcast([P, MT, heads, n])
                q = [x[:, 0:MT * heads * n].rearrange("p (m h d) -> p m h d", m=MT, h=heads) for x in tmp]
                ch.wait()
                ch.add(nc.vector.tensor_tensor(q[0], x1, cs, ALU.mult))
                ch.add(nc.vector.tensor_tensor(q[1], x2, sn, ALU.mult))
                ch.add(nc.vector.tensor_tensor(q[2], x2, cs, ALU.mult))
                ch.add(nc.vector.tensor_tensor(q[3], x1, sn, ALU.mult))
                ch.wait()
                ch.add(nc.vector.tensor_tensor(x1, q[0], q[1], ALU.subtract))
                ch.add(nc.vector.tensor_tensor(x2, q[2], q[3], ALU.add))

        ROPE_STEPS = ANGLE_STEPS + 30

        def odd_act_tables(act):
            act.wait_ge(r_ch, ANGLE_STEPS)
            nc.scalar.activation(rope_tab[:], rope_tab[:], ACT.Sin).then_inc(r_sn, 1)

        def ret_pool(pool):
            pool.wait_ge(r_ch, ROPE_STEPS)
            p_od.wait_all(pool)
            with pool.Fori(0, RH) as h:
                for src, dst in ((RQ_, R_q), (RK_, R_k)):
                    nc.gpsimd.tensor_copy(dst, Zo[:, :, bass.ds(h * RD + src, RD)]).then_inc(r_pool, 1)
                pool.wait_ge(t_o, h + 1)
                nc.gpsimd.tensor_copy(R_v, Zo[:, :, bass.ds(h * RD + RV_, RD)]).then_inc(r_pool, 1)
                pool.wait_ge(t_mm, h * 2 + 2)

        def ret_pe(pe):
            pe.sem_inc(t_o, 1)
            with pe.Fori(0, RH) as h:
                pe.wait_ge(r_pool, h * 3 + 2)
                for i, s in enumerate((R_q, R_k)):
                    for m in range(MT):
                        t = nc.tensor.transpose(PB[:, i, m * P:(m + 1) * P], s[:, m, :], ident[:])
                    t.then_inc(t_mm, 1)
                pe.wait_ge(r_pool, h * 3 + 3)
                pe.wait_ge(t_ev, h * 2 + 2)
                for j in range(MT):
                    nc.tensor.matmul(PB[:, 2 + j, 0:T - j * P], RkT[:, j * P:(j + 1) * P], RqT[:, j * P:T],
                                     start=True, stop=True).then_inc(t_s, 1)
                for i in range(MT):
                    pe.wait_ge(t_d, h * MT + i + 1)
                    if i == 0:
                        pe.wait_ge(t_c, h * 5 + 1)
                    for j in range(i + 1):
                        t = nc.tensor.matmul(PB[:, 6, i * P:(i + 1) * P], Rs[j][:, (i - j) * P:(i - j + 1) * P],
                                             R_v[:, j, :], start=(j == 0), stop=(j == i))
                t.then_inc(t_o, 1)

        def ret_act(act):
            p_od.wait_all(act)
            nc.scalar.activation(gate_s[:], Zo[:, :, GT_:GT_ + 24], ACT.Sigmoid).then_inc(o_gate, 1)
            act.wait_ge(r_ch, ROPE_STEPS)
            with act.Fori(0, RH) as h:
                for i, dst in enumerate((RqT, RkT)):
                    act.wait_ge(t_mm, h * 2 + i + 1)
                    nc.scalar.activation(dst, PB[:, i, :], ACT.Copy).then_inc(t_ev, 1)
                act.wait_ge(t_y, h + 1)
                nc.scalar.activation(SBI[:, 0, :].rearrange("p (m d) -> p m d", m=MT),
                                     Zo[:, :, bass.ds(h * RD + RG_, RD)], ACT.Silu).then_inc(t_g, 1)
                act.wait_ge(t_c, h * 5 + 5)
                nc.scalar.activation(stat[:, 48:52], stat[:, 44:48], ACT.Sqrt, bias=stat[:, 61:62], scale=1.0 / RD
                                     ).then_inc(t_sd, 1)

        s_ret = sem("decay_loaded")

        def ret_dve(dve):
            dve.wait_ge(s_ret, 32)
            dve.sem_inc(t_c, 1)
            dve.sem_inc(t_y, 1)
            with dve.Fori(0, RH) as h:
                for j in range(MT):
                    dve.wait_ge(t_s, h * MT + j + 1)
                    w = T - j * P
                    nc.vector.tensor_tensor(Rs[j], PB[:, 2 + j, 0:w],
                                            decay[:, bass.ds(h, 1), 0:w].rearrange("p a w -> p (a w)"), ALU.mult
                                            ).then_inc(t_d, 1)
                dve.wait_ge(t_o, h + 2)
                o = PB[:, 6, :].rearrange("p (m d) -> p m d", m=MT)
                ch = Chain(dve, t_c, h * 5 + 1)
                nc.vector.tensor_reduce(stat[:, 40:44], o, AX.X, ALU.add).then_inc(t_sd2, 1)
                dve.wait_ge(t_sd2, h * 3 + 1)
                nc.vector.tensor_scalar(stat[:, 40:44], stat[:, 40:44], 1.0 / RD, None, ALU.mult).then_inc(t_sd2, 1)
                dve.wait_ge(t_sd2, h * 3 + 2)
                nc.vector.tensor_tensor(Rc, o, stat[:, 40:44].unsqueeze(2).to_broadcast([P, MT, RD]), ALU.subtract
                                        ).then_inc(t_sd2, 1)
                dve.wait_ge(t_sd2, h * 3 + 3)
                ch.add(nc.vector.tensor_tensor(Rsq, Rc, Rc, ALU.mult))
                ch.wait()
                ch.add(nc.vector.tensor_reduce(stat[:, 44:48], Rsq, AX.X, ALU.add))
                ch.wait()
                g = gnr.rearrange("p (h d) -> p h d", h=RH)[:, bass.ds(h, 1), :].to_broadcast([P, MT, RD])
                ch.add(nc.vector.tensor_tensor(Rc, Rc, g, ALU.mult))
                ch.wait()
                dve.wait_ge(t_g, h + 1)
                ch.add(nc.vector.tensor_tensor(Rc, Rc, SBI[:, 0, :].rearrange("p (m d) -> p m d", m=MT), ALU.mult))
                dve.wait_ge(t_sd, h + 1)
                ch.wait()
                ch.add(nc.vector.reciprocal(stat[:, 52:56], stat[:, 48:52]))
                ch.wait()
                nc.vector.tensor_tensor(Y[:, :, bass.ds(h * RD + 512, RD)], Rc,
                                        stat[:, 52:56].unsqueeze(2).to_broadcast([P, MT, RD]), ALU.mult
                                        ).then_inc(t_y, 1)

        t_sd2 = sem("ret_center")

        c_t = sem("cmp_T_mm")
        c_b = sem("cmp_blocks")
        c_g = sem("cmp_gelu")
        c_m = sem("cmp_out_mm")
        c_o = sem("cmp_out")

        def cmp_blk(i):
            return HT[0:DH, 4 * i:4 * i + 4, :].rearrange("p a b -> p (a b)")[:, 0:CB * 2 * NC].rearrange(
                "p (l g n) -> p l g n", l=CB, g=2)

        def cmp_pe(pe):
            pe.wait_ge(t_d, RH * MT)
            for i, base in enumerate((KC_, VC_)):
                for g in range(2):
                    for m in range(MT):
                        t = nc.tensor.transpose(PB[0:DH, 2 * i + g, m * P:(m + 1) * P],
                                                Zo[:, m, base + g * DH:base + (g + 1) * DH], ident[:])
                    t.then_inc(c_t, 1)
            for i in range(2):
                arrived(pe, cmp_n[i])
                pe.wait_ge(c_b, 2 * i + 2)
                w = RING[0:DH, (cmp_n[i] % 3) * WR:(cmp_n[i] % 3 + 1) * WR].rearrange("p (l n) -> p l n", l=CB)
                blk = cmp_blk(i)
                for l in range(CB):
                    t = nc.tensor.matmul(PB[:, 4 + i, 0:2 * NC], w[:, l, :], blk[:, l, :, :], start=(l == 0), stop=(l == CB - 1))
                t.then_inc(c_h, 1)
            pe.wait_ge(c_g, 2)
            nc.tensor.matmul(PB[0:DH, 0, 0:2 * NC], cmpw2[:, 0, :], hidc[:, 0, :], start=True, stop=True).then_inc(c_m, 1)
            for g in range(2):
                nc.tensor.matmul(PB[0:NC, 1 + g, 0:DH], hidc[:, 1, g * NC:(g + 1) * NC], cmpw2[:, 1, :],
                                 start=True, stop=True).then_inc(c_m, 1)

        def cmp_dve(dve):
            dve.wait_ge(t_o, RH + 1)
            for i in range(2):
                for g in range(2):
                    dve.wait_ge(c_t, 2 * i + g + 1)
                    src = PB[0:DH, 2 * i + g, :]
                    win = bass.AP(src.tensor, src.offset, [list(src.ap[0]), [1, CB], [CS, NC]])
                    pos = cmpos[:, i, :].unsqueeze(2).to_broadcast([DH, CB, NC])
                    nc.vector.tensor_tensor(cmp_blk(i)[:, :, g, :], win, pos, ALU.add).then_inc(c_b, 1)
            dve.wait_ge(c_m, 1)
            nc.vector.tensor_copy(kcT[:].rearrange("p g n -> p (g n)"), PB[0:DH, 0, 0:2 * NC]).then_inc(c_o, 1)
            for g in range(2):
                dve.wait_ge(c_m, 2 + g)
                nc.vector.tensor_copy(vcc[:, g, :], PB[0:NC, 1 + g, 0:DH]).then_inc(c_o, 1)

        def cmp_act(act):
            for i in range(2):
                act.wait_ge(c_h, i + 1)
                nc.scalar.activation(hidc[:, i, :], PB[:, 4 + i, 0:2 * NC], ACT.Gelu_apprx_tanh).then_inc(c_g, 1)

        class Attention:

            def __init__(self, name, pairs, units, staged):
                self.name, self.pairs, self.units, self.staged = name, pairs, units, staged
                self.NU = len(units)
                self.stg = sem(name + "_staged")
                self.tm = sem(name + "_T_mm")
                self.te = sem(name + "_T")
                self.qk = sem(name + "_scores_mm")
                self.mx = sem(name + "_max")
                self.bi = sem(name + "_biased")
                self.ex = sem(name + "_exp")
                self.tr = sem(name + "_PT_mm")
                self.pa = sem(name + "_PT_even")
                self.pd = sem(name + "_PT_odd")
                self.pv = sem(name + "_out_mm")
                self.sc = sem(name + "_scale")
                self.oe = sem(name + "_out")
                self.nb = sum(u["bias"] is not None for u in units)

            def pe(self, pe):
                us, NU = self.units, self.NU

                def scores(it, u):
                    x = us[u]
                    w = x["w"]
                    s = PB[:, u % 2, 0:w]
                    m = x["i"]
                    nc_ = nc.tensor.matmul(s, x["qT"][:, m * P:(m + 1) * P], x["kT"][:, 0:w], start=True,
                                           stop=x["mask"] is None)
                    if x["mask"] is not None:
                        mask, c0 = x["mask"]
                        nc_ = nc.tensor.matmul(PB[:, u % 2, c0:w], ident_b[:], mask, start=False, stop=True)
                    nc_.then_inc(self.qk, 1)

                def turned(it, u):
                    x = us[u]
                    pe.wait_ge(self.ex, it * NU + u + 1)
                    w = x["w"]
                    for b in range((w + P - 1) // P):
                        bw = min(P, w - b * P)
                        t = nc.tensor.transpose(PB[0:bw, 2 + u % 2, b * P:(b + 1) * P],
                                                PR[:, u % 2, b * P:b * P + bw], ident[:])
                    t.then_inc(self.tr, 1)

                def values(it, u):
                    x = us[u]
                    if u % 2 == 0:
                        pe.wait_ge(self.pa, it * (NU // 2) + u // 2 + 1)
                    else:
                        pe.wait_ge(self.pd, it * (NU // 2) + u // 2 + 1)
                    pe.wait_ge(self.oe, it * NU + u + 1)
                    w = x["w"]
                    n = (w + P - 1) // P
                    for b in range(n):
                        bw = min(P, w - b * P)
                        t = nc.tensor.matmul(PB[:, 4 + u % 2, 0:DH], PTS[0:bw, u % 2, b, :], x["v"](b)[0:bw],
                                             start=(b == 0), stop=(b == n - 1))
                    t.then_inc(self.pv, 1)

                with pe.Fori(0, self.pairs) as it:
                    ns = len(self.staged)
                    pe.wait_ge(self.stg, it * self.n_pool + self.n_qk)
                    for k, (src, dst, scale) in enumerate(self.staged):
                        if k >= 2:
                            pe.wait_ge(self.te, it * ns + k - 1)
                        rows = src.shape[2]
                        nc.tensor.matmul(PB[0:DH, 6 + k % 2, 0:8], ident[:, 0:DH], ident[:, 0:8], start=True, stop=True)
                        for m in range(MT):
                            t = nc.tensor.transpose(PB[0:rows, 6 + k % 2, m * P:(m + 1) * P], src[:, m, :], ident[:])
                        t.then_inc(self.tm, 1)
                    pe.wait_ge(self.te, it * ns + ns)
                    scores(it, 0)
                    scores(it, 1)
                    pe.wait_ge(self.stg, it * self.n_pool + self.n_pool)
                    for u in range(NU):
                        turned(it, u)
                        if u + 2 < NU:
                            scores(it, u + 2)
                        if u >= 1:
                            values(it, u - 1)
                    values(it, NU - 1)

            def act(self, act):
                us, NU = self.units, self.NU

                def exps(it, u):
                    x = us[u]
                    act.wait_ge(self.mx, it * NU + u + 1)
                    src = PB[:, u % 2, 0:x["w"]] if x["bias"] is None else SBI[:, u % 2, 0:x["w"]]
                    nc.scalar.activation(PR[:, u % 2, 0:x["w"]], src, ACT.Exp, bias=nmx[:, u % 2:u % 2 + 1],
                                         accum_out=den[:, u % 8:u % 8 + 1]).then_inc(self.ex, 1)

                with act.Fori(0, self.pairs) as it:
                    ns = len(self.staged)
                    for k, (src, dst, scale) in enumerate(self.staged):
                        act.wait_ge(self.tm, it * ns + k + 1)
                        nc.scalar.activation(dst, PB[0:src.shape[2], 6 + k % 2, :], ACT.Copy, scale=scale
                                             ).then_inc(self.te, 1)
                    exps(it, 0)
                    for u in range(NU):
                        if u + 1 < NU:
                            exps(it, u + 1)
                        if u % 2 == 0:
                            self.out_T(act, it, u)

            def out_T(self, eng, it, u):
                x = self.units[u]
                w = x["w"]
                eng.wait_ge(self.tr, it * self.NU + u + 1)
                rows = min(w, P)
                n = (w + P - 1) // P
                src = PB[0:rows, 2 + u % 2, 0:n * P]
                dst = PTS[0:rows, u % 2, 0:n, :].rearrange("p a b -> p (a b)")
                if u % 2 == 0:
                    nc.scalar.activation(dst, src, ACT.Copy).then_inc(self.pa, 1)
                else:
                    nc.vector.tensor_copy(dst, src).then_inc(self.pd, 1)

            def dve(self, dve):
                us, NU = self.units, self.NU
                ns_ = sum(1 if x["gate"] is None else (3 if x["valid"] else 2) for x in us)
                dve.sem_inc(self.oe, 2)

                def maxima(it, u):
                    x = us[u]
                    w = x["w"]
                    dve.wait_ge(self.qk, it * NU + u + 1)
                    src = PB[:, u % 2, 0:w]
                    if x["bias"] is not None:
                        nb_ = sum(y["bias"] is not None for y in us[:u + 1])
                        nc.vector.tensor_tensor(SBI[:, u % 2, 0:w], src, x["bias"](it), ALU.add).then_inc(self.bi, 1)
                        dve.wait_ge(self.bi, it * self.nb + nb_)
                        src = SBI[:, u % 2, 0:w]
                    nc.vector.tensor_reduce(nmx[:, u % 2:u % 2 + 1], src, AX.X, ALU.max, negate=True).then_inc(self.mx, 1)

                def add_out(it, u, cnt):
                    x = us[u]
                    dve.wait_ge(self.pv, it * NU + u + 1)
                    r = osc[:, u % 8:u % 8 + 1]

                    def step(ins):
                        cnt[0] += 1
                        ins.then_inc(self.sc, 1)
                        dve.wait_ge(self.sc, it * ns_ + cnt[0])
                    step(nc.vector.reciprocal(r, den[:, u % 8:u % 8 + 1]))
                    if x["gate"] is not None:
                        step(nc.vector.tensor_tensor(r, r, x["gate"](it), ALU.mult))
                        if x["valid"]:
                            step(nc.vector.tensor_tensor(r, r, cvalid[:, x["i"]:x["i"] + 1], ALU.mult))
                    y = x["y"](it)
                    if x["first"]:
                        nc.vector.tensor_scalar(y, PB[:, 4 + u % 2, 0:DH], r, None, ALU.mult).then_inc(self.oe, 1)
                    else:
                        dve.wait_ge(self.oe, it * NU + u + 2)
                        nc.vector.scalar_tensor_tensor(y, PB[:, 4 + u % 2, 0:DH], r, y, ALU.mult, ALU.add
                                                       ).then_inc(self.oe, 1)

                with dve.Fori(0, self.pairs) as it:
                    cnt = [0]
                    maxima(it, 0)
                    maxima(it, 1)
                    for u in range(NU):
                        if u % 2 == 1:
                            self.out_T(dve, it, u)
                        if u + 2 < NU:
                            maxima(it, u + 2)
                        if u >= 1:
                            add_out(it, u - 1, cnt)
                    add_out(it, NU - 1, cnt)

            def done(self, eng):
                eng.wait_ge(self.oe, 2 + self.pairs * self.NU)

        stv = lambda k, w: ST[:, k * 264:k * 264 + MT * w].rearrange("p (m d) -> p m d", m=MT)
        ksT = [HT[0:DH, 0 + g, :] for g in range(2)]
        kwT = [HT[0:DH, 2 + g, :] for g in range(2)]
        qTn = [HT[0:DH, 4 + g, :] for g in range(2)]
        k_mm = sem("nsa_kT_mm")
        k_ev = sem("nsa_kT")

        def unit(i, w, qT, kT, mask, v, y, gate=None, valid=False, bias=None, first=True):
            return dict(i=i, w=w, qT=qT, kT=kT, mask=mask, v=v, y=y, gate=gate, valid=valid, bias=bias, first=first)

        nsa_units = []
        for g in range(2):
            for i in range(MT):
                y = lambda it, g=g, i=i: Y[:, i, bass.ds(it * DH + g * 4 * DH, DH)]
                gate = lambda c, g=g, i=i: (lambda it: gate_s[:, i, bass.ds(it * 3 + (12 * g + c), 1)])
                w = (i + 1) * P
                nsa_units += [
                    unit(i, NC, qTn[g], kcT[:, g, :], (cmask_b[:, i, 0:NC], 0), lambda b, g=g: vcc[:, g, :], y, gate(0), True),
                    unit(i, w, qTn[g], ksT[g], (causal_b[:], i * P),
                         lambda b, g=g: Zo[:, b, VS_ + g * DH:VS_ + (g + 1) * DH], y, gate(1), first=False),
                    unit(i, w, qTn[g], kwT[g], (causal_b[:], i * P),
                         lambda b, g=g: Zo[:, b, VW_ + g * DH:VW_ + (g + 1) * DH], y, gate(2), first=False)]
        nsa = Attention("nsa", 4, nsa_units, [(stv(g, DH), qTn[g], 0.125) for g in range(2)])
        nsa.n_pool, nsa.n_qk = 2, 2

        def nsa_pool(pool):
            pool.wait_ge(t_o, RH + 1)
            with pool.Fori(0, 4) as it:
                pool.wait_ge(nsa.tm, it * 2)
                for g in range(2):
                    nc.gpsimd.tensor_copy(stv(g, DH), Zo[:, :, bass.ds(it * DH + g * 4 * DH, DH)]).then_inc(nsa.stg, 1)

        def nsa_keys_pe(pe):
            pe.wait_ge(c_o, 3)
            for k, (base, g) in enumerate(((KS_, 0), (KS_, 1), (KW_, 0), (KW_, 1))):
                for m in range(MT):
                    t = nc.tensor.transpose(PB[0:DH, k, m * P:(m + 1) * P], Zo[:, m, base + g * DH:base + (g + 1) * DH],
                                            ident[:])
                t.then_inc(k_mm, 1)
            pe.wait_ge(k_ev, 4)

        def nsa_keys_act(act):
            for k, dst in enumerate(ksT + kwT):
                act.wait_ge(k_mm, k + 1)
                nc.scalar.activation(dst, PB[0:DH, k, :], ACT.Copy).then_inc(k_ev, 1)

        n_y1 = Norm("y1", Y, (nsa.oe, lambda m: 2 + nsa.pairs * nsa.NU), [(0, D)], normed=False)
        d_od = Down("od_out", KT, a["od_w_out"][0], 2, lambda eng, k: eng.wait_ge(*n_y1.ready_tile(MT - 1)))
        n4 = Norm("n4", X, d_od.ready(), [(0, D)], gain=3)
        f1 = GateUp("ffn1", n4, a["ffn_w_gate"][1], a["ffn_w_up"][1])
        d_f1 = Down("ffn1_down", FT, a["ffn_w_down"][1], 3, ffn=f1)
        n5 = Norm("n5", X, d_f1.ready(), [(0, D)], gain=4)
        Z2 = Z[:, 0:MT * W2].rearrange("p (m n) -> p m n", m=MT)
        p_2 = Proj("in2", n5, a["w_in_2"][0], W2, Z2, alt)

        lf = sb("lf", [P, MT, NH])
        lt = sb("lt", [P, 3, MT, NH])
        c8 = sb("c8", [P, 2, MT, NH])
        bfr = sb("bfr", [P, NH])
        rb = sb("rb", [NH * 4, NH])
        s_2 = sem("second_consts")
        g_ch = sem("forget_chain")
        g_ex = sem("forget_exp")
        g_mm = sem("forget_cumsum_mm")
        g_c = sem("forget_c8")
        b_mm = sem("bias_row_mm")
        b_sb = sem("bias_row")
        b_dr = sem("bias_row_dram")
        b_ld = sem("bias_table")

        def forget_dve(dve):
            dve.wait_ge(s_2, 16 * 2)
            p_2.wait_all(dve)
            ch = Chain(dve, g_ch)
            ch.add(nc.vector.tensor_tensor(lf[:], Z2[:, :, FP_:FP_ + NH], bfr[:].unsqueeze(1).to_broadcast([P, MT, NH]), ALU.add))
            ch.wait()
            ch.add(nc.vector.tensor_scalar(lt[:, 0], lf[:], -1.0, None, ALU.mult))
            ch.wait()
            ch.add(nc.vector.tensor_tensor(lt[:, 1], lt[:, 0], lf[:], ALU.min))
            ch.add(nc.vector.tensor_scalar(lf[:], lf[:], 0.0, None, ALU.min))
            dve.wait_ge(g_ex, 2)
            ch.wait()
            ch.add(nc.vector.tensor_tensor(lf[:], lf[:], lt[:, 2], ALU.subtract))
            dve.wait_ge(g_mm, 1)
            nc.vector.tensor_scalar(c8[:, 0], PB[:, 6, 0:MT * NH].rearrange("p (m h) -> p m h", m=MT), 8.0, None, ALU.mult
                                    ).then_inc(g_c, 1)
            nc.vector.tensor_scalar(c8[:, 1], PB[:, 6, 0:MT * NH].rearrange("p (m h) -> p m h", m=MT), -8.0, None, ALU.mult
                                    ).then_inc(g_c, 1)

        def forget_act(act):
            act.wait_ge(g_ch, 3)
            nc.scalar.activation(lt[:, 2], lt[:, 1], ACT.Exp).then_inc(g_ex, 1)
            act.wait_ge(g_ex, 1)
            nc.scalar.activation(lt[:, 2], lt[:, 2], ACT.Ln, bias=1.0).then_inc(g_ex, 1)

        def forget_pe(pe):
            pe.wait_ge(g_ch, 5)
            for m in range(MT):
                for j in range(m + 1):
                    t = nc.tensor.matmul(PB[:, 6, m * NH:(m + 1) * NH], upper[:] if j == m else ones[:], lf[:, j, :],
                                         start=(j == 0), stop=(j == m))
            t.then_inc(g_mm, 1)

        ohot = ST[0:NH * 4, 0:TW]
        brow = ST[0:NH, TW:2 * TW]
        badd = ST[0:NH, 2 * TW:3 * TW]

        def bias_pe(pe):
            pe.wait_ge(s_2, 16 * 2)
            pe.wait_ge(s_2b, 16 * 2)
            for k, (c0, c1) in enumerate(((0, 512), (512, TW))):
                t = nc.tensor.matmul(PB[0:NH, 6 + k, 0:c1 - c0], rb[:], ohot[:, c0:c1], start=True, stop=True)
            t.then_inc(b_mm, 1)

        s_2b = sem("bias_consts")

        def bias_dve(dve):
            dve.wait_ge(b_mm, 1)
            for k, (c0, c1) in enumerate(((0, 512), (512, TW))):
                nc.vector.tensor_tensor(brow[:, c0:c1], PB[0:NH, 6 + k, 0:c1 - c0], badd[:, c0:c1], ALU.add).then_inc(b_sb, 1)

        b_rev = sem("bias_turned")
        bias_raw = [x.rearrange("p (h t) -> p h t", h=4) for x in (ST[:, 0:4 * T], WK[:, 1024:1024 + 4 * T])]

        def load_bias(pool, half):
            src = bass.AP(bias_dram.tensor, half * 4 * TW, [[1, P], [TW, 4], [1, T]])
            pool.dma_start(bias_raw[half], src).then_inc(b_ld, 16)

        def bias_turn_dve(dve):
            dve.wait_ge(*p_2.mm.at((MT + 1) * len(p_2.cols)))
            dve.wait_ge(b_ld, 32)
            for half in range(2):
                nc.vector.tensor_copy(BIAS[:, 4 * half:4 * half + 4, :], bias_raw[half][:, :, T - 1::-1]).then_inc(b_rev, 1)

        STG = sb("STG", [P, 12 * 264 - 2112])
        def st2(k, w):
            buf, kk = (ST, k) if k < 8 else (STG, k - 8)
            return buf[:, kk * 264:kk * 264 + MT * w].rearrange("p (m d) -> p m d", m=MT)

        two_units = []
        staged = []
        for p in range(2):
            w66 = DH + 2
            qd, kd, qf, kf = [HT[0:(DH if t < 2 else w66), 4 * p + t, :] for t in range(4)]
            staged += [(st2(6 * p + 0, DH), qd, 0.125), (st2(6 * p + 1, DH), kd, 1.0),
                       (st2(6 * p + 2, w66), qf, 0.125), (st2(6 * p + 3, w66), kf, 1.0)]
            for i in range(MT):
                w = (i + 1) * P
                for k, (q_, k_, base) in enumerate(((qd, kd, 0), (qf, kf, 512))):
                    y = lambda it, p=p, i=i, base=base: Y[:, i, bass.ds(it * 2 * DH + (p * DH + base), DH)]
                    v = lambda b, p=p, k=k: st2(6 * p + 4 + k, DH)[:, b, :]
                    if k == 0:
                        bias = lambda it, p=p, i=i, w=w: BIAS[:, bass.ds(it * 2 + p, 1), T - w:T].rearrange("p a w -> p (a w)")
                        two_units.append(unit(i, w, q_, k_, None, v, y, bias=bias))
                    else:
                        two_units.append(unit(i, w, q_, k_, (causal_b[:], i * P), v, y))
        two = Attention("two", 4, two_units, staged)
        s_one = sem("staged_ones")

        def two_pool(pool):
            pool.wait_ge(nsa.tm, 8)
            pool.wait_ge(b_rev, 1)
            for p in range(2):
                nc.gpsimd.memset(st2(6 * p + 2, DH + 2)[:, :, DH + 1:DH + 2], 1.0).then_inc(s_one, 1)
                nc.gpsimd.memset(st2(6 * p + 3, DH + 2)[:, :, DH:DH + 1], 1.0).then_inc(s_one, 1)
            pool.wait_ge(g_c, 2)
            pool.wait_ge(s_one, 4)
            p_2.wait_all(pool)
            with pool.Fori(0, 4) as it:
                def z(base, p):
                    return Z2[:, :, bass.ds(it * 2 * DH + (p * DH + base), DH)]
                for p in range(2):
                    h = lambda k: c8[:, k, :, bass.ds(it * 2 + p, 1)]
                    for k, src in enumerate((QA_, KA_, QF_, KF_)):
                        dst = st2(6 * p + k, DH + 2 if k in (2, 3) else DH)
                        nc.gpsimd.tensor_copy(dst[:, :, 0:DH], z(src, p)).then_inc(two.stg, 1)
                    nc.gpsimd.tensor_copy(st2(6 * p + 2, DH + 2)[:, :, DH:DH + 1], h(0)).then_inc(two.stg, 1)
                    nc.gpsimd.tensor_copy(st2(6 * p + 3, DH + 2)[:, :, DH + 1:DH + 2], h(1)).then_inc(two.stg, 1)
                pool.wait_ge(two.oe, it * two.NU + 2)
                for p in range(2):
                    for k, src in ((4, VA_), (5, VF_)):
                        nc.gpsimd.tensor_copy(st2(6 * p + k, DH), z(src, p)).then_inc(two.stg, 1)
                pool.wait_ge(two.tm, it * 8 + 8)
        two.n_pool, two.n_qk = 16, 12

        n_y2 = Norm("y2", Y, (two.oe, lambda m: 2 + two.pairs * two.NU), [(0, 512), (512, D)], gain=5)
        d_2 = Down("out2", KT, a["w_out_2"][0], None, lambda eng, k: eng.wait_ge(*n_y2.ready_tile(MT - 1)))
        n6 = Norm("n6", X, d_2.ready(), [(0, D)], rows=GP[:, 0, :], split=False)

        o_ = [0]
        Zr = lambda words: (Z[:, o_[0]:o_[0] + words], o_.__setitem__(0, o_[0] + words))[0]
        wrt = Zr(KT * 36).rearrange("p (k n) -> p k n", k=KT)
        brt = Zr(36)
        strict = Zr(P)
        o_io = o_[0]
        io128, io40, tokid, pri = Zr(P), Zr(NB), Zr(MT), Zr(EG)
        lg = Zr(MT * 36).rearrange("p (m n) -> p m n", m=MT)
        L = lambda n: Zr(MT * n).rearrange("p (m n) -> p m n", m=MT)
        gm, g_oh, g_t, g1 = L(1), L(4), L(4), L(1)
        sel, se_t = L(EG), L(EG)
        oh1, oh2 = L(EG), L(EG)
        v1, v2, w1_, w2_, pm = L(1), L(1), L(1), L(1), L(1)
        a1, a2, aa = L(NE), L(NE), L(NE)
        rank, t32 = L(NE), L(NE)
        cnt_ = Zr(NE)
        nblk = Zr(NE)
        bend, bst, t32b = Zr(NE), Zr(NE), Zr(NE)
        slot1, slot2 = L(1), L(1)
        blk_ = L(1)
        si = sb("slot_i", [P, 2, MT], i32)
        idxf = Zr(NB)
        idxi = sb("idx_i", [P, NB + 2], i32)
        bex = Zr(NO * NE).rearrange("p (b e) -> p b e", e=NE)
        bexs = Zr(NO)
        bexi = sb("block_expert", [P, NB], i32)
        ohp = Zr(2 * P).rearrange("p (s n) -> p s n", s=2)
        ohb = Zr(2 * NB).rearrange("p (s n) -> p s n", s=2)
        moe0 = o_[0]
        s_rc = sem("router_consts")
        q_mm = sem("router_logits_mm")
        q_ch = sem("router_chain")
        q_ex = sem("router_exp")
        q_rk = sem("router_rank_mm")
        q_oh = sem("router_onehot")
        q_id = sem("router_index_mm")
        q_done = sem("router_done")
        s_h2 = sem("h2_rows_stored")

        def bc(x, n):
            return x.to_broadcast([P, MT, n])

        def router_pe(pe):
            pe.wait_ge(s_rc, 16 * 7)
            pe.wait_ge(*n6.ready_tile(MT - 1))
            for m in range(MT):
                for k in range(KT):
                    t = nc.tensor.matmul(PB[:, 4, m * 36:(m + 1) * 36], HT[:, k, m * P:(m + 1) * P], wrt[:, k, :],
                                         start=(k == 0), stop=(k == KT - 1))
            t.then_inc(q_mm, 1)
            pe.wait_ge(q_done, 1)
            for m in range(MT):
                for j in range(m + 1):
                    t = nc.tensor.matmul(PB[:, 5, m * NE:(m + 1) * NE], strict if j == m else ones[:], aa[:, j, :],
                                         start=(j == 0), stop=(j == m))
            t.then_inc(q_rk, 1)
            for j in range(MT):
                t = nc.tensor.matmul(PB[:, 6, 0:NE], ones[:], aa[:, j, :], start=(j == 0), stop=(j == MT - 1))
            t.then_inc(q_rk, 1)
            for n in range(2 * MT):
                pe.wait_ge(q_oh, 2 * (n + 1))
                nc.tensor.matmul(PB[:, 7, 0:NB], ohp[:, n % 2, :], ohb[:, n % 2, :], start=(n == 0), stop=(n == 2 * MT - 1)
                                 ).then_inc(q_id, 1)

        def router_act(act):
            act.wait_ge(q_ch, 3)
            nc.scalar.activation(g_t, g_t, ACT.Exp).then_inc(q_ex, 1)
            act.wait_ge(q_ch, ROUTER_V)
            nc.scalar.activation(w2_, w2_, ACT.Exp).then_inc(q_ex, 1)

        ROUTER_V = 31

        def router_dve(dve):
            dve.wait_ge(s_rc, 16 * 7)
            dve.wait_ge(q_mm, 1)
            ch = Chain(dve, q_ch)

            def tt(o, x, y, op):
                ch.wait() if ch.n else None
                ch.add(nc.vector.tensor_tensor(o, x, y, op))

            def ts(o, x, s1, s2, op0, op1=None):
                ch.wait()
                ch.add(nc.vector.tensor_scalar(o, x, s1, s2, op0, op1) if op1 is not None
                       else nc.vector.tensor_scalar(o, x, s1, None, op0))

            def red(o, x, op):
                ch.wait()
                ch.add(nc.vector.tensor_reduce(o, x, AX.X, op))

            def first_max(oh, x, mx_, n, tmp):
                tt(oh, x, bc(mx_, n), ALU.is_equal)
                tt(tmp, oh, pri[:, 0:n].unsqueeze(1).to_broadcast([P, MT, n]), ALU.mult)
                red(pm, tmp, ALU.max)
                tt(oh, tmp, bc(pm, n), ALU.is_equal)

            tt(lg, PB[:, 4, 0:MT * 36].rearrange("p (m n) -> p m n", m=MT), brt.unsqueeze(1).to_broadcast([P, MT, 36]), ALU.add)
            red(gm, lg[:, :, 0:4], ALU.max)
            tt(g_t, lg[:, :, 0:4], bc(gm, 4), ALU.subtract)
            dve.wait_ge(q_ex, 1)
            red(g1, g_t, ALU.add)
            ch.wait()
            ch.add(nc.vector.reciprocal(g1, g1))
            first_max(g_oh, lg[:, :, 0:4], gm, 4, g_t)
            le = lg[:, :, 4:36].rearrange("p m (g e) -> p m g e", g=NG)
            for g in range(NG):
                if g == 0:
                    tt(sel, le[:, :, 0, :], bc(g_oh[:, :, 0:1], EG), ALU.mult)
                else:
                    tt(se_t, le[:, :, g, :], bc(g_oh[:, :, g:g + 1], EG), ALU.mult)
                    tt(sel, sel, se_t, ALU.add)
            red(v1, sel, ALU.max)
            first_max(oh1, sel, v1, EG, se_t)
            ts(se_t, oh1, -3.0e38, None, ALU.mult)
            tt(sel, sel, se_t, ALU.add)
            red(v2, sel, ALU.max)
            first_max(oh2, sel, v2, EG, se_t)
            tt(w2_, v2, v1, ALU.subtract)
            for g in range(NG):
                o4 = lambda x: x.rearrange("p m (g e) -> p m g e", g=NG)[:, :, g, :]
                tt(o4(a1), oh1, bc(g_oh[:, :, g:g + 1], EG), ALU.mult)
                tt(o4(a2), oh2, bc(g_oh[:, :, g:g + 1], EG), ALU.mult)
            ch.wait()
            nc.vector.tensor_tensor(aa, a1, a2, ALU.add).then_inc(q_done, 1)
            dve.wait_ge(q_ex, 2)
            ts(w1_, w2_, 1.0, None, ALU.add)
            ch.wait()
            ch.add(nc.vector.reciprocal(w1_, w1_))
            tt(w2_, w2_, w1_, ALU.mult)
            tt(w1_, w1_, g1, ALU.mult)
            tt(w2_, w2_, g1, ALU.mult)
            dve.wait_ge(q_rk, 2)
            ch.wait()
            ch.add(nc.vector.tensor_copy(cnt_, PB[:, 6, 0:NE]))
            ch.wait()
            ch.add(nc.vector.tensor_copy(rank, PB[:, 5, 0:MT * NE].rearrange("p (m n) -> p m n", m=MT)))
            ts(nblk, cnt_, float(P), None, ALU.is_gt)
            for j in range(2, MT):
                ts(t32b, cnt_, float(j * P), None, ALU.is_gt)
                tt(nblk, nblk, t32b, ALU.add)
            ts(t32b, nblk, 0.0, None, ALU.mult)
            ch.wait()
            ch.add(nc.vector.tensor_tensor_scan(bend, nblk, t32b, 0.0, ALU.add, ALU.add))
            tt(bst, bend, nblk, ALU.subtract)
            tt(bex, bend.unsqueeze(1).to_broadcast([P, NO, NE]), io40[:, 0:NO].unsqueeze(2).to_broadcast([P, NO, NE]), ALU.is_le)
            red(bexs, bex, ALU.add)
            ts(bexs, bexs, float(NE - 1), None, ALU.min)
            ch.wait()
            ch.add(nc.vector.tensor_copy(bexi[:, NE:NB], bexs))
            ch.add(nc.vector.tensor_copy(bexi[:, 0:NE], io40[:, 0:NE]))
            ts(bst, bst, float(NE - 1), float(P), ALU.add, ALU.mult)
            tt(bst, bst, io40x[:, 0:NE], ALU.subtract)
            ts(t32, rank, float(P), None, ALU.is_ge)
            tt(t32, t32, bst.unsqueeze(1).to_broadcast([P, MT, NE]), ALU.mult)
            tt(rank, rank, t32, ALU.add)
            tt(rank, rank, io40x[:, 0:NE].unsqueeze(1).to_broadcast([P, MT, NE]), ALU.add)
            n = 0
            for k, (as_, sl) in enumerate(((a1, slot1), (a2, slot2))):
                tt(t32, rank, as_, ALU.mult)
                red(sl, t32, ALU.add)
                ch.wait()
                ch.add(nc.vector.tensor_copy(si[:, k, :], sl.rearrange("p m a -> p (m a)")))
                tt(bex2, bc(sl, NB), io40x.unsqueeze(1).to_broadcast([P, MT, NB]), ALU.is_ge)
                red(blk_, bex2, ALU.add)
                ts(blk_, blk_, 1.0, None, ALU.subtract)
                ts(pm, blk_, -float(P), None, ALU.mult)
                tt(pm, pm, sl, ALU.add)
                for m in range(MT):
                    if n >= 2:
                        dve.wait_ge(q_id, n - 1)
                    ch.wait()
                    nc.vector.tensor_scalar(ohp[:, n % 2, :], io128, pm[:, m, :], None, ALU.is_equal).then_inc(q_oh, 1)
                    nc.vector.tensor_scalar(ohb[:, n % 2, :], io40, blk_[:, m, :], tokid[:, m:m + 1], ALU.is_equal, ALU.mult
                                            ).then_inc(q_oh, 1)
                    n += 1
            dve.wait_ge(q_id, 2 * MT)
            ch.add(nc.vector.memset(idxi[:, NB:NB + 2], 0))
            nc.vector.tensor_copy(idxi[:, 0:NB], PB[:, 7, 0:NB]).then_inc(q_done, 1)
            ch.wait()
            dve.wait_ge(q_done, 2)

        bex2 = Zr(MT * NB).rearrange("p (m b) -> p m b", m=MT)
        io40x = Zr(NB)
        moe0 = o_[0]

        Xg = Z[:, moe0:moe0 + 3 * D].rearrange("p (s n) -> p s n", s=3)
        XgT = Y[:].rearrange("p m n -> p (m n)")[:, 0:3 * D].rearrange("p (s k n) -> p s k n", s=3, k=KT)
        Ob = [ST[:, 0:D], ST[:, D:2 * D], Z[:, moe0 + 3 * D:moe0 + 4 * D]]
        Hs, Hh, HhT = [WK[:, i * 768:(i + 1) * 768].rearrange("p (s n) -> p s n", s=3) for i in range(3)]
        assert moe0 + 4 * D <= MT * OD, moe0
        idc = sb("idx_col", [P, 3], i32)
        ht_flat = HT.rearrange("p k n -> p (k n)")
        bias_flat = BIAS.rearrange("p k n -> p (k n)")
        EGU = [RING[:, 0:4096], RING[:, 4096:8192], ht_flat]
        EDW = [RING[:, 8192:10240], RING[:, 10240:12288], bias_flat[:, 0:2048]]
        m_w = [sem(f"expert_gate_up_w{s}") for s in range(3)]
        m_wd = [sem(f"expert_down_w{s}") for s in range(3)]
        m_idle = sem("idle_steps")
        m_ix = sem("block_index")
        m_g = [sem(f"rows_gathered{s}") for s in range(3)]
        m_t = sem("rows_T_mm")
        m_te = sem("rows_T")
        m_gu = sem("gate_up_mm")
        m_si = sem("expert_silu")
        m_h = sem("expert_hidden")
        m_ht = sem("hidden_T_mm")
        m_he = sem("hidden_T")
        m_d = sem("expert_down_mm")
        m_od = sem("rows_out")
        m_st = [sem(f"rows_stored{s}") for s in range(3)]
        LOOPS = NB // 3 - 1

        def moe_sync(sp):
            def load_gu(s, e):
                gu = EGU[s].rearrange("p (k t n) -> p k t n", k=KT, t=2)
                for t, w in enumerate(("w_expert_gate_2", "w_expert_up_2")):
                    sp.dma_start(gu[:, :, t, :], a[w][0][e].rearrange("a (k p) n -> p (a k) n", p=P)).then_inc(m_w[s], 16)

            def load_d(s, e):
                sp.dma_start(EDW[s].rearrange("p (k n) -> p k n", k=2),
                             a["w_expert_down_2"][0][e].rearrange("a (k p) n -> p (a k) n", p=P)).then_inc(m_wd[s], 16)

            n = len(chunks)
            for c in range(n - 3, n):
                s, v = chunks[c]["done"]
                sp.wait_ge(s, v)
            for s in range(3):
                if s == 2:
                    sp.wait_ge(q_mm, 1)
                load_gu(s, slice(s, s + 1))
                load_d(s, slice(s, s + 1))
            sp.wait_ge(q_done, 2)
            with sp.Fori(0, LOOPS) as it:
                for s in range(3):
                    e = sp.value_load(bexi[0:1, bass.ds(it * 3 + (3 + s), 1)], min_val=0, max_val=NE - 1)
                    sp.wait_ge(m_gu, it * 3 + (s + 1))
                    load_gu(s, bass.ds(e, 1))
                    sp.wait_ge(m_d, it * 6 + (2 * s + 2))
                    load_d(s, bass.ds(e, 1))

        def moe_pool(pool):
            pool.wait_ge(s_h2, 16 * MT)
            pool.sem_inc(m_idle, 1)
            with pool.Fori(0, NB // 3) as it:
                for s in range(3):
                    pool.wait_ge(m_ix, it * 3 + (s + 1))
                    pool.wait_ge(m_idle, it * 3 + (s + 1))
                    nc.gpsimd.tensor_tensor(idle[:, 0:1], idle[:, 1:2], idle[:, 1:2], ALU.mult).then_inc(m_idle, 1)
                    nc.gpsimd.indirect_dma_start(
                        Xg[:, s, :], None, h2_dram[:, :],
                        bass.IndirectOffsetOnAxis(ap=idc[:, s:s + 1], axis=0)).then_inc(m_g[s], 16)

        def moe_pe(pe):
            def turn_rows(it, s):
                if not (isinstance(it, int) and 3 * it + s == 0):
                    pe.wait_ge(m_te, it * 6 + 2 * s)
                pe.wait_ge(m_g[s % 3], it * 16 + 16 * (s // 3 + 1))
                for hf in range(2):
                    for k in range(4):
                        t = nc.tensor.transpose(PB[:, hf, k * P:(k + 1) * P],
                                                Xg[:, s % 3, (4 * hf + k) * P:(4 * hf + k + 1) * P], ident[:])
                    t.then_inc(m_t, 1)

            def gate_up(it, s):
                pe.wait_ge(m_te, it * 6 + (2 * s + 2))
                pe.wait_ge(m_w[s % 3], it * 32 + 32 * (s // 3 + 1))
                gu = EGU[s % 3].rearrange("p (k n) -> p k n", k=KT)
                for k in range(KT):
                    t = nc.tensor.matmul(PB[:, 2 + s % 3, :], XgT[:, s % 3, k, :], gu[:, k, :], start=(k == 0), stop=(k == KT - 1))
                t.then_inc(m_gu, 1)

            def turn_hidden(it, s):
                pe.wait_ge(m_h, it * 3 + (s + 1))
                for j in range(2):
                    t = nc.tensor.transpose(PB[:, 5, j * P:(j + 1) * P], Hh[:, s, j * P:(j + 1) * P], ident[:])
                t.then_inc(m_ht, 1)

            def down(it, s):
                pe.wait_ge(m_he, it * 3 + (s + 1))
                pe.wait_ge(m_wd[s], it * 16 + 16)
                pe.wait_ge(m_od, it * 6 + (2 * s + 2))
                wd = EDW[s].rearrange("p (k n) -> p k n", k=2)
                for hf in range(2):
                    for j in range(2):
                        t = nc.tensor.matmul(PB[:, 6 + hf, :], HhT[:, s, j * P:(j + 1) * P], wd[:, j, hf * 512:(hf + 1) * 512],
                                             start=(j == 0), stop=(j == 1))
                    t.then_inc(m_d, 1)

            def step(it, s, turn=True, gu=True):
                if turn:
                    turn_rows(it, s + 2)
                turn_hidden(it, s)
                if gu:
                    gate_up(it, s + 1)
                down(it, s)

            turn_rows(0, 0)
            turn_rows(0, 1)
            gate_up(0, 0)
            with pe.Fori(0, LOOPS) as it:
                for s in range(3):
                    step(it, s)
            for s in range(3):
                step(LOOPS, s, turn=(s < 1), gu=(s < 2))

        def moe_act(act):
            def silu(it, s):
                act.wait_ge(m_gu, it * 3 + (s + 1))
                nc.scalar.activation(Hs[:, s % 3, :], PB[:, 2 + s % 3, 0:256], ACT.Silu).then_inc(m_si, 1)

            def store(it, s):
                act.wait_ge(m_od, it * 6 + (2 * s + 4))
                act.dma_start(slot_dram[bass.ds(it * (3 * P) + s * P, P), :], Ob[s]).then_inc(m_st[s], 16)

            silu(0, 0)
            with act.Fori(0, LOOPS) as it:
                for s in range(3):
                    silu(it, s + 1)
                    store(it, s)
            for s in range(3):
                if s < 2:
                    silu(LOOPS, s + 1)
                store(LOOPS, s)

        def moe_dve(dve):
            dve.sem_inc(m_od, 2)
            for s in range(3):
                dve.sem_inc(m_st[s], 16)
                nc.vector.tensor_copy(idc[:, s:s + 1], idxi[:, s:s + 1]).then_inc(m_ix, 1)

            def rows_T(it, s, index=True):
                for hf in range(2):
                    dve.wait_ge(m_t, it * 6 + (2 * s + hf + 1))
                    nc.vector.tensor_copy(XgT[:, s % 3, 4 * hf:4 * hf + 4, :].rearrange("p k n -> p (k n)"), PB[:, hf, :]
                                          ).then_inc(m_te, 1)
                if index:
                    nc.vector.tensor_copy(idc[:, s % 3:s % 3 + 1], idxi[:, bass.ds(it * 3 + (s + 3), 1)]).then_inc(m_ix, 1)

            def hidden_T(it, s):
                dve.wait_ge(m_ht, it * 3 + (s + 1))
                nc.vector.tensor_copy(HhT[:, s, :], PB[:, 5, 0:256]).then_inc(m_he, 1)

            def hidden(it, s):
                dve.wait_ge(m_si, it * 3 + (s + 1))
                nc.vector.tensor_tensor(Hh[:, s % 3, :], PB[:, 2 + s % 3, 256:512], Hs[:, s % 3, :], ALU.mult).then_inc(m_h, 1)

            def rows_out(it, s):
                dve.wait_ge(m_st[s], it * 16 + 16)
                for hf in range(2):
                    dve.wait_ge(m_d, it * 6 + (2 * s + hf + 1))
                    nc.vector.tensor_copy(Ob[s][:, hf * 512:(hf + 1) * 512], PB[:, 6 + hf, :]).then_inc(m_od, 1)

            def step(it, s, turn=True, gu=True, index=True):
                if turn:
                    rows_T(it, s + 2, index)
                hidden_T(it, s)
                if gu:
                    hidden(it, s + 1)
                rows_out(it, s)

            rows_T(0, 0)
            rows_T(0, 1)
            hidden(0, 0)
            with dve.Fori(0, LOOPS) as it:
                for s in range(3):
                    step(it, s)
            for s in range(3):
                step(LOOPS, s, turn=(s < 1), gu=(s < 2), index=False)

        l_g = [sem("token_rows0"), sem("token_rows1")]
        l_a = sem("last_add")
        l_sq = sem("last_square")
        l_st = sem("last_std")
        l_r = sem("last_rstd")
        l_y = sem("last_y")
        s_out = sem("out_stored")
        R1 = Z[:, moe0:moe0 + 2 * D].rearrange("p (s n) -> p s n", s=2)
        R2 = Z[:, moe0 + 2 * D:moe0 + 4 * D].rearrange("p (s n) -> p s n", s=2)

        def last_pool(pool):
            for s in range(3):
                pool.wait_ge(m_st[s], 16 + 16 * (NB // 3))
            pool.wait_ge(m_gu, NB)
            for m in range(MT):
                if m >= 2:
                    pool.wait_ge(l_a, 2 * (m - 1))
                for k, r in enumerate((R1, R2)):
                    nc.gpsimd.indirect_dma_start(
                        r[:, m % 2, :], None, slot_dram[:, :],
                        bass.IndirectOffsetOnAxis(ap=si[:, k, m:m + 1], axis=0)).then_inc(l_g[m % 2], 16)

        def last_dve(dve):
            wait_gain(dve, 5)
            for m in range(MT):
                dve.wait_ge(l_g[m % 2], 32 * (m // 2 + 1))
                nc.vector.scalar_tensor_tensor(X[:, m, :], R1[:, m % 2, :], w1_[:, m, :], X[:, m, :], ALU.mult, ALU.add
                                               ).then_inc(l_a, 1)
                dve.wait_ge(l_a, 2 * m + 1)
                nc.vector.scalar_tensor_tensor(X[:, m, :], R2[:, m % 2, :], w2_[:, m, :], X[:, m, :], ALU.mult, ALU.add
                                               ).then_inc(l_a, 1)
            for m in range(MT):
                dve.wait_ge(l_st, m + 1)
                nc.vector.reciprocal(stat[:, 32 + m:33 + m], stat[:, 16 + m:17 + m]).then_inc(l_r, 1)
                dve.wait_ge(l_r, m + 1)
                nc.vector.scalar_tensor_tensor(Y[:, m, :], X[:, m, :], stat[:, 32 + m:33 + m], GP[:, 1, :],
                                               ALU.mult, ALU.mult).then_inc(l_y, 1)

        def last_act(act):
            for m in range(MT):
                act.wait_ge(l_a, 2 * (m + 1))
                nc.scalar.activation(SIL[:, 0:2, :].rearrange("p a b -> p (a b)"), X[:, m, :], ACT.Square,
                                     accum_out=stat[:, m:m + 1]).then_inc(l_sq, 1)
                act.wait_ge(l_sq, m + 1)
                nc.scalar.activation(stat[:, 16 + m:17 + m], stat[:, m:m + 1], ACT.Sqrt, bias=stat[:, 60:61],
                                     scale=1.0 / D).then_inc(l_st, 1)

        out_v = out[0].rearrange("(m p) n -> p m n", p=P)
        s_init = sem("init")

        block = ctx.enter_context(nc.Block())

        @block.sync
        def _(sp):
            sp.dma_start(ident[:], a["c_ident"]).then_inc(s_const, 16)
            sp.dma_start(X[:], a["x"][0].rearrange("(m p) n -> p m n", p=P)).then_inc(s_x, 16)
            for n in range(3):
                load_chunk(sp, n)
            for n in range(3, len(chunks)):
                load_chunk(sp, n)
            moe_sync(sp)
            for m in range(MT):
                sp.wait_ge(l_y, m + 1)
                sp.dma_start(out_v[:, m, :], Y[:, m, :]).then_inc(s_out, 16)
            sp.wait_ge(s_out, 16 * MT)

        @block.gpsimd
        def _(pool):
            nc.gpsimd.memset(ones[:], 1.0).then_inc(s_init, 1)
            nc.gpsimd.memset(idle[:], 0.0)
            nc.gpsimd.memset(stat[:, 60:61], 1e-6).then_inc(s_init, 1)
            nc.gpsimd.memset(stat[:, 61:62], 1e-5).then_inc(s_init, 1)
            for i, v in enumerate((a["ln_mix_pre"][0], a["ln_mix_pre"][1], a["ln_ffn_pre"][0], a["ln_ffn_pre"][1],
                                   a["attn_norm_2"][0])):
                pool.dma_start(gains[:, i, :], v.rearrange("(k p) -> p k", p=P), allow_slow_non_contiguous=True
                               ).then_inc(s_gain_n1 if i == 0 else s_gains, 16)
            pool.dma_start(gains[:, 5, 0:4], a["out_norm_dil_2"][0].rearrange("(k p) -> p k", p=P),
                           allow_slow_non_contiguous=True).then_inc(s_gains, 16)
            pool.dma_start(gains[:, 5, 4:8], a["out_norm_fox_2"][0].rearrange("(k p) -> p k", p=P),
                           allow_slow_non_contiguous=True).then_inc(s_gains, 16)
            pool.dma_start(upper[:], a["c_upper"]).then_inc(s_gains, 16)
            for dst, src in ((poolA, a["c_poolA"]), (poolB, a["c_poolB"]),
                             (poolW, a["ev_pool_w"][0].rearrange("g c d -> c g d")),
                             (sguW, a["ev_sgu_w"][0].rearrange("g t s -> t g s")),
                             (lng, a["ev_sgu_ln_g"].to_broadcast([P, 512])),
                             (lnb, a["ev_sgu_ln_b"].to_broadcast([P, 512])),
                             (sgub[0:1, :], a["ev_sgu_b"].rearrange("a g t -> a (g t)")),
                             (pscale, a["ev_pool_scale"][0].rearrange("(k p) -> p k", p=P))):
                pool.dma_start(dst, src, allow_slow_non_contiguous=True).then_inc(s_ev, 16)
            load_gain(pool, 0)
            load_gain(pool, 1)
            for dst, src in ((posi[:], a["positions"][0].rearrange("(m p) -> p m", p=P)),
                             (invf[:], a["c_invf"].to_broadcast([P, 72])), (cvalid[:], a["c_cvalid"]),
                             (cmpw2[:, 0, :], a["od_cmp_k_w2"][0]), (cmpw2[:, 1, :], a["od_cmp_v_w2"][0]),
                             (cmpos[:, 0, :], a["od_cmp_k_pos"][0].rearrange("l d -> d l")),
                             (cmpos[:, 1, :], a["od_cmp_v_pos"][0].rearrange("l d -> d l")),
                             (causal_b[:], a["c_causal"]), (cmask_b[:], a["c_cmask"]), (ident_b[:], a["c_ident"])):
                pool.dma_start(dst, src, allow_slow_non_contiguous=True).then_inc(s_od, 16)
            for dst, src in ((bfr[:], a["b_forget_2"].to_broadcast([P, NH])), (rb[:], a["rel_bias_2"])):
                pool.dma_start(dst, src, allow_slow_non_contiguous=True).then_inc(s_2, 16)
            pool.wait_ge(*d_ev.xr.at(MT))
            load_gain(pool, 2)
            pool.wait_ge(*p_od.mm.at((MT + 1) * len(p_od.cols)))
            pool.dma_start(decay, a["c_decay"]).then_inc(s_ret, 16)
            pool.dma_start(gnr, a["od_ret_gn_g"].to_broadcast([P, 512])).then_inc(s_ret, 16)
            ret_pool(pool)
            nsa_pool(pool)
            pool.wait_ge(*d_f0.xr.at(MT))
            load_gain(pool, 3)
            nsa.done(pool)
            for dst, src in ((ohot, a["c_onehot"]), (badd, a["c_badd"].to_broadcast([NH, TW]))):
                pool.dma_start(dst, src, allow_slow_non_contiguous=True).then_inc(s_2b, 16)
            pool.wait_ge(b_sb, 2)
            pool.dma_start(bias_dram[:, :], brow).then_inc(b_dr, 16)
            pool.wait_ge(b_dr, 16)
            load_bias(pool, 0)
            pool.wait_ge(*d_od.xr.at(MT))
            load_gain(pool, 4)
            pool.wait_ge(*d_f1.xr.at(MT))
            load_gain(pool, 5)
            pool.wait_ge(*n5.ready_tile(MT - 1))
            load_bias(pool, 1)
            two_pool(pool)
            two.done(pool)
            for dst, src in ((wrt[:, :, 0:4], a["w_router_group_2"][0].rearrange("(k p) n -> p k n", p=P)),
                             (wrt[:, :, 4:36], a["w_router_expert_2"][0].rearrange("(k p) n -> p k n", p=P)),
                             (brt[:, 0:4], a["b_router_group_2"].to_broadcast([P, 4])),
                             (brt[:, 4:36], a["b_router_expert_2"].to_broadcast([P, NE])),
                             (strict, a["c_strict"]),
                             (Z[:, o_io:o_io + P + NB + MT + EG], a["c_iotas"]),
                             (io40x, a["c_io40x"].to_broadcast([P, NB]))):
                pool.dma_start(dst, src, allow_slow_non_contiguous=True).then_inc(s_rc, 16)
            for m in range(MT):
                pool.wait_ge(*n6.xn.at(m + 1))
                pool.dma_start(h2_dram[m * P:(m + 1) * P, :], Y[:, m, :]).then_inc(s_h2, 16)
            moe_pool(pool)
            last_pool(pool)

        @block.scalar
        def _(act):
            act.wait_ge(s_init, 3)
            n1.act(act)
            p_ev.take(act, "act")
            even_act(act)
            d_ev.act(act)
            n2.act(act)
            f0.act(act)
            d_f0.act(act)
            n3.act(act)
            odd_act_tables(act)
            p_od.take(act, "act")
            ret_act(act)
            cmp_act(act)
            nsa_keys_act(act)
            split_to(act, "act", d_od.n0 + 2)
            nsa.act(act)
            n_y1.act(act)
            d_od.act(act)
            n4.act(act)
            f1.act(act)
            d_f1.act(act)
            n5.act(act)
            p_2.take(act, "act")
            forget_act(act)
            two.act(act)
            n_y2.act(act)
            d_2.act(act)
            n6.act(act)
            router_act(act)
            moe_act(act)
            last_act(act)

        @block.vector
        def _(dve):
            dve.wait_ge(s_const, 16)
            dve.wait_ge(s_gain_n1, 16)
            dve.wait_ge(s_x, 16)
            n1.dve(dve)
            dve.wait_ge(s_gains, 16 * 7)
            p_ev.take(dve, "dve")
            even_dve(dve)
            d_ev.dve(dve, n2)
            n2.dve(dve)
            f0.dve(dve)
            d_f0.dve(dve, n3)
            n3.dve(dve)
            ch = angles_dve(dve)
            p_od.take(dve, "dve", {2: lambda: rope_dve(dve, ch, Q_ROPES), 3: lambda: rope_dve(dve, ch, (RET_Q,)),
                                   4: lambda: rope_dve(dve, ch, (RET_K,))})
            ret_dve(dve)
            cmp_dve(dve)
            split_to(dve, "dve", d_od.n0 + 2)
            nsa.dve(dve)
            bias_dve(dve)
            n_y1.dve(dve)
            d_od.dve(dve, n4)
            n4.dve(dve)
            f1.dve(dve)
            d_f1.dve(dve, n5)
            n5.dve(dve)
            p_2.take(dve, "dve")
            bias_turn_dve(dve)
            forget_dve(dve)
            dve.wait_ge(b_rev, 2)
            two.dve(dve)
            n_y2.dve(dve)
            d_2.dve(dve, n6)
            wait_gain(dve, 4)
            n6.dve(dve)
            router_dve(dve)
            moe_dve(dve)
            last_dve(dve)

        @block.tensor
        def _(pe):
            pe.wait_ge(s_init, 3)
            pe.wait_ge(s_const, 16)
            n1.pe(pe)
            pe.wait_ge(s_gains, 16 * 7)
            p_ev.pe(pe)
            even_pe(pe)
            d_ev.pe(pe)
            n2.pe(pe)
            f0.pe(pe)
            d_f0.pe(pe)
            n3.pe(pe)
            p_od.pe(pe)
            ret_pe(pe)
            cmp_pe(pe)
            nsa_keys_pe(pe)
            nsa.pe(pe)
            bias_pe(pe)
            n_y1.pe(pe)
            d_od.pe(pe)
            n4.pe(pe)
            f1.pe(pe)
            d_f1.pe(pe)
            n5.pe(pe)
            p_2.pe(pe)
            forget_pe(pe)
            two.pe(pe)
            n_y2.pe(pe)
            d_2.pe(pe)
            n6.pe(pe)
            router_pe(pe)
            moe_pe(pe)


def shape_constants():
    f = np.float32
    p, c = np.arange(P)[:, None], np.arange(P)[None, :]
    k = {"c_ident": (p == c).astype(f), "c_upper": (p <= c).astype(f), "c_strict": (p < c).astype(f)}
    poolA, poolB = np.zeros((P, 4, 2, P), f), np.zeros((P, 4, P), f)
    for g, w in enumerate((2, 4, 8, 16)):
        for v in range(2):
            count = np.minimum(c + 1, w) if v == 0 else w
            poolA[:, g, v] = ((p <= c) & (p > c - w)) / count - (p == c)
        poolB[:, g] = ((p > c + P - w)) / f(w)
    k["c_poolA"], k["c_poolB"] = poolA, poolB
    decay = np.zeros((P, RH, T), f)
    rel = np.arange(T)[None, :] - p
    for h in range(RH):
        decay[:, h] = np.where(rel >= 0, np.exp(np.maximum(rel, 0) * np.log1p(-2.0 ** (-5.0 - h))), 0) * RD ** -0.5
    k["c_decay"] = decay
    i8, i64 = np.arange(0, 16, 2, dtype=f), np.arange(0, 128, 2, dtype=f)
    inv = np.concatenate([f(1) / (f(500000.0) ** (i8 / f(16))), f(1) / (f(10000.0) ** (i64 / f(128)))])
    k["c_invf"] = inv.astype(f)[None]
    tq = np.arange(MT)[None, :] * P + p
    k["c_cvalid"] = (tq >= CB - 1).astype(f)
    k["c_causal"] = np.where(c <= p, 0, -BIG).astype(f)
    cm = np.zeros((P, MT, NC + 1), f)
    cm[:, :, :NC] = np.where(np.arange(NC) * CS + CB - 1 <= tq[:, :, None], 0, -BIG)
    k["c_cmask"] = cm
    dist = np.arange(TW) - (P - 1)
    d = np.maximum(dist, 1).astype(f)
    large = 16 + (np.log(d / f(16)) / f(np.log(2048 / 16)) * f(16)).astype(np.int32)
    bucket = np.where(dist < 16, np.maximum(dist, 0), np.minimum(large, 31))
    ok = dist >= 0
    count = (dist <= 128) * 1 + (dist % 4 == 0) + (dist % 16 == 0)
    k["c_onehot"] = ((np.arange(32)[:, None] == bucket[None]) & ok & (count > 0)).astype(f)
    k["c_badd"] = np.where(ok & (count > 0), np.log(np.maximum(count, 1)), -BIG).astype(f)[None]
    io = np.zeros((P, P + NB + MT + EG), f)
    io[:, :P] = np.arange(P)
    io[:, P:P + NB] = np.arange(NB)
    io[:, P + NB:P + NB + MT] = tq
    io[:, P + NB + MT:] = EG - np.arange(EG)
    k["c_iotas"] = io
    k["c_io40x"] = (np.arange(NB) * P).astype(f)[None]
    return k


def kernel(**inputs):
    import concourse.bacc as bacc
    from concourse.bass_utils import run_bass_kernel_spmd

    nc = bacc.Bacc("TRN2", target_bir_lowering=False, num_devices=1)
    arrays = {n: np.ascontiguousarray(v) for n, v in inputs.items()}
    arrays.update(shape_constants())
    aps = {n: nc.dram_tensor("in_" + n, v.shape, mybir.dt.from_np(v.dtype), kind="ExternalInput").ap()
           for n, v in arrays.items()}
    out = nc.dram_tensor("out_x", (1, T, D), fp32, kind="ExternalOutput").ap()
    program(nc, aps, out)
    r = run_bass_kernel_spmd(nc, [{"in_" + n: v for n, v in arrays.items()}], core_ids=[0])
    return r.results[0]["out_x"]
```
